# Optimizing a Trainium2 kernel written in Bass

```python
import jax, jax.numpy as jnp
from jax import lax
import numpy as np

D_MODEL = 1024
BATCH = 1
SEQ = 512
DEPTH = 1

CHUNK = 64
N_META = 16
Q_BLOCK = 128
D_MIX = D_MODEL
FOX_HEADS = 8
FOX_HEAD_DIM = 64
FOX_WIDTH = FOX_HEADS * FOX_HEAD_DIM
HG_HEADS = 4
HG_EXPAND = 128
HG_HEAD_V = (D_MIX - FOX_WIDTH) // HG_HEADS
HG_K = HG_HEADS * HG_EXPAND
HG_V = HG_HEADS * HG_HEAD_V
D_FF = -(-8 * D_MODEL // (3 * 256)) * 256
EPS = 1e-6
MASK_VALUE = -1e30
LOG_F_MIN = -30.0
IN_SIZES = (FOX_WIDTH, FOX_WIDTH, FOX_WIDTH, FOX_HEADS, HG_K, HG_K, HG_V, HG_V)
IN_COLS = sum(IN_SIZES)


def rms_norm(x, w):
    xf = x.astype(jnp.float32)
    y = xf * lax.rsqrt(jnp.mean(xf * xf, axis=-1, keepdims=True) + EPS)
    return (y * w.astype(jnp.float32)).astype(x.dtype)

def forgetting_attention(q, k, v, log_f):
    B, L, H, Dh = q.shape
    n_blk = -(-L // Q_BLOCK)
    Lp = n_blk * Q_BLOCK
    pad = Lp - L
    padf = lambda a: jnp.pad(a, [(0, 0), (0, pad)] + [(0, 0)] * (a.ndim - 2))
    q, k, v, log_f = padf(q), padf(k), padf(v), padf(log_f)
    c = jnp.cumsum(log_f, axis=1)
    cT = c.transpose(0, 2, 1)
    scale = Dh ** -0.5
    key_pos = jnp.arange(Lp)
    qb = q.reshape(B, n_blk, Q_BLOCK, H, Dh).transpose(1, 0, 2, 3, 4)
    cb = c.reshape(B, n_blk, Q_BLOCK, H).transpose(1, 0, 3, 2)

    def block(args):
        i, q_i, c_i = args
        s = jnp.einsum('bqhd,bkhd->bhqk', q_i, k, preferred_element_type=jnp.float32) * scale
        s = s + (c_i[..., :, None] - cT[:, :, None, :])
        q_pos = i * Q_BLOCK + jnp.arange(Q_BLOCK)
        s = jnp.where(key_pos[None, :] <= q_pos[:, None], s, MASK_VALUE)
        p = jax.nn.softmax(s, axis=-1)
        return jnp.einsum('bhqk,bkhd->bqhd', p.astype(v.dtype), v)

    o = lax.map(block, (jnp.arange(n_blk), qb, cb))
    return o.transpose(1, 0, 2, 3, 4).reshape(B, Lp, H, Dh)[:, :L]

def hgrn2_recurrence(q, k, v, log_f):
    B, L, H, K = q.shape
    V = v.shape[-1]
    pad = (-L) % CHUNK
    padf = lambda a: jnp.pad(a, ((0, 0), (pad, 0), (0, 0), (0, 0)))
    q, k, v, log_f = padf(q), padf(k), padf(v), padf(log_f)
    Lp = L + pad
    n = Lp // CHUNK
    to_chunks = lambda a: a.reshape(B, n, CHUNK, H, a.shape[-1]).transpose(1, 0, 3, 2, 4)
    causal = jnp.tril(jnp.ones((CHUNK, CHUNK), dtype=bool))[:, :, None]

    def step(S, inp):
        q_c, k_c, v_c, g_c = inp
        b = jnp.cumsum(g_c, axis=2)
        o_inter = jnp.einsum('bhtk,bhkv->bhtv', q_c * jnp.exp(b), S)
        rel = b[:, :, :, None, :] - b[:, :, None, :, :]
        decay = jnp.where(causal, jnp.exp(jnp.where(causal, rel, 0.0)), 0.0)
        A = jnp.einsum('bhtk,bhsk,bhtsk->bhts', q_c, k_c, decay)
        o_intra = jnp.einsum('bhts,bhsv->bhtv', A, v_c)
        b_last = b[:, :, -1]
        k_dec = k_c * jnp.exp(b_last[:, :, None, :] - b)
        S = jnp.exp(b_last)[..., None] * S + jnp.einsum('bhsk,bhsv->bhkv', k_dec, v_c)
        return S, o_inter + o_intra

    S0 = jnp.zeros((B, H, K, V), jnp.float32)
    _, o = lax.scan(step, S0, (to_chunks(q), to_chunks(k), to_chunks(v), to_chunks(log_f)))
    o = o.transpose(1, 0, 3, 2, 4).reshape(B, Lp, H, V)
    return o[:, pad:]

def first_inputs(seed: int = 0) -> dict:
    key = jax.random.key(seed)
    ks = jax.random.split(key, 14)
    nrm = lambda k, shape, s: jax.random.normal(k, shape, jnp.float32) * s
    return {
        "x": nrm(ks[0], (BATCH, SEQ, D_MODEL), 1.0),
        "meta": nrm(ks[1], (N_META, D_MODEL), 1.0),
        "norm_mix_w": 1.0 + nrm(ks[2], (DEPTH, D_MODEL), 0.02),
        "w_in": nrm(ks[3], (DEPTH, D_MODEL, IN_COLS), D_MODEL ** -0.5),
        "fox_f_bias": 2.0 + nrm(ks[4], (DEPTH, FOX_HEADS), 0.5),
        "hgrn_lb_raw": nrm(ks[5], (DEPTH, HG_K), 1.0),
        "hgrn_norm_w": 1.0 + nrm(ks[6], (DEPTH, HG_HEAD_V), 0.02),
        "w_out": nrm(ks[7], (DEPTH, D_MIX, D_MODEL), D_MIX ** -0.5),
        "norm_ffn_w": 1.0 + nrm(ks[8], (DEPTH, D_MODEL), 0.02),
        "w_ffn_gate": nrm(ks[9], (DEPTH, D_MODEL, D_FF), D_MODEL ** -0.5),
        "w_ffn_up": nrm(ks[10], (DEPTH, D_MODEL, D_FF), D_MODEL ** -0.5),
        "w_ffn_down": nrm(ks[11], (DEPTH, D_FF, D_MODEL), D_FF ** -0.5),
        "norm_final_w": 1.0 + nrm(ks[12], (D_MODEL,), 0.02),
    }

def first_block(x, meta, norm_mix_w, w_in, fox_f_bias, hgrn_lb_raw, hgrn_norm_w, w_out,
              norm_ffn_w, w_ffn_gate, w_ffn_up, w_ffn_down, norm_final_w):
    B = x.shape[0]
    h = jnp.concatenate([jnp.broadcast_to(meta[None].astype(x.dtype), (B, N_META, D_MODEL)), x], axis=1)
    L = h.shape[1]
    s_lb = jax.nn.softmax(hgrn_lb_raw.astype(jnp.float32), axis=0)
    lower_bounds = jnp.cumsum(s_lb, axis=0) - s_lb[0]
    split_at = tuple(int(v) for v in np.cumsum(IN_SIZES)[:-1])

    for l in range(DEPTH):
        u = rms_norm(h, norm_mix_w[l])
        proj = u @ w_in[l]
        fq, fk, fv, ff, hq, hf, hi, hg = jnp.split(proj, split_at, axis=-1)

        fox_log_f = jax.nn.log_sigmoid(ff.astype(jnp.float32) + fox_f_bias[l].astype(jnp.float32))
        hs = (B, L, FOX_HEADS, FOX_HEAD_DIM)
        fox_out = forgetting_attention(fq.reshape(hs), fk.reshape(hs), fv.reshape(hs), fox_log_f)
        fox_out = fox_out.reshape(B, L, FOX_WIDTH).astype(h.dtype)

        lb = lower_bounds[l]
        one_minus_f = (1.0 - lb) * jax.nn.sigmoid(-hf.astype(jnp.float32))
        log_f = jnp.maximum(jnp.log1p(-one_minus_f), LOG_F_MIN)
        k_in = -jnp.expm1(log_f)
        q_h = jax.nn.silu(hq.astype(jnp.float32)) * (HG_EXPAND ** -0.5)
        ks_ = (B, L, HG_HEADS, HG_EXPAND)
        o_h = hgrn2_recurrence(q_h.reshape(ks_), k_in.reshape(ks_),
                               hi.astype(jnp.float32).reshape(B, L, HG_HEADS, HG_HEAD_V),
                               log_f.reshape(ks_))
        o_h = rms_norm(o_h, hgrn_norm_w[l])
        hgrn_out = (o_h.reshape(B, L, HG_V) * jax.nn.silu(hg.astype(jnp.float32))).astype(h.dtype)

        mixed = jnp.concatenate([fox_out, hgrn_out], axis=-1) @ w_out[l]
        h = h + mixed

        u = rms_norm(h, norm_ffn_w[l])
        h = h + (jax.nn.silu(u @ w_ffn_gate[l]) * (u @ w_ffn_up[l])) @ w_ffn_down[l]

    return rms_norm(h, norm_final_w)[:, N_META:]


DEPTH_2 = 2

CONV_WIDTH = 3
D_CONV = D_MODEL
N_RET_HEADS = 4
RET_QK_DIM = 256
RET_V_DIM = 512
D_RET_QK = N_RET_HEADS * RET_QK_DIM
D_RET_V = N_RET_HEADS * RET_V_DIM
ROPE_BASE = 10000.0
RMS_EPS = 1e-6
GN_EPS = 1e-5
D_IN = 4 * D_CONV + 2 * D_RET_QK + 2 * D_RET_V + 2 * D_MODEL


def _rmsnorm(x, g):
    xf = x.astype(jnp.float32)
    y = xf * lax.rsqrt(jnp.mean(xf * xf, axis=-1, keepdims=True) + RMS_EPS)
    return (y * g.astype(jnp.float32)).astype(x.dtype)

def _rope(x, pos):
    half = x.shape[-1] // 2
    inv = ROPE_BASE ** (-jnp.arange(half, dtype=jnp.float32) / half)
    ang = pos[:, None] * inv[None, :]
    cos = jnp.cos(ang)[None, :, None, :]
    sin = jnp.sin(ang)[None, :, None, :]
    x1, x2 = x[..., :half], x[..., half:]
    return jnp.concatenate([x1 * cos - x2 * sin, x1 * sin + x2 * cos], axis=-1)

def _short_conv_branch(h, gb, gc, z, conv_w, conv_b, w_out):
    u = gc * h
    up = jnp.pad(u, ((0, 0), (CONV_WIDTH - 1, 0), (0, 0)))
    T = u.shape[1]
    y = conv_b + sum(conv_w[j] * up[:, j:j + T] for j in range(CONV_WIDTH))
    y = gb * y * jax.nn.silu(z)
    return y @ w_out

def _retention_branch(q, k, v, z, gn_g, w_out):
    Bsz, T, _ = q.shape
    H, dk, dv = N_RET_HEADS, RET_QK_DIM, RET_V_DIM
    pos = jnp.arange(T, dtype=jnp.float32)
    qf = _rope(q.astype(jnp.float32).reshape(Bsz, T, H, dk), pos)
    kf = _rope(k.astype(jnp.float32).reshape(Bsz, T, H, dk), pos) * (dk ** -0.5)
    vf = v.astype(jnp.float32).reshape(Bsz, T, H, dv)
    n_pad = (-N_META) % CHUNK
    padw = ((0, 0), (n_pad, 0), (0, 0), (0, 0))
    qf, kf, vf = (jnp.pad(a, padw) for a in (qf, kf, vf))
    L = T + n_pad
    n_chunks = L // CHUNK

    def to_chunks(a):
        return a.reshape(Bsz, n_chunks, CHUNK, H, a.shape[-1]).transpose(1, 0, 3, 2, 4)

    qc, kc, vc = to_chunks(qf), to_chunks(kf), to_chunks(vf)
    log_g = jnp.log(1.0 - 2.0 ** (-5.0 - jnp.arange(H, dtype=jnp.float32)))
    idx = jnp.arange(CHUNK, dtype=jnp.float32)
    intra_dec = jnp.exp(log_g[:, None, None] * jnp.abs(idx[:, None] - idx[None, :]))
    q_dec = jnp.exp(log_g[:, None] * (idx + 1.0))[None, :, :, None]
    k_dec = jnp.exp(log_g[:, None] * (CHUNK - 1.0 - idx))[None, :, :, None]
    chunk_dec = jnp.exp(log_g * CHUNK)[None, :, None, None]

    def step(state, inp):
        qi, ki, vi = inp
        s = jnp.einsum('bhnd,bhmd->bhnm', qi, ki) * intra_dec
        intra = jnp.einsum('bhnm,bhmv->bhnv', s, vi)
        cross = jnp.einsum('bhnd,bhdv->bhnv', qi * q_dec, state)
        new_state = state * chunk_dec + jnp.einsum('bhmd,bhmv->bhdv', ki * k_dec, vi)
        return new_state, intra + cross

    state0 = jnp.zeros((Bsz, H, dk, dv), jnp.float32)
    _, out = lax.scan(step, state0, (qc, kc, vc))
    out = out.transpose(1, 0, 3, 2, 4).reshape(Bsz, L, H, dv)[:, n_pad:]
    mu = jnp.mean(out, axis=-1, keepdims=True)
    var = jnp.mean(jnp.square(out - mu), axis=-1, keepdims=True)
    out = (out - mu) * lax.rsqrt(var + GN_EPS) * gn_g.astype(jnp.float32).reshape(H, dv)
    out = out.reshape(Bsz, T, D_RET_V).astype(z.dtype) * jax.nn.silu(z)
    return out @ w_out

def second_inputs(seed: int = 0) -> dict:
    key = jax.random.key(seed)
    ks = jax.random.split(key, 16)
    nrm = jax.random.normal
    f32 = jnp.float32
    return {
        "x": nrm(ks[0], (BATCH, SEQ, D_MODEL), f32),
        "meta": nrm(ks[1], (N_META, D_MODEL), f32),
        "pre_norm_g": 1.0 + 0.05 * nrm(ks[2], (DEPTH_2, D_MODEL), f32),
        "w_in": nrm(ks[3], (DEPTH_2, D_MODEL, D_IN), f32) * D_MODEL ** -0.5,
        "b_in": 0.02 * nrm(ks[4], (DEPTH_2, D_IN), f32),
        "conv_w": nrm(ks[5], (DEPTH_2, CONV_WIDTH, D_CONV), f32) * CONV_WIDTH ** -0.5,
        "conv_b": 0.02 * nrm(ks[6], (DEPTH_2, D_CONV), f32),
        "w_conv_out": nrm(ks[7], (DEPTH_2, D_CONV, D_MODEL), f32) * D_CONV ** -0.5,
        "ret_gn_g": 1.0 + 0.05 * nrm(ks[8], (DEPTH_2, D_RET_V), f32),
        "w_ret_out": nrm(ks[9], (DEPTH_2, D_RET_V, D_MODEL), f32) * D_RET_V ** -0.5,
        "w_o": nrm(ks[10], (DEPTH_2, D_MODEL, D_MODEL), f32) * D_MODEL ** -0.5,
        "post_norm_g": 1.0 + 0.05 * nrm(ks[11], (DEPTH_2, D_MODEL), f32),
    }

def second_block(x, meta, pre_norm_g, w_in, b_in, conv_w, conv_b, w_conv_out,
              ret_gn_g, w_ret_out, w_o, post_norm_g):
    Bsz = x.shape[0]
    meta_b = jnp.broadcast_to(meta[None].astype(x.dtype), (Bsz, N_META, D_MODEL))
    h = jnp.concatenate([meta_b, x], axis=1)
    sizes = (D_CONV,) * 4 + (D_RET_QK,) * 2 + (D_RET_V,) * 2 + (D_MODEL,) * 2
    split_at = [int(s) for s in np.cumsum(sizes)[:-1]]
    for l in range(DEPTH_2):
        xn = _rmsnorm(h, pre_norm_g[l])
        proj = xn @ w_in[l] + b_in[l]
        c_h, c_b, c_c, c_z, r_q, r_k, r_v, r_z, g_a, g_b = jnp.split(proj, split_at, axis=-1)
        y_a = _short_conv_branch(c_h, c_b, c_c, c_z, conv_w[l], conv_b[l], w_conv_out[l])
        y_b = _retention_branch(r_q, r_k, r_v, r_z, ret_gn_g[l], w_ret_out[l])
        y = jax.nn.sigmoid(g_a) * y_a + jax.nn.sigmoid(g_b) * y_b
        y = y @ w_o[l]
        h = h + _rmsnorm(y, post_norm_g[l])
    return h[:, N_META:]


def setup_inputs(seed=0):
    out = dict(first_inputs(seed))
    for name, value in second_inputs(seed + 1).items():
        if name != "x":
            out[name + "_2"] = value
    return out


def reference(
    x, meta, norm_mix_w, w_in, fox_f_bias, hgrn_lb_raw, hgrn_norm_w, w_out, norm_ffn_w,
    w_ffn_gate, w_ffn_up, w_ffn_down, norm_final_w, meta_2, pre_norm_g_2, w_in_2, b_in_2,
    conv_w_2, conv_b_2, w_conv_out_2, ret_gn_g_2, w_ret_out_2, w_o_2, post_norm_g_2,
):
    x = first_block(
        x, meta, norm_mix_w, w_in, fox_f_bias, hgrn_lb_raw, hgrn_norm_w, w_out, norm_ffn_w,
        w_ffn_gate, w_ffn_up, w_ffn_down, norm_final_w,
    )
    return second_block(
        x, meta_2, pre_norm_g_2, w_in_2, b_in_2, conv_w_2, conv_b_2, w_conv_out_2, ret_gn_g_2,
        w_ret_out_2, w_o_2, post_norm_g_2,
    )


_drawn_inputs = setup_inputs


def setup_inputs(seed=0):
    import zlib

    import numpy as np

    out = dict(_drawn_inputs(seed))
    spreads = {}
    factors = {'hgrn_norm_w': 2.788, 'conv_b_2': 3.374}
    for name, (base, spread) in spreads.items():
        noise = np.random.default_rng([zlib.crc32(name.encode()), seed]).standard_normal(out[name].shape)
        drawn = base * np.exp(spread * noise) if base else spread * noise
        out[name] = __import__('jax').numpy.asarray(drawn.astype(out[name].dtype))
    for name, factor in factors.items():
        out[name] = (out[name] * factor).astype(out[name].dtype)
    return out
```

```python
from contextlib import ExitStack

import concourse.bass as bass
from concourse import mybir

F32 = mybir.dt.float32
F32R = mybir.dt.float32r
BF16 = mybir.dt.bfloat16
I32 = mybir.dt.int32
ALU = mybir.AluOpType
ACT = mybir.ActivationFunctionType
AX = mybir.AxisListType

P = 128
D = 1024
KT = D // P
META = 16
SEQ = 512
L = META + SEQ
XT = SEQ // P
FF = 2816
FT = FF // P
HEADS = 4
EPS = 1e-6
GN_EPS = 1e-5
F_MIN = 9.357622968840175e-14
LEVELS = 7

Q_IN, Q_OUT, Q_FF, Q_DOWN, Q_B2 = 0, 7, 9, 20, 26
Q_HEAD, Q_CONV, Q_MERGE, Q_WO, Q_LAYER = 4, 16, 24, 30, 32
QUADS = Q_B2 + 2 * Q_LAYER
A_OUT, A_FF, A_DOWN, A_B2 = 14, 18, 40, 44
A_HEAD, A_CONV, A_MERGE, A_WO, A_LAYER = 10, 40, 56, 68, 72

V_MIX, V_FFN, V_FINAL, V_HNORM, V_LB, V_PRE, V_POST = 0, 8, 16, 24, 25, 29, 45
V_CW, V_CB, V_GN, V_BIAS = 61, 109, 125, 157
V_EPS = V_BIAS + 2 * 4 * Q_LAYER
V_COLS = V_EPS + 2

KEYS = [(0, META)] + [(META + P * i, META + P * (i + 1)) for i in range(XT)]


def build(nc, io):
    with ExitStack() as ctx:
        def sb(name, shape, dt=F32, scope=ctx):
            return scope.enter_context(nc.sbuf_tensor(name, shape, dt))

        def sem(name):
            return ctx.enter_context(nc.semaphore(name))

        h = sb("h", [P, KT, L])
        uh, ul = sb("uh", [P, KT, L], F32R), sb("ul", [P, KT, L], F32R)
        raw = sb("raw", [P, 4, KT * P])
        wh, wl = sb("wh", [P, 2, KT * P], F32R), sb("wl", [P, 2, KT * P], F32R)
        vec = sb("vec", [P, V_COLS])
        ident = sb("ident", [P, P])
        ones = sb("ones", [P, P])
        val = sb("val", [P, 2, L])
        sq = sb("sq", [P, 2, L])
        root = sb("root", [P, L])
        rstd = sb("rstd", [P, L])
        meta2 = sb("meta2", [P, KT, META])
        ea = sb("ea", [P, 2, L])

        mix = ExitStack()
        proj = sb("proj", [P, 28, L], F32, mix)
        lbt = sb("lbt", [P, 8, 4], F32, mix)
        fox = ExitStack()
        wff_raw = sb("wff_raw", [P, KT * 8], F32, fox)
        wffh, wffl = sb("wffh", [P, KT * 8], F32R, fox), sb("wffl", [P, KT * 8], F32R, fox)
        fbias = sb("fbias", [8, 1], F32, fox)
        cz, ct, ccum, cone = (sb(n, [8, L], F32, fox) for n in ("cz", "ct", "ccum", "cone"))
        sel = sb("sel", [8, 8, P], F32, fox)
        selp = sb("selp", [8, 2, P], F32, fox)
        causal = sb("causal", [P, P], F32, fox)
        vnat = sb("vnat", [P, 5, 4 * P], F32, fox)
        qs, ks = sb("qs", [P, L], F32, fox), sb("ks", [P, L], F32, fox)
        vs = sb("vs", [P, 5, P], F32, fox)
        probs = sb("probs", [P, 2, L], F32, fox)
        pT = sb("pT", [P, 2, 5, P], F32, fox)
        fmax, fneg, fsum, finv = (sb(n, [P, 2], F32, fox) for n in ("fmax", "fneg", "fsum", "finv"))
        onat = proj[:, 8:8 + XT, 0:4 * P]
        fox.close()
        sgf, sgq, sgg, fgate, kin, gl, qh, vt = (proj[:, i, :] for i in range(8))
        eq, ek = proj[:, 8:10, 0:SEQ], proj[:, 10:12, 0:SEQ]
        hg = ExitStack()
        vn = sb("hg_vn", [P, 5, P], F32, hg)
        xq, xk = sb("hg_xq", [P, 2, SEQ], F32, hg), sb("hg_xk", [P, 2, SEQ], F32, hg)
        ql, kl = sb("hg_ql", [P, 2, SEQ], F32, hg), sb("hg_kl", [P, 2, SEQ], F32, hg)
        em, xm, km, pm = (sb("hg_" + n, [P, META], F32, hg) for n in ("em", "xm", "km", "pm"))
        resets = sb("hg_resets", [P, LEVELS, SEQ], BF16, hg)
        odd = sb("hg_odd", [P, SEQ], BF16, hg)
        masks = sb("hg_masks", [P, LEVELS, P], I32, hg)
        carrier = sb("hg_carrier", [P, LEVELS], F32, hg)
        amat = sb("hg_amat", [P, SEQ], F32, hg)
        kn = sb("hg_kn", [P, 4, P], F32, hg)
        st = sb("hg_state", [P, 4, P], F32, hg)
        ot = sb("hg_ot", [P, SEQ], F32, hg)
        hg.close()
        mix.close()

        ffn = ExitStack()
        gs = sb("gs", [P, L], F32, ffn)
        gh, gl_ = sb("gh", [P, FT, SEQ], F32R, ffn), sb("gl", [P, FT, SEQ], F32R, ffn)
        ffn.close()

        y = sb("y", [P, KT, L])
        ret = ExitStack()
        cos, sin = sb("cos", [P, L], F32, ret), sb("sin", [P, L], F32, ret)
        decx, decm = sb("decx", [P, HEADS, SEQ], F32, ret), sb("decm", [META, HEADS, L], F32, ret)
        kq = sb("kq", [P, 4, L], F32, ret)
        kr, qr = sb("kr", [P, 2, L], F32, ret), sb("qr", [P, 2, L], F32, ret)
        r1, r2 = sb("r1", [P, L], F32, ret), sb("r2", [P, L], F32, ret)
        vraw, zs = ea, r1
        rvn = sb("rvn", [P, 5, 4 * P], F32, ret)
        vmean = sb("vmean", [P, 5], F32, ret)
        vneg = sb("vneg", [P, 5], F32, ret)
        sd = sb("sd", [P, 5, L], F32, ret)
        o = sb("o", [P, 4, L], F32, ret)
        rh, rl = sb("rh", [P, 4, L], F32R, ret), sb("rl", [P, 4, L], F32R, ret)
        keep = ExitStack()
        ret.close()
        sb("keep_tables", [P, 2 * L + HEADS * SEQ + HEADS * L], F32, keep)
        ch, cl = sb("ch", [P, KT, L], F32R, keep), sb("cl", [P, KT, L], F32R, keep)
        eh = sb("eh", [P, L], F32, keep)
        cu = sb("cu", [P, L + 2], F32, keep)
        c0, c1, c2, cb_, cs = (sb("cv_" + n, [P, L], F32, keep) for n in ("c0", "c1", "c2", "b", "s"))
        ya, g1, g2 = (sb(n, [P, 2, L], F32, keep) for n in ("ya", "g1", "g2"))
        m1, m2 = sb("m1", [P, L], F32, keep), sb("m2", [P, L], F32, keep)
        keep.close()

        ps = ctx.enter_context(nc.psum_tensor("ps", [P, 8, 512], F32))

        raw_full = [sem(f"raw_full{i}") for i in range(4)]
        hi_ready, lo_ready = sem("hi_ready"), sem("lo_ready")
        panel_done = sem("panel_done")
        half_done = sem("half_done")
        acc_free = [sem(f"acc_free{i}") for i in range(2)]
        h_loaded, small_loaded, tables_loaded = sem("h_loaded"), sem("small_loaded"), sem("tables_loaded")
        consts_set, masks_set, masks_loaded = sem("consts_set"), sem("masks_set"), sem("masks_loaded")
        sq_ready, sq_free = sem("sq_ready"), sem("sq_free")
        root_ready = sem("root_ready")
        val_ready, valhi_ready, vallo_ready = sem("val_ready"), sem("valhi_ready"), sem("vallo_ready")
        h_ready = sem("h_ready")
        sig_ready = sem("sig_ready")
        wff_hi, wff_lo, ff_psum, ff_abs, ff_ln, cum_ready = (sem(n) for n in (
            "wff_hi", "wff_lo", "ff_psum", "ff_abs", "ff_ln", "cum_ready"))
        fv_psum, fv_ready, fox_in, scores_ready, negmax_ready, probs_ready = (sem(n) for n in (
            "fv_psum", "fv_ready", "fox_in", "scores_ready", "negmax_ready", "probs_ready"))
        probsT_psum, probsT_ready, heads_psum, heads_ready, headsT_psum = (sem(n) for n in (
            "probsT_psum", "probsT_ready", "heads_psum", "heads_ready", "headsT_psum"))
        hg_sig, hg_f, hg_g, hg_vt, hg_vpsum, hg_vn, hg_exp_in, hg_exp_out = (sem("hg_" + n) for n in (
            "sig", "f_ready", "g_ready", "vt_ready", "v_psum", "v_nat", "exp_in", "exp_out"))
        hg_qk, hg_s, hg_pred, hg_min, hg_mout, hg_km, hg_kpsum, hg_kn, hg_upsum, hg_state = (
            sem("hg_" + n) for n in ("qk_ready", "s_psum", "a_ready", "meta_in", "meta_out",
                                     "meta_k", "k_psum", "k_nat", "u_psum", "state_ready"))
        hg_o, hg_sq, hg_ss, hg_root, hg_inv = (sem("hg_" + n) for n in (
            "o_psum", "squares", "ss_psum", "root_ready", "iter_free"))
        lb_exp, lb_in = sem("lb_exp"), sem("lb_in")
        rope_ready, vt_psum, vn_ready, v_centred, s_psum, sd_ready, o_psum, o_ready = (sem(n) for n in (
            "rope_ready", "vt_psum", "vn_ready", "v_centred", "s_psum", "sd_ready", "o_psum", "o_ready"))
        y_ready, cu_ready, out_stored = sem("y_ready"), sem("cu_ready"), sem("out_stored")

        block = ctx.enter_context(nc.Block())

        def full(t):
            return t.rearrange("p (a b) -> p a b", a=2)

        def seq(t):
            return t[:, META:L].rearrange("p (a b) -> p a b", a=2)

        def acc(slot, n=L):
            return ps[:, 2 * slot:2 * slot + 2, 0:n // 2]

        def col(c, width=1):
            return vec[:, bass.ds(c, width)]

        def tile(t, i):
            return t[:, bass.ds(i, 1), :].rearrange("p a b -> p (a b)")

        def scores(b):
            return ps[:, 2 * b:2 * b + 2, :].rearrange("p a b -> p (a b)")[:, 240:240 + L]

        def bias(quad, s):
            return col(4 * quad + (s + V_BIAS - 4 * Q_B2))

        @block.sync
        def _(sp):
            sp.dma_start(h[:, :, META:L], io["x"]).then_inc(h_loaded, 16)
            sp.dma_start(h[:, :, 0:META], io["meta"]).then_inc(h_loaded, 16)
            for s in range(4):
                sp.dma_start(raw[:, s, :], io["weights"][s]).then_inc(raw_full[s], 16)
            with sp.Fori(1, QUADS) as q:
                for s in range(4):
                    sp.wait_ge(lo_ready, 4 * q + (s - 3))
                    sp.dma_start(raw[:, s, :], io["weights"][4 * q + s]).then_inc(raw_full[s], 16)
            for s in range(2):
                sp.wait_ge(lo_ready, 4 * QUADS - 3 + s)
                sp.dma_start(raw[:, s, :], io["weights"][4 * QUADS + s]).then_inc(raw_full[s], 16)
            sp.wait_ge(h_ready, 5)
            sp.dma_start(io["out"], h[:, :, META:L]).then_inc(out_stored, 16)
            sp.wait_ge(out_stored, 16)

        @block.gpsimd
        def _(pool):
            pool.dma_start(vec[:], io["vec"]).then_inc(small_loaded, 16)
            pool.dma_start(ident[:], io["ident"]).then_inc(small_loaded, 16)
            pool.dma_start(wff_raw[:], io["wff"]).then_inc(small_loaded, 16)
            pool.dma_start(fbias[:], io["fbias"]).then_inc(small_loaded, 16)
            pool.dma_start(sel[:], io["sel"]).then_inc(small_loaded, 16)
            pool.dma_start(causal[:], io["causal"]).then_inc(small_loaded, 16)
            pool.dma_start(meta2[:], io["meta2"]).then_inc(small_loaded, 16)
            pool.memset(ones[:], 1.0)
            pool.memset(cone[:], 1.0)
            pool.drain().then_inc(consts_set, 1)

            def split_low(q):
                for s in range(4):
                    pool.wait_ge(hi_ready, 4 * q + (s + 1))
                    nc.gpsimd.tensor_tensor(wl[:, s % 2, :], raw[:, s, :], wh[:, s % 2, :].bitcast(F32),
                                            ALU.subtract).then_inc(lo_ready, 1)

            with pool.Fori(0, Q_OUT) as q:
                split_low(q)
            pool.wait_ge(headsT_psum, 4)
            pool.dma_start(masks[:], io["masks"]).then_inc(masks_loaded, 16)
            pool.memset(resets[:], 1.0)
            pool.memset(odd[:], 0.0)
            pool.drain()
            for l in range(1, LEVELS + 1):
                pool.memset(resets[:, l - 1, :].rearrange("p (n b) -> p n b", b=2 ** l)[:, :, 0:1], 0.0)
            pool.memset(odd.rearrange("p (n b) -> p n b", b=2)[:, :, 1:2], 1.0)
            pool.drain().then_inc(masks_set, 1)
            with pool.Fori(Q_OUT, Q_B2) as q:
                split_low(q)
            pool.wait_ge(h_ready, 2)
            for dst, name in ((cos, "cos"), (sin, "sin"), (decx, "decx"), (decm, "decm")):
                pool.dma_start(dst[:], io[name]).then_inc(tables_loaded, 16)
            with pool.Fori(Q_B2, QUADS) as q:
                split_low(q)

        @block.scalar
        def _(act):
            def split_ahead(quad, s):
                s2 = (s + 2) % 4
                act.wait_ge(raw_full[s2], 16 * quad + 16 * (1 + (s + 2) // 4))
                act.wait_ge(panel_done, 4 * quad + (s + 1))
                nc.scalar.activation(wh[:, s2 % 2, :], raw[:, s2, :], ACT.Copy).then_inc(hi_ready, 1)

            def split_value(index, slot, dst, vindex=None, c0=0):
                act.wait_ge(val_ready, (index if vindex is None else vindex) + 1)
                nc.scalar.activation(dst, val[:, slot, c0:L], ACT.Copy).then_inc(valhi_ready, 1)

            def norm_stats(first, nth, src, tiles, width, eps, c0):
                for k in range(tiles):
                    act.wait_ge(sq_free, first + (k + 1))
                    nc.scalar.activation(sq[:, k % 2, c0:L], src(k)[:, c0:L], ACT.Square).then_inc(sq_ready, 1)
                act.wait_ge(sq_free, first + (tiles + 2))
                v = seq if c0 else full
                nc.scalar.activation(v(root[:]), acc(2, L - c0), ACT.Sqrt, bias=epsb[eps],
                                     scale=1.0 / width).then_inc(root_ready, 1)

            epsb = {EPS: col(V_EPS), GN_EPS: col(V_EPS + 1)}

            for s in range(2):
                act.wait_ge(raw_full[s], 16)
                nc.scalar.activation(wh[:, s, :], raw[:, s, :], ACT.Copy).then_inc(hi_ready, 1)
            act.wait_ge(small_loaded, 16 * 7)
            nc.scalar.activation(wffh[:], wff_raw[:], ACT.Copy).then_inc(wff_hi, 1)
            act.wait_ge(lb_in, 1)
            nc.scalar.activation(lbt[:, 1, :], lbt[:, 0, :], ACT.Exp).then_inc(lb_exp, 1)
            act.wait_ge(h_loaded, 32)
            norm_stats(0, 0, lambda k: h[:, k, :], KT, D, EPS, 0)
            for k in range(KT):
                split_value(k, k % 2, uh[:, k, :])
            act.wait_ge(ff_psum, 1)
            nc.scalar.activation(full(cz[:]), ps[0:8, 4:6, 0:L // 2], ACT.Identity, bias=fbias[:])
            act.drain()
            nc.scalar.activation(ct[:], cz[:], ACT.Abs)
            act.drain()
            nc.scalar.activation(ct[:], ct[:], ACT.Exp, scale=-1.0)
            act.drain()
            nc.scalar.activation(ct[:], ct[:], ACT.Ln, bias=1.0).then_inc(ff_ln, 1)
            with act.Fori(0, 7) as q:
                for s in range(4):
                    split_ahead(q, s)
                    nc.scalar.activation(full(tile(proj, 4 * q + s)), acc(s % 2), ACT.Copy)\
                        .then_inc(acc_free[s % 2], 1)

            with act.Fori(0, 4) as hp:
                for n in range(8):
                    b, i = n % 2, n % 4
                    nk = KEYS[i + 1][1]
                    act.wait_ge(negmax_ready, 8 * hp + (n + 1))
                    act.wait_ge(probsT_psum, 8 * hp + (n + 1))
                    act.wait_ge(heads_ready, 8 * hp + (n + 1))
                    nc.scalar.activation(probs[:, b, 0:nk], scores(b)[:, 0:nk], ACT.Exp,
                                         bias=fneg[:, b:b + 1], scale=0.125,
                                         accum_out=fsum[:, b:b + 1]).then_inc(probs_ready, 1)
            for k in range(4):
                split_value(8 + k, k % 2, uh[:, k, META:L], c0=META)

            with act.Fori(0, HEADS) as hd:
                act.wait_ge(hg_inv, hd + 1)
                nc.scalar.activation(sgf[:], tile(proj, hd + 16), ACT.Sigmoid, scale=-1.0)
                nc.scalar.activation(sgq[:], tile(proj, hd + 12), ACT.Sigmoid)
                nc.scalar.activation(sgg[:], tile(proj, hd + 24), ACT.Sigmoid).then_inc(hg_sig, 1)
                act.wait_ge(hg_f, hd + 1)
                nc.scalar.activation(gl[:], fgate[:], ACT.Ln).then_inc(hg_g, 1)
                for l in range(LEVELS + 1):
                    act.wait_ge(hg_exp_in, (LEVELS + 1) * hd + (l + 1))
                    nc.scalar.activation(xq[:, l % 2, :], eq[:, l % 2, :], ACT.Exp)
                    nc.scalar.activation(xk[:, l % 2, :], ek[:, l % 2, :], ACT.Exp).then_inc(hg_exp_out, 1)
                act.wait_ge(hg_min, hd + 1)
                nc.scalar.activation(xm[:], em[:], ACT.Exp).then_inc(hg_mout, 1)
                act.wait_ge(hg_o, hd + 1)
                nc.scalar.activation(sq[:, 0, 0:SEQ], ps[:, 0, :], ACT.Square).then_inc(hg_sq, 1)
                act.wait_ge(hg_ss, hd + 1)
                nc.scalar.activation(root[:, 0:SEQ], ps[:, 1, :], ACT.Sqrt, bias=epsb[EPS],
                                     scale=1.0 / P).then_inc(hg_root, 1)
                split_value(hd + 12, 0, tile(uh, hd + 4)[:, META:L], c0=META)

            with act.Fori(Q_OUT, Q_FF) as q:
                for s in range(4):
                    split_ahead(q, s)
            act.wait_ge(h_ready, 1)
            norm_stats(8, 1, lambda k: h[:, k, :], KT, D, EPS, META)
            for k in range(KT):
                split_value(16 + k, k % 2, uh[:, k, META:L], c0=META)
            with act.Fori(0, 11) as r:
                for s in range(4):
                    split_ahead(r + Q_FF, s)
                    if s % 2 == 0:
                        nc.scalar.activation(seq(ea[:, s // 2, :]), acc(0, SEQ), ACT.Sigmoid).then_inc(sig_ready, 1)
                    else:
                        j = s // 2
                        split_value(2 * r + (24 + j), j, tile(gh, 2 * r + j), c0=META)
            with act.Fori(Q_DOWN, Q_B2) as q:
                for s in range(4):
                    split_ahead(q, s)
            act.wait_ge(h_ready, 2)
            norm_stats(16, 2, lambda k: h[:, k, :], KT, D, EPS, META)

            with act.Fori(0, 2) as lay:
                quad0 = lay * Q_LAYER + Q_B2
                v0, i0 = 32 * lay + 46, 40 * lay + 46
                act.wait_ge(h_ready, lay + 3)
                norm_stats(32 * lay + 24, 6 * lay + 3, lambda k: h[:, k, :], KT, D, EPS, 0)
                for k in range(KT):
                    split_value(i0 + k, k % 2, uh[:, k, :], v0 + k)
                with act.Fori(0, HEADS) as hd:
                    quad = 4 * hd + quad0
                    it = 4 * lay + hd
                    for s in range(4):
                        split_ahead(quad, s)
                        nc.scalar.activation(full(kq[:, s, :]), acc(s % 2), ACT.Identity,
                                             bias=bias(quad, s)).then_inc(acc_free[s % 2], 1)
                    for s in range(4):
                        split_ahead(quad + 1, s)
                        if s >= 2:
                            act.wait_ge(vt_psum, 4 * it + (s - 1))
                        nc.scalar.activation(full(vraw[:, s % 2, :]), acc(s % 2), ACT.Identity,
                                             bias=bias(quad + 1, s)).then_inc(acc_free[s % 2], 1)
                    act.wait_ge(o_ready, it + 1)
                    sq0 = 32 * lay + 4 * hd + 32
                    for k in range(4):
                        act.wait_ge(sq_free, sq0 + (k + 1))
                        nc.scalar.activation(sq[:, k % 2, :], o[:, k, :], ACT.Square).then_inc(sq_ready, 1)
                    for s in range(4):
                        split_ahead(quad + 2, s)
                        nc.scalar.activation(full(ea[:, s % 2, :]), acc(s % 2), ACT.Sigmoid,
                                             bias=bias(quad + 2, s)).then_inc(sig_ready, 1)
                        if s == 0:
                            act.wait_ge(sq_free, sq0 + 6)
                            nc.scalar.activation(full(root[:]), acc(2), ACT.Sqrt, bias=epsb[GN_EPS],
                                                 scale=1.0 / (4 * P)).then_inc(root_ready, 1)
                        split_value(i0 + 4 * hd + (8 + s), s % 2, rh[:, s, :], v0 + 4 * hd + (8 + s))
                    for s in range(4):
                        split_ahead(quad + 3, s)
                with act.Fori(0, KT) as j:
                    quad = quad0 + Q_CONV + j
                    for s in range(4):
                        split_ahead(quad, s)
                        if s == 0:
                            nc.scalar.activation(full(eh[:]), acc(0), ACT.Identity,
                                                 bias=bias(quad, 0)).then_inc(acc_free[0], 1)
                        if s == 3:
                            nc.scalar.activation(full(ea[:, 1, :]), acc(1), ACT.Sigmoid,
                                                 bias=bias(quad, 3)).then_inc(sig_ready, 1)
                            split_value(i0 + 24 + j, 0, tile(ch, j), v0 + 24 + j)
                with act.Fori(0, 2) as r:
                    quad = quad0 + Q_MERGE + 3 * r
                    for n in range(12):
                        t, m = n // 3, n % 3
                        split_ahead(quad + n // 4, n % 4)
                        if m == 0:
                            act.wait_ge(y_ready, 8 * lay + 4 * r + (t + 1))
                        dst = (ya, g1, g2)[m][:, t % 2, :]
                        if m == 0:
                            nc.scalar.activation(full(dst), acc(n % 2), ACT.Copy).then_inc(acc_free[n % 2], 1)
                        else:
                            nc.scalar.activation(full(dst), acc(n % 2), ACT.Sigmoid,
                                                 bias=bias(quad + n // 4, n % 4)).then_inc(acc_free[n % 2], 1)
                for k in range(KT):
                    act.wait_ge(y_ready, 8 * lay + (k + 3))
                    nc.scalar.activation(uh[:, k, :], y[:, k, :], ACT.Copy).then_inc(valhi_ready, 1)
                with act.Fori(0, 2) as r:
                    for s in range(4):
                        split_ahead(quad0 + Q_WO + r, s)
                        if s == 0:
                            act.wait_ge(vallo_ready, i0 + 40)
                        nc.scalar.activation(full(tile(y, 4 * r + s)), acc(s % 2), ACT.Copy)\
                            .then_inc(acc_free[s % 2], 1)
                act.drain()
                norm_stats(32 * lay + 48, 6 * lay + 8, lambda k: y[:, k, :], KT, D, EPS, 0)

        @block.vector
        def _(dve):
            v = nc.vector

            def low_part(index, slot, dst, hi, c0=0):
                dve.wait_ge(valhi_ready, index + 1)
                v.tensor_tensor(dst, val[:, slot, c0:L], hi.bitcast(F32), ALU.subtract).then_inc(vallo_ready, 1)
                dve.drain()

            def inv_root(nth):
                dve.wait_ge(root_ready, nth + 2)
                v.reciprocal(rstd[:], root[:])
                dve.drain()

            def apply_norm(index, nth, src, wcol, c0):
                dve.wait_ge(root_ready, nth + 2)
                v.reciprocal(rstd[:, c0:L], root[:, c0:L])
                dve.drain()
                for k in range(KT + 1):
                    if k < KT:
                        v.scalar_tensor_tensor(val[:, k % 2, c0:L], src[:, k, c0:L], col(wcol + k), rstd[:, c0:L],
                                               ALU.mult, ALU.mult).then_inc(val_ready, 1)
                    if k >= 1:
                        low_part(index + k - 1, (k - 1) % 2, ul[:, k - 1, c0:L], uh[:, k - 1, c0:L], c0)

            dve.wait_ge(small_loaded, 16 * 7)
            v.tensor_tensor(lbt[:, 0, :], vec[:, V_LB:V_LB + 4], vec[:, V_LB:V_LB + 4], ALU.subtract).then_inc(lb_in, 1)
            dve.wait_ge(lb_exp, 1)
            v.reciprocal(lbt[:, 2, :], lbt[:, 1, :])
            dve.drain()
            v.tensor_tensor(lbt[:, 3, :], lbt[:, 1, :], lbt[:, 2, :], ALU.mult)
            dve.drain()
            v.tensor_tensor(lbt[:, 4, :], lbt[:, 3, :], lbt[:, 3, :], ALU.subtract)
            dve.drain()
            v.tensor_scalar(lbt[:, 5, :], lbt[:, 4, :], -1.0, 1.0, ALU.mult, ALU.add)
            dve.wait_ge(wff_hi, 1)
            v.tensor_tensor(wffl[:], wff_raw[:], wffh[:].bitcast(F32), ALU.subtract).then_inc(wff_lo, 1)
            dve.wait_ge(h_loaded, 32)
            apply_norm(0, 0, h, V_MIX, 0)
            dve.wait_ge(ff_ln, 1)
            v.scalar_tensor_tensor(cz[:], cz[:], 0.0, ct[:], ALU.min, ALU.subtract)
            dve.wait_ge(consts_set, 1)
            dve.drain()
            v.tensor_tensor_scan(ccum[:], cone[:], cz[:], 0.0, ALU.mult, ALU.add).then_inc(cum_ready, 1)
            for j in range(4):
                dve.wait_ge(fv_psum, j + 1)
                v.tensor_copy(vnat[:, 1:5, P * j:P * j + P], ps[:, 4, :].rearrange("p (a b) -> p a b", a=4))
                v.tensor_copy(vnat[0:META, 0, P * j:P * j + P], ps[0:META, 5, 0:P]).then_inc(fv_ready, 1)
            dve.drain()

            with dve.Fori(0, 4) as hp:
                dve.wait_ge(heads_psum, 8 * hp + 1)
                v.tensor_copy(qs[:], tile(proj, hp))
                v.tensor_copy(ks[:], tile(proj, hp + 4))
                v.tensor_copy(selp[:], sel[:, bass.ds(2 * hp, 2), :])
                v.tensor_copy(vs[0:META, 0, :], vnat[0:META, 0, bass.ds(P * hp, P)])
                v.tensor_copy(vs[:, 1:5, :], vnat[:, 1:5, bass.ds(P * hp, P)]).then_inc(fox_in, 1)
                for n in range(9):
                    if n < 8:
                        b, i = n % 2, n % 4
                        nk = KEYS[i + 1][1]
                        dve.wait_ge(scores_ready, 8 * hp + (n + 1))
                        v.tensor_reduce(fmax[:, b:b + 1], scores(b)[:, 0:nk], AX.X, ALU.max)
                        dve.drain()
                        dve.wait_ge(probs_ready, 8 * hp + (n + 1))
                        v.tensor_scalar(fneg[:, b:b + 1], fmax[:, b:b + 1], -0.125, None, ALU.mult)\
                            .then_inc(negmax_ready, 1)
                    if n >= 1:
                        m = n - 1
                        b, i, e = m % 2, m % 4, m // 4
                        dve.wait_ge(probsT_psum, 8 * hp + (m + 3))
                        v.tensor_copy(pT[0:META, b, 0, :], ps[0:META, 5, 0:P])
                        v.tensor_copy(pT[:, b, 1:i + 2, :], ps[:, 4, 0:P * (i + 1)].rearrange(
                            "p (a b) -> p a b", b=P)).then_inc(probsT_ready, 1)
                        dve.wait_ge(probs_ready, 8 * hp + (m + 3))
                        v.reciprocal(finv[:, b:b + 1], fsum[:, b:b + 1])
                        dve.drain()
                        dve.wait_ge(heads_psum, 8 * hp + (m + 2))
                        v.tensor_scalar(onat[:, i, bass.ds(P * hp + 64 * e, 64)], ps[:, 6 + b, 0:64],
                                        finv[:, b:b + 1], None, ALU.mult).then_inc(heads_ready, 1)
            for k in range(4):
                dve.wait_ge(headsT_psum, k + 1)
                v.tensor_copy(val[:, k % 2, META:L], ps[:, k, :]).then_inc(val_ready, 1)
                low_part(8 + k, k % 2, ul[:, k, META:L], uh[:, k, META:L], META)

            dve.wait_ge(masks_set, 1)
            dve.wait_ge(masks_loaded, 16)
            with dve.Fori(0, HEADS) as hd:
                lev = (LEVELS + 1) * hd
                dve.wait_ge(hg_sig, hd + 1)
                v.tensor_copy(vt[:], tile(proj, hd + 20)).then_inc(hg_vt, 1)
                v.tensor_scalar(kin[:], sgf[:], lbt[:, 5, bass.ds(hd, 1)], None, ALU.mult)
                v.scalar_tensor_tensor(qh[:], tile(proj, hd + 12), float(P) ** -0.5, sgq[:], ALU.mult, ALU.mult)
                v.memset(amat[:], 0.0)
                dve.drain()
                v.tensor_scalar(fgate[:], kin[:], -1.0, 1.0, ALU.mult, ALU.add)
                dve.drain()
                v.tensor_scalar(fgate[:], fgate[:], F_MIN, None, ALU.max).then_inc(hg_f, 1)
                dve.wait_ge(hg_vpsum, hd + 1)
                v.tensor_copy(vn[:, 1:5, :], ps[:, 4, :].rearrange("p (a b) -> p a b", a=4))
                v.tensor_copy(vn[0:META, 0, :], ps[0:META, 5, 0:P]).then_inc(hg_vn, 1)
                dve.wait_ge(hg_g, hd + 1)

                def exponents(l):
                    b = l % 2
                    if l == 0:
                        v.tensor_tensor(eq[:, b, :], gl[:, META:L], odd[:], ALU.mult)
                        dve.drain()
                        v.tensor_scalar(ek[:, b, :], eq[:, b, :], -1.0, None, ALU.mult).then_inc(hg_exp_in, 1)
                        return
                    v.tensor_tensor_scan(eq[:, b, :], resets[:, l - 1, :], gl[:, META:L], 0.0, ALU.mult, ALU.add)
                    dve.drain()
                    w = 2 ** l
                    e3 = eq[:, b, :].rearrange("p (n b) -> p n b", b=w)
                    v.tensor_tensor(ek[:, b, :].rearrange("p (n b) -> p n b", b=w),
                                    e3[:, :, w - 1:w].broadcast_to([P, SEQ // w, w]), e3,
                                    ALU.subtract).then_inc(hg_exp_in, 1)

                exponents(0)
                for l in range(LEVELS + 2):
                    b = l % 2
                    if l <= LEVELS:
                        if l < LEVELS:
                            exponents(l + 1)
                        dve.wait_ge(hg_exp_out, lev + (l + 1))
                        if l >= 2:
                            dve.wait_ge(hg_s, LEVELS * hd + (l - 1))
                        v.tensor_tensor(ql[:, b, :], qh[:, META:L], xq[:, b, :], ALU.mult)
                        v.tensor_tensor(kl[:, b, :], kin[:, META:L], xk[:, b, :], ALU.mult).then_inc(hg_qk, 1)
                    if 1 <= l <= LEVELS:
                        m = l - 1
                        dve.drain()
                        dve.wait_ge(hg_s, LEVELS * hd + l)
                        v.memset(carrier[:, m:m + 1], 0.0)
                        v.copy_predicated(amat.rearrange("p (a b) -> p a b", a=XT),
                                          masks[:, m:m + 1, :].broadcast_to([P, XT, P]),
                                          ps[:, 6 + m % 2, :].rearrange("p (a b) -> p a b", a=XT)).then_inc(hg_pred, 1)
                v.tensor_tensor_scan(pm[:], ones[:, 0:META], gl[:, 0:META], 0.0, ALU.mult, ALU.add)
                dve.drain()
                v.tensor_tensor(em[:], pm[:, META - 1:META].broadcast_to([P, META]), pm[:],
                                ALU.subtract).then_inc(hg_min, 1)
                dve.wait_ge(hg_mout, hd + 1)
                v.tensor_tensor(km[:], kin[:, 0:META], xm[:], ALU.mult).then_inc(hg_km, 1)
                dve.wait_ge(hg_kpsum, hd + 1)
                v.tensor_copy(kn[:, 1:4, :], ps[:, 4, 0:3 * P].rearrange("p (a b) -> p a b", a=3))
                v.tensor_copy(kn[0:META, 0, :], ps[0:META, 5, 0:P]).then_inc(hg_kn, 1)
                dve.wait_ge(hg_upsum, hd + 1)
                v.tensor_copy(st[:, 0, :], ps[:, 4, 0:P])
                for i in range(1, XT):
                    dve.drain()
                    step = v.scalar_tensor_tensor(st[:, i, :], st[:, i - 1, :],
                                                  xq[:, LEVELS % 2, P * i - 1:P * i],
                                                  ps[:, 4, P * i:P * i + P], ALU.mult, ALU.add)
                step.then_inc(hg_state, 1)
                dve.wait_ge(hg_root, hd + 1)
                v.reciprocal(rstd[:, 0:SEQ], root[:, 0:SEQ])
                v.tensor_tensor(sgg[:], tile(proj, hd + 24), sgg[:], ALU.mult)
                dve.drain()
                v.scalar_tensor_tensor(ot[:], ps[:, 0, :], col(V_HNORM), rstd[:, 0:SEQ], ALU.mult, ALU.mult)
                dve.drain()
                v.tensor_tensor(val[:, 0, META:L], ot[:], sgg[:, META:L], ALU.mult).then_inc(val_ready, 1)
                dve.wait_ge(valhi_ready, hd + 13)
                v.tensor_tensor(tile(ul, hd + 4)[:, META:L], val[:, 0, META:L],
                                tile(uh, hd + 4)[:, META:L].bitcast(F32), ALU.subtract).then_inc(vallo_ready, 1)
                dve.drain().then_inc(hg_inv, 1)

            with dve.Fori(0, 2) as r:
                for s in range(4):
                    dve.wait_ge(panel_done, 4 * r + (4 * Q_OUT + s + 1))
                    t = seq(tile(h, 4 * r + s))
                    v.tensor_tensor(t, acc(s % 2, SEQ), t, ALU.add).then_inc(acc_free[s % 2], 1)
            dve.drain().then_inc(h_ready, 1)
            apply_norm(16, 1, h, V_FFN, META)
            with dve.Fori(0, 11) as r:
                for s in range(4):
                    j = s // 2
                    if s % 2 == 0:
                        dve.wait_ge(sig_ready, 2 * r + (j + 1))
                        v.tensor_tensor(seq(gs[:]), acc(0, SEQ), seq(ea[:, j, :]), ALU.mult).then_inc(acc_free[0], 1)
                        dve.drain()
                    else:
                        dve.wait_ge(panel_done, 4 * r + (4 * Q_FF + s + 1))
                        v.tensor_tensor(seq(val[:, j, :]), acc(1, SEQ), seq(gs[:]), ALU.mult).then_inc(acc_free[1], 1)
                        dve.drain().then_inc(val_ready, 1)
                        low_part(2 * r + (24 + j), j, tile(gl_, 2 * r + j), tile(gh, 2 * r + j), META)
            with dve.Fori(0, 2) as r:
                for t in range(4):
                    dve.wait_ge(panel_done, 12 * r + (4 * Q_DOWN + 3 * t + 3))
                    x = seq(tile(h, 4 * r + t))
                    v.tensor_tensor(x, acc(t % 2, SEQ), x, ALU.add).then_inc(acc_free[t % 2], 1)
            dve.drain().then_inc(h_ready, 1)
            dve.wait_ge(root_ready, 4)
            v.reciprocal(rstd[:, META:L], root[:, META:L])
            dve.drain()
            for k in range(KT):
                v.scalar_tensor_tensor(h[:, k, META:L], h[:, k, META:L], col(V_FINAL + k), rstd[:, META:L],
                                       ALU.mult, ALU.mult)
            v.tensor_copy(h[:, :, 0:META], meta2[:])
            dve.drain().then_inc(h_ready, 1)

            with dve.Fori(0, 2) as lay:
                quad0 = lay * Q_LAYER + Q_B2
                i0 = 40 * lay + 46
                v.memset(y[:], 0.0)
                dve.wait_ge(root_ready, 6 * lay + 5)
                v.reciprocal(rstd[:], root[:])
                dve.drain()
                for k in range(KT + 1):
                    if k < KT:
                        v.scalar_tensor_tensor(val[:, k % 2, :], h[:, k, :], col(8 * lay + (V_PRE + k)), rstd[:],
                                               ALU.mult, ALU.mult).then_inc(val_ready, 1)
                    if k >= 1:
                        low_part(i0 + (k - 1), (k - 1) % 2, ul[:, k - 1, :], uh[:, k - 1, :])
                dve.wait_ge(tables_loaded, 64)
                with dve.Fori(0, HEADS) as hd:
                    quad = 4 * hd + quad0
                    it = 4 * lay + hd
                    a0 = A_LAYER * lay + A_HEAD * hd + A_B2
                    for n, dst in enumerate((kr, qr)):
                        dve.wait_ge(acc_free[0], a0 + (n + 2))
                        dve.wait_ge(acc_free[1], a0 + (n + 2))
                        x1, x2 = kq[:, 2 * n, :], kq[:, 2 * n + 1, :]
                        v.tensor_tensor(r1[:], x1, cos[:], ALU.mult)
                        v.tensor_tensor(r2[:], x2, sin[:], ALU.mult)
                        dve.drain()
                        v.tensor_tensor(dst[:, 0, :], r1[:], r2[:], ALU.subtract)
                        dve.drain()
                        v.tensor_tensor(r1[:], x1, sin[:], ALU.mult)
                        v.tensor_tensor(r2[:], x2, cos[:], ALU.mult)
                        dve.drain()
                        v.tensor_tensor(dst[:, 1, :], r1[:], r2[:], ALU.add).then_inc(rope_ready, 1)
                        dve.drain()
                    for j in range(4):
                        dve.wait_ge(vt_psum, 4 * it + (j + 1))
                        v.tensor_copy(rvn[:, 1:5, P * j:P * j + P], ps[:, 4, :].rearrange("p (a b) -> p a b", a=4))
                        v.tensor_copy(rvn[0:META, 0, P * j:P * j + P], ps[0:META, 5, 0:P]).then_inc(vn_ready, 1)
                    dve.drain()
                    v.tensor_reduce(vmean[:, 1:5], rvn[:, 1:5, :], AX.X, ALU.add)
                    v.tensor_reduce(vmean[0:META, 0:1], rvn[0:META, 0, :], AX.X, ALU.add)
                    dve.drain()
                    v.tensor_scalar(vneg[:, 1:5], vmean[:, 1:5], -1.0 / (4 * P), None, ALU.mult)
                    v.tensor_scalar(vneg[0:META, 0:1], vmean[0:META, 0:1], -1.0 / (4 * P), None, ALU.mult)
                    dve.drain()
                    v.tensor_scalar(rvn[0:META, 0, :], rvn[0:META, 0, :], vneg[0:META, 0:1], None, ALU.add)
                    for i in range(1, 5):
                        last = v.tensor_scalar(rvn[:, i, :], rvn[:, i, :], vneg[:, i:i + 1], None, ALU.add)
                    last.then_inc(v_centred, 1)
                    dve.wait_ge(s_psum, 5 * it + 1)
                    dm = decm[:, bass.ds(hd, 1), :].rearrange("p a b -> p (a b)")
                    v.tensor_tensor(sd[0:META, 0, META:L], ps[0:META, 6, :], dm[:, META:L], ALU.mult)
                    v.tensor_tensor(sd[0:META, 0, 0:META], ps[0:META, 7, 0:META], dm[:, 0:META],
                                    ALU.mult).then_inc(sd_ready, 1)
                    for i in range(XT):
                        w = SEQ - P * i
                        dx = decx[:, bass.ds(hd, 1), :].rearrange("p a b -> p (a b)")
                        dve.wait_ge(s_psum, 5 * it + (i + 2))
                        v.tensor_tensor(sd[:, i + 1, META + P * i:L], ps[:, 4 + i % 2, 0:w], dx[:, 0:w],
                                        ALU.mult).then_inc(sd_ready, 1)
                    dve.wait_ge(o_psum, 4 * it + 1)
                    v.tensor_copy(o[:, :, 0:META], ps[:, 3, 320:320 + 4 * META].rearrange("p (a b) -> p a b", a=4))
                    for j in range(4):
                        dve.wait_ge(o_psum, 4 * it + (j + 1))
                        last = v.tensor_copy(o[:, j, META:L], ps[:, 4 + j, :])
                    last.then_inc(o_ready, 1)
                    inv_root(6 * lay + hd + 4)
                    for j in range(4):
                        v.scalar_tensor_tensor(o[:, j, :], o[:, j, :], col(16 * lay + 4 * hd + (V_GN + j)), rstd[:],
                                               ALU.mult, ALU.mult)
                    dve.drain()
                    for s in range(4):
                        dve.wait_ge(sig_ready, 24 * lay + 4 * hd + (22 + s + 1))
                        v.scalar_tensor_tensor(full(zs[:]), acc(s % 2), bias(quad + 2, s), full(ea[:, s % 2, :]),
                                               ALU.add, ALU.mult).then_inc(acc_free[s % 2], 1)
                        dve.drain()
                        v.tensor_tensor(val[:, s % 2, :], zs[:], o[:, s, :], ALU.mult).then_inc(val_ready, 1)
                        low_part(i0 + 4 * hd + (8 + s), s % 2, rl[:, s, :], rh[:, s, :])
                    for s in range(4):
                        dve.wait_ge(half_done, 4 * it + (s + 1))
                        v.tensor_tensor(full(y[:, 2 * s, :]), acc(0), full(y[:, 2 * s, :]), ALU.add)\
                            .then_inc(acc_free[0], 1)
                        dve.wait_ge(panel_done, 4 * quad + (12 + s + 1))
                        v.tensor_tensor(full(y[:, 2 * s + 1, :]), acc(1), full(y[:, 2 * s + 1, :]), ALU.add)\
                            .then_inc(acc_free[1], 1)
                with dve.Fori(0, KT) as j:
                    quad = quad0 + Q_CONV + j
                    a0 = A_LAYER * lay + 2 * j + (A_B2 + A_CONV)
                    dve.wait_ge(acc_free[0], a0 + 2)
                    dve.wait_ge(panel_done, 4 * quad + 2)
                    v.memset(cu[:, 0:2], 0.0)
                    v.scalar_tensor_tensor(full(cu[:, 2:L + 2]), acc(1), bias(quad, 1), full(eh[:]),
                                           ALU.add, ALU.mult).then_inc(acc_free[1], 1)
                    dve.drain()
                    cw = 24 * lay + j + V_CW
                    v.tensor_scalar(c0[:], cu[:, 2:L + 2], col(cw + 16), col(8 * lay + j + V_CB), ALU.mult, ALU.add)
                    dve.drain()
                    v.scalar_tensor_tensor(c1[:], cu[:, 1:L + 1], col(cw + 8), c0[:], ALU.mult, ALU.add)
                    dve.drain()
                    v.scalar_tensor_tensor(c2[:], cu[:, 0:L], col(cw), c1[:], ALU.mult, ALU.add)
                    dve.drain()
                    dve.wait_ge(panel_done, 4 * quad + 3)
                    v.scalar_tensor_tensor(full(cb_[:]), acc(0), bias(quad, 2), full(c2[:]),
                                           ALU.add, ALU.mult).then_inc(acc_free[0], 1)
                    dve.wait_ge(sig_ready, 24 * lay + j + (22 + 16 + 1))
                    v.scalar_tensor_tensor(full(cs[:]), acc(1), bias(quad, 3), full(ea[:, 1, :]),
                                           ALU.add, ALU.mult).then_inc(acc_free[1], 1)
                    dve.drain()
                    v.tensor_tensor(val[:, 0, :], cs[:], cb_[:], ALU.mult).then_inc(val_ready, 1)
                    low_part(i0 + 24 + j, 0, tile(cl, j), tile(ch, j))
                with dve.Fori(0, 2) as r:
                    a0 = A_LAYER * lay + 6 * r + (A_B2 + A_MERGE)
                    for t in range(4):
                        for n in range(3 * t + 1, 3 * t + 3):
                            dve.wait_ge(acc_free[n % 2], a0 + (n // 2 + 2))
                        yt = tile(y, 4 * r + t)
                        v.tensor_tensor(m1[:], ya[:, t % 2, :], g1[:, t % 2, :], ALU.mult)
                        v.tensor_tensor(m2[:], yt, g2[:, t % 2, :], ALU.mult)
                        dve.drain()
                        v.tensor_tensor(yt, m1[:], m2[:], ALU.add).then_inc(y_ready, 1)
                        dve.drain()
                for k in range(KT):
                    dve.wait_ge(valhi_ready, i0 + (33 + k))
                    v.tensor_tensor(ul[:, k, :], y[:, k, :], uh[:, k, :].bitcast(F32), ALU.subtract)\
                        .then_inc(vallo_ready, 1)
                inv_root(6 * lay + 8)
                for k in range(KT):
                    v.scalar_tensor_tensor(m1[:], y[:, k, :], col(8 * lay + (V_POST + k)), rstd[:],
                                           ALU.mult, ALU.mult)
                    dve.drain()
                    v.tensor_tensor(h[:, k, :], h[:, k, :], m1[:], ALU.add)
                    dve.drain()
                dve.drain().then_inc(h_ready, 1)

        @block.tensor
        def _(pe):
            mm = nc.tensor.matmul

            for s in acc_free:
                pe.sem_inc(s, 1)
            pe.sem_inc(sq_free, 2)
            pe.sem_inc(root_ready, 1)
            pe.sem_inc(probsT_psum, 2)
            pe.sem_inc(heads_ready, 2)
            pe.sem_inc(probs_ready, 2)
            pe.sem_inc(heads_psum, 1)
            pe.sem_inc(hg_inv, 1)
            pe.sem_inc(y_ready, 2)

            def product(slot, wslot, xh, xl, k0, k1, rows0, first, last, n, ready=None):
                half = n // 2
                c = L - n
                for k in range(k0, k1):
                    if ready is not None:
                        pe.wait_ge(vallo_ready, ready + (k + 1))
                    wcol = slice(P * k, P * k + P)
                    for w, x, part in ((wh, xh, 0), (wh, xl, 1), (wl, xh, 2)):
                        for a in range(2):
                            out = mm(ps[:, 2 * slot + a, 0:half], w[:, wslot, wcol],
                                     x(rows0 + k - k0, c + a * half, c + (a + 1) * half),
                                     start=first and k == k0 and part == 0,
                                     stop=last and k == k1 - 1 and part == 2)
                return out

            def xu(t, off=0):
                return lambda k, a, b: t[:, k, a - off:b - off]

            def use_panel(quad, s, a, xh=xu(uh), xl=xu(ul), n=L, ready=None):
                pe.wait_ge(lo_ready, 4 * quad + (s + 1))
                pe.wait_ge(acc_free[s % 2], a + 1)
                product(s % 2, s % 2, xh, xl, 0, KT, 0, True, True, n, ready).then_inc(panel_done, 1)

            def norm_sum(first, nth, tiles, n):
                pe.wait_ge(root_ready, nth + 1)
                half, c = n // 2, L - n
                for k in range(tiles):
                    pe.wait_ge(sq_ready, first + (k + 1))
                    for a in range(2):
                        out = mm(ps[:, 4 + a, 0:half], ones[:], sq[:, k % 2, c + a * half:c + (a + 1) * half],
                                 start=k == 0, stop=k == tiles - 1)
                    out.then_inc(sq_free, 1)

            def transposes(src, done, blocks=KEYS):
                for n, (a, b) in enumerate(blocks):
                    dst = ps[0:b - a, 5, 0:P] if b - a == META else ps[:, 4, P * (n - 1):P * n]
                    out = nc.tensor.transpose(dst, src[:, a:b], ident[:])
                out.then_inc(done, 1)

            pe.wait_ge(small_loaded, 16 * 7)
            pe.wait_ge(consts_set, 1)
            norm_sum(0, 0, KT, L)
            pe.wait_ge(wff_lo, 1)
            pe.wait_ge(root_ready, 2)
            for k in range(KT):
                pe.wait_ge(vallo_ready, k + 1)
                for w, x, part in ((wffh, uh, 0), (wffh, ul, 1), (wffl, uh, 2)):
                    for a in range(2):
                        out = mm(ps[0:8, 4 + a, 0:L // 2], w[:, 8 * k:8 * k + 8], x[:, k, a * (L // 2):(a + 1) * (L // 2)],
                                 start=k == 0 and part == 0, stop=k == KT - 1 and part == 2)
            out.then_inc(ff_psum, 1)
            with pe.Fori(0, 7) as q:
                for s in range(4):
                    use_panel(q, s, 2 * q + s // 2)
            pe.wait_ge(ff_ln, 1)
            pe.wait_ge(acc_free[1], A_OUT + 1)
            for j in range(4):
                if j:
                    pe.wait_ge(fv_ready, j)
                transposes(proj[:, 8 + j, :], fv_psum)
            pe.wait_ge(cum_ready, 1)
            pe.wait_ge(fv_ready, 4)
            pe.wait_ge(acc_free[0], A_OUT + 1)
            with pe.Fori(0, 4) as hp:
                pe.wait_ge(fox_in, hp + 1)
                for n in range(9):
                    if n < 8:
                        b, i, e = n % 2, n % 4, n // 4
                        q0, nk = KEYS[i + 1]
                        pe.wait_ge(probs_ready, 8 * hp + (n + 1))
                        for bank, (ka, kb) in enumerate(((0, min(nk, 272)), (272, nk))):
                            if ka >= kb:
                                continue
                            c = 240 if bank == 0 else 0
                            diag = ka <= q0 < kb
                            dst = ps[:, 2 * b + bank, c:c + kb - ka]
                            mm(dst, qs[64 * e:64 * e + 64, q0:nk], ks[64 * e:64 * e + 64, ka:kb], start=True, stop=False)
                            out = mm(dst, selp[:, e, :], ccum[:, ka:kb], start=False, stop=not diag)
                            if diag:
                                out = mm(ps[:, 2 * b + bank, c + q0 - ka:c + nk - ka], ident[:], causal[:],
                                         start=False, stop=True)
                        out.then_inc(scores_ready, 1)
                    if n >= 1:
                        m = n - 1
                        b, i, e = m % 2, m % 4, m // 4
                        pe.wait_ge(probs_ready, 8 * hp + (m + 3))
                        if m >= 1:
                            pe.wait_ge(probsT_ready, 8 * hp + m)
                        transposes(probs[:, b, :], probsT_psum, KEYS[:i + 2])
                        pe.wait_ge(probsT_ready, 8 * hp + (m + 1))
                        pe.wait_ge(heads_ready, 8 * hp + (m + 1))
                        for t in range(i + 2):
                            rows = META if t == 0 else P
                            out = mm(ps[:, 6 + b, 0:64], pT[0:rows, b, t, :], vs[0:rows, t, 64 * e:64 * e + 64],
                                     start=t == 0, stop=t == i + 1)
                        out.then_inc(heads_psum, 1)
            pe.wait_ge(heads_ready, 34)
            for k in range(4):
                for i in range(XT):
                    out = nc.tensor.transpose(ps[:, k, P * i:P * i + P], onat[:, i, P * k:P * k + P], ident[:])
                out.then_inc(headsT_psum, 1)

            with pe.Fori(0, HEADS) as hd:
                pe.wait_ge(hg_vt, hd + 1)
                pe.wait_ge(vallo_ready, hd + 12)
                transposes(vt[:], hg_vpsum)
                for l in range(LEVELS + 1):
                    b = l % 2
                    pe.wait_ge(hg_qk, (LEVELS + 1) * hd + (l + 1))
                    if l == LEVELS:
                        break
                    if l >= 2:
                        pe.wait_ge(hg_pred, LEVELS * hd + (l - 1))
                    for i in range(XT):
                        out = mm(ps[:, 6 + b, P * i:P * i + P], kl[:, b, P * i:P * i + P], ql[:, b, P * i:P * i + P],
                                 start=True, stop=True)
                    out.then_inc(hg_s, 1)
                last = LEVELS % 2
                pe.wait_ge(hg_km, hd + 1)
                pe.wait_ge(hg_vn, hd + 1)
                nc.tensor.transpose(ps[0:META, 5, 0:P], km[:], ident[:])
                for i in range(XT - 1):
                    out = nc.tensor.transpose(ps[:, 4, P * i:P * i + P], kl[:, last, P * i:P * i + P], ident[:])
                out.then_inc(hg_kpsum, 1)
                pe.wait_ge(hg_kn, hd + 1)
                for i in range(XT):
                    rows = META if i == 0 else P
                    out = mm(ps[:, 4, P * i:P * i + P], kn[0:rows, i, :], vn[0:rows, i, :], start=True, stop=True)
                out.then_inc(hg_upsum, 1)
                pe.wait_ge(hg_pred, LEVELS * hd + LEVELS)
                pe.wait_ge(hg_state, hd + 1)
                for i in range(XT):
                    dst = ps[:, 0, P * i:P * i + P]
                    mm(dst, vn[:, i + 1, :], amat[:, P * i:P * i + P], start=True, stop=False)
                    out = mm(dst, st[:, i, :], ql[:, last, P * i:P * i + P], start=False, stop=True)
                out.then_inc(hg_o, 1)
                pe.wait_ge(hg_sq, hd + 1)
                mm(ps[:, 1, :], ones[:], sq[:, 0, 0:SEQ], start=True, stop=True).then_inc(hg_ss, 1)

            pe.wait_ge(vallo_ready, 16)
            with pe.Fori(0, 2) as r:
                for s in range(4):
                    use_panel(r + Q_OUT, s, 2 * r + (A_OUT + s // 2), n=SEQ)
            norm_sum(8, 1, KT, SEQ)
            pe.wait_ge(vallo_ready, 24)
            with pe.Fori(0, 11) as r:
                for s in range(4):
                    use_panel(r + Q_FF, s, 2 * r + (A_FF + s // 2), n=SEQ)
            pe.wait_ge(vallo_ready, 24 + FT)
            with pe.Fori(0, 2) as r:
                for n in range(12):
                    t, third = n // 3, n % 3
                    pe.wait_ge(lo_ready, 12 * r + (4 * Q_DOWN + n + 1))
                    if third == 0:
                        pe.wait_ge(acc_free[t % 2], 2 * r + (A_DOWN + t // 2 + 1))
                    product(t % 2, n % 2, xu(gh, META), xu(gl_, META), 0, KT if third < 2 else FT - 2 * KT,
                            KT * third, third == 0, third == 2, SEQ).then_inc(panel_done, 1)
            norm_sum(16, 2, KT, SEQ)

            with pe.Fori(0, 2) as lay:
                quad0 = lay * Q_LAYER + Q_B2
                i0 = 40 * lay + 46
                norm_sum(32 * lay + 24, 6 * lay + 3, KT, L)
                with pe.Fori(0, HEADS) as hd:
                    pe.wait_ge(vallo_ready, i0 + 8)
                    quad = 4 * hd + quad0
                    it = 4 * lay + hd
                    a0 = A_LAYER * lay + A_HEAD * hd + A_B2
                    for s in range(4):
                        use_panel(quad, s, a0 + s // 2)

                    def v_transposes(j):
                        pe.wait_ge(acc_free[j % 2], a0 + (2 + j // 2 + 2))
                        if j:
                            pe.wait_ge(vn_ready, 4 * it + j)
                        else:
                            pe.wait_ge(root_ready, 6 * lay + hd + 5)
                        transposes(vraw[:, j % 2, :], vt_psum)

                    for s in range(4):
                        use_panel(quad + 1, s, a0 + (2 + s // 2))
                        if s:
                            v_transposes(s - 1)
                    v_transposes(3)
                    pe.wait_ge(rope_ready, 2 * it + 2)
                    for j, (ka, kb) in enumerate(KEYS):
                        if j == 1:
                            pe.wait_ge(vn_ready, 4 * it + 4)
                        if j >= 3:
                            pe.wait_ge(sd_ready, 5 * it + (j - 1))
                        bank = 6 if j == 0 else 4 + (j - 1) % 2
                        qa = META if j == 0 else ka
                        for c in range(2):
                            out = mm(ps[0:kb - ka, bank, 0:L - qa], kr[:, c, ka:kb], qr[:, c, qa:L],
                                     start=c == 0, stop=c == 1)
                        if j == 0:
                            for c in range(2):
                                out = mm(ps[0:META, 7, 0:META], kr[:, c, 0:META], qr[:, c, 0:META],
                                         start=c == 0, stop=c == 1)
                        out.then_inc(s_psum, 1)
                    pe.wait_ge(v_centred, it + 1)
                    pe.wait_ge(sd_ready, 5 * it + 5)
                    for j in range(4):
                        mm(ps[:, 3, 320 + META * j:320 + META * (j + 1)], rvn[0:META, 0, P * j:P * j + P],
                           sd[0:META, 0, 0:META], start=True, stop=True)
                    for j in range(4):
                        for t, (ka, kb) in enumerate(KEYS):
                            qa = META if t == 0 else ka
                            out = mm(ps[:, 4 + j, qa - META:SEQ], rvn[0:kb - ka, t, P * j:P * j + P],
                                     sd[0:kb - ka, t, qa:L], start=t == 0, stop=t == 4)
                        out.then_inc(o_psum, 1)
                    use_panel(quad + 2, 0, a0 + 4)
                    pe.wait_ge(o_ready, it + 1)
                    norm_sum(32 * lay + 4 * hd + 32, 6 * lay + hd + 4, 4, L)
                    for s in range(1, 4):
                        use_panel(quad + 2, s, a0 + (4 + s // 2))
                    for s in range(4):
                        pe.wait_ge(lo_ready, 4 * quad + (12 + s + 1))
                        pe.wait_ge(acc_free[0], a0 + (6 + s + 1))
                        product(0, s % 2, xu(rh), xu(rl), 0, 4, 0, True, True, L,
                                i0 + 4 * hd + 8 if s == 0 else None).then_inc(half_done, 1)
                        pe.wait_ge(acc_free[1], a0 + (6 + s + 1))
                        product(1, s % 2, xu(rh), xu(rl), 4, 8, 0, True, True, L).then_inc(panel_done, 1)
                with pe.Fori(0, KT) as j:
                    for s in range(4):
                        use_panel(quad0 + Q_CONV + j, s, A_LAYER * lay + 2 * j + (A_B2 + A_CONV + s // 2))
                with pe.Fori(0, 2) as r:
                    pe.wait_ge(vallo_ready, i0 + 32)
                    for n in range(12):
                        a = A_LAYER * lay + 6 * r + (A_B2 + A_MERGE + n // 2)
                        x = (xu(ch), xu(cl)) if n % 3 == 0 else (xu(uh), xu(ul))
                        use_panel(quad0 + Q_MERGE + 3 * r + n // 4, n % 4, a, *x)
                with pe.Fori(0, 2) as r:
                    pe.wait_ge(vallo_ready, i0 + 40)
                    for s in range(4):
                        use_panel(quad0 + Q_WO + r, s, A_LAYER * lay + 2 * r + (A_B2 + A_WO + s // 2))
                norm_sum(32 * lay + 48, 6 * lay + 8, KT, L)


def panels(w):
    import numpy as np
    k, n = w.shape
    out = np.zeros((n // P, P, KT, P), np.float32)
    out[:, :, :k // P] = w.reshape(k // P, P, n // P, P).transpose(2, 1, 0, 3)
    return out


def weight_stream(i):
    import numpy as np
    win, wd = i["w_in"][0], i["w_ffn_down"][0]
    parts = [panels(win[:, c:c + 512]) for c in (0, 512, 1024, 1544, 2056, 2568, 3080)]
    parts.append(panels(i["w_out"][0]))
    gate, up = panels(i["w_ffn_gate"][0]), panels(i["w_ffn_up"][0])
    parts.append(np.stack([gate, up], 1).reshape(2 * FT, P, KT, P))
    down = [panels(wd[r:r + D]) for r in range(0, FF, D)]
    parts.append(np.stack(down, 1).reshape(3 * KT, P, KT, P))
    for l in range(2):
        w = i["w_in_2"][l]
        p = panels(w)
        wr = i["w_ret_out_2"][l]
        for hd in range(HEADS):
            parts += [p[40 + 2 * hd:42 + 2 * hd], p[32 + 2 * hd:34 + 2 * hd], p[48 + 4 * hd:52 + 4 * hd],
                      p[64 + 4 * hd:68 + 4 * hd]]
            r = wr[512 * hd:512 * hd + 512].reshape(4, P, 4, 2, P)
            parts.append(r.transpose(2, 1, 3, 0, 4).reshape(4, P, KT, P))
        parts.append(np.stack([p[0:8], p[16:24], p[8:16], p[24:32]], 1).reshape(32, P, KT, P))
        parts.append(np.stack([panels(i["w_conv_out_2"][l]), p[80:88], p[88:96]], 1).reshape(24, P, KT, P))
        parts.append(panels(i["w_o_2"][l]))
    parts.append(np.zeros((2, P, KT, P), np.float32))
    return np.concatenate(parts).reshape(4 * QUADS + 2, P, KT * P)


def vector_table(i):
    import numpy as np
    v = np.zeros((P, V_COLS), np.float32)

    def put(c, x):
        x = np.asarray(x).reshape(-1, P)
        v[:, c:c + len(x)] = x.T
    put(V_MIX, i["norm_mix_w"][0])
    put(V_FFN, i["norm_ffn_w"][0])
    put(V_FINAL, i["norm_final_w"])
    put(V_HNORM, i["hgrn_norm_w"][0])
    put(V_LB, i["hgrn_lb_raw"][0])
    for l in range(2):
        put(V_PRE + 8 * l, i["pre_norm_g_2"][l])
        put(V_POST + 8 * l, i["post_norm_g_2"][l])
        put(V_CW + 24 * l, i["conv_w_2"][l])
        put(V_CB + 8 * l, i["conv_b_2"][l])
        put(V_GN + 16 * l, i["ret_gn_g_2"][l])
        b = i["b_in_2"][l].reshape(96, P)
        c = V_BIAS + 4 * Q_LAYER * l
        for hd in range(HEADS):
            put(c + 16 * hd, np.concatenate([b[40 + 2 * hd:42 + 2 * hd], b[32 + 2 * hd:34 + 2 * hd],
                                             b[48 + 4 * hd:52 + 4 * hd], b[64 + 4 * hd:68 + 4 * hd]]))
        put(c + 4 * Q_CONV, np.stack([b[0:8], b[16:24], b[8:16], b[24:32]], 1))
        put(c + 4 * Q_MERGE, np.stack([np.zeros((8, P), np.float32), b[80:88], b[88:96]], 1))
    v[:, V_EPS], v[:, V_EPS + 1] = EPS, GN_EPS
    return v


def tables():
    import numpy as np
    inv = (10000.0 ** (-np.arange(P, dtype=np.float64) / P)).astype(np.float32)
    ang = (np.arange(L, dtype=np.float32)[None, :] * inv[:, None]).astype(np.float64)
    lg = np.log(1.0 - 2.0 ** (-5.0 - np.arange(HEADS)))[None, :, None]
    p, x = np.arange(P)[:, None, None], np.arange(SEQ)[None, None, :]
    decx = np.exp(lg * abs(x - p)) * (p // 64 <= x // 64) / 16.0
    p, x = np.arange(META)[:, None, None], np.arange(L)[None, None, :]
    decm = np.exp(lg * abs(x - p)) / 16.0
    s, t = np.arange(P)[:, None], np.arange(P)[None, :]
    masks = np.zeros((P, LEVELS, P), np.int32)
    masks[:, 0] = (s // 2 == t // 2) & (s <= t)
    for l in range(1, LEVELS):
        b = 2 ** l
        masks[:, l] = (s // b + 1 == t // b) & (s // b % 2 == 0)
    sel = np.zeros((8, 8, P), np.float32)
    sel[np.arange(8), np.arange(8)] = -8.0
    f = np.float32
    return {"cos": np.cos(ang).astype(f), "sin": np.sin(ang).astype(f), "decx": decx.astype(f),
            "decm": decm.astype(f), "masks": masks, "sel": sel, "ident": np.eye(P, dtype=f),
            "causal": np.where(t > s, f(-8e30), f(0)).astype(f)}


def kernel(**inputs):
    import numpy as np
    import concourse.bacc as bacc
    from concourse.bass_utils import run_bass_kernel_spmd as run

    i = {k: np.asarray(a) for k, a in inputs.items()}

    def feature_major(a):
        return np.ascontiguousarray(a.reshape(-1, KT, P).transpose(2, 1, 0))

    arrays = tables()
    arrays["x"] = feature_major(i["x"][0])
    arrays["meta"] = feature_major(i["meta"])
    arrays["meta2"] = feature_major(i["meta_2"])
    arrays["weights"] = weight_stream(i)
    arrays["wff"] = np.ascontiguousarray(i["w_in"][0][:, 1536:1544].reshape(KT, P, 8).transpose(1, 0, 2)).reshape(P, KT * 8)
    arrays["fbias"] = np.ascontiguousarray(i["fox_f_bias"][0].reshape(8, 1))
    arrays["vec"] = vector_table(i)

    nc = bacc.Bacc("TRN2", target_bir_lowering=False, num_devices=1)
    io = {n: nc.dram_tensor("in_" + n, a.shape, mybir.dt.from_np(a.dtype), kind="ExternalInput").ap()
          for n, a in arrays.items()}
    io["out"] = nc.dram_tensor("out", (P, KT, SEQ), F32, kind="ExternalOutput").ap()
    build(nc, io)
    r = run(nc, [{"in_" + n: a for n, a in arrays.items()}], core_ids=[0])
    return r.results[0]["out"].transpose(2, 1, 0).reshape(1, SEQ, D)
```

```python
from contextlib import ExitStack

import concourse.bass as bass
from concourse import mybir

F32 = mybir.dt.float32
F32R = mybir.dt.float32r
BF16 = mybir.dt.bfloat16
I32 = mybir.dt.int32
ALU = mybir.AluOpType
ACT = mybir.ActivationFunctionType
AX = mybir.AxisListType

P = 128
D = 1024
KT = D // P
META = 16
SEQ = 512
L = META + SEQ
XT = SEQ // P
FF = 2816
FT = FF // P
HEADS = 4
EPS = 1e-6
GN_EPS = 1e-5
F_MIN = 9.357622968840175e-14
LEVELS = 7

Q_IN, Q_OUT, Q_FF, Q_DOWN, Q_B2 = 0, 7, 9, 20, 26
Q_HEAD, Q_CONV, Q_MERGE, Q_WO, Q_LAYER = 4, 16, 24, 30, 32
QUADS = Q_B2 + 2 * Q_LAYER
A_OUT, A_FF, A_DOWN, A_B2 = 14, 18, 40, 44
A_HEAD, A_CONV, A_MERGE, A_WO, A_LAYER = 10, 40, 56, 68, 72

V_MIX, V_FFN, V_FINAL, V_HNORM, V_LB, V_PRE, V_POST = 0, 8, 16, 24, 25, 29, 45
V_CW, V_CB, V_GN, V_BIAS = 61, 109, 125, 157
V_EPS = V_BIAS + 2 * 4 * Q_LAYER
V_COLS = V_EPS + 2

KEYS = [(0, META)] + [(META + P * i, META + P * (i + 1)) for i in range(XT)]


def build(nc, io):
    with ExitStack() as ctx:
        def sb(name, shape, dt=F32, scope=ctx):
            return scope.enter_context(nc.sbuf_tensor(name, shape, dt))

        def sem(name):
            return ctx.enter_context(nc.semaphore(name))

        h = sb("h", [P, KT, L])
        uh, ul = sb("uh", [P, KT, L], F32R), sb("ul", [P, KT, L], F32R)
        raw = sb("raw", [P, 4, KT * P])
        wh, wl = sb("wh", [P, 2, KT * P], F32R), sb("wl", [P, 2, KT * P], F32R)
        vec = sb("vec", [P, V_COLS])
        ident = sb("ident", [P, P])
        mean_d, mean_h = sb("mean_d", [P, P]), sb("mean_h", [P, P])
        ones = sb("ones", [P, META])
        val = sb("val", [P, 2, L])
        sq = sb("sq", [P, 2, L])
        ssum = sb("ssum", [P, L])
        rstd = sb("rstd", [P, L])
        meta2 = sb("meta2", [P, KT, META])
        ea = sb("ea", [P, 2, L])

        mix = ExitStack()
        proj = sb("proj", [P, 28, L], F32, mix)
        lbt = sb("lbt", [P, 6, 4], F32, mix)
        fbias = sb("fbias", [8, 1], F32, mix)
        wffh, wffl = sb("wffh", [P, KT * 8], F32R, mix), sb("wffl", [P, KT * 8], F32R, mix)
        cparts = sb("cparts", [96, L], BF16, mix)
        cz, ct, cone, ccum, cres = (proj[0:8, i, :] for i in range(5))
        cparts0 = [sb(f"cpart{n}", [8, L], BF16, mix) for n in range(3)]
        wff_raw = proj[:, 6, 0:KT * 8]
        hg = ExitStack()
        gl, sgq, vt = (sb("hg_" + n, [P, L], F32, hg) for n in ("g", "sgq", "vt"))
        vn = sb("hg_vn", [P, 5, P], F32, hg)
        eq, ek = sb("hg_eq", [P, 2, SEQ], F32, hg), sb("hg_ek", [P, 2, SEQ], F32, hg)
        ql, kl = sb("hg_ql", [P, 2, SEQ], F32, hg), sb("hg_kl", [P, 2, SEQ], F32, hg)
        em, km, pm = (sb("hg_" + n, [P, META], F32, hg) for n in ("em", "km", "pm"))
        resets = sb("hg_resets", [P, LEVELS, SEQ], BF16, hg)
        odd = sb("hg_odd", [P, SEQ], BF16, hg)
        masks = sb("hg_masks", [P, LEVELS, P], I32, hg)
        carrier = sb("hg_carrier", [P, LEVELS], F32, hg)
        amat = sb("hg_amat", [P, SEQ], F32, hg)
        kn = sb("hg_kn", [P, 4, P], F32, hg)
        st = sb("hg_state", [P, 4, P], F32, hg)
        ot = val[:, 0, 0:SEQ]
        hg.close()
        fox = ExitStack()
        sel = sb("sel", [96, 8, P], BF16, fox)
        selp = sb("selp", [96, 2, P], BF16, fox)
        causal, identb = sb("causal", [P, P], BF16, fox), sb("identb", [P, P], BF16, fox)
        vnat = sb("vnat", [P, 5, 4 * P], F32, fox)
        qs, ks = sb("qs", [P, L], F32, fox), sb("ks", [P, L], F32, fox)
        vs = sb("vs", [P, 5, P], F32, fox)
        probs = sb("probs", [P, 2, L], F32, fox)
        pT = sb("pT", [P, 2, 5, P], F32, fox)
        fmax, fneg, fsum, finv = (sb(n, [P, 2], F32, fox) for n in ("fmax", "fneg", "fsum", "finv"))
        onat = proj[:, 8:8 + XT, 0:4 * P]
        fox.close()
        mix.close()

        ffn = ExitStack()
        gs = sb("gs", [P, L], F32, ffn)
        gh, gl_ = sb("gh", [P, FT, SEQ], F32R, ffn), sb("gl", [P, FT, SEQ], F32R, ffn)
        ffn.close()

        y = sb("y", [P, KT, L])
        ret = ExitStack()
        cos, sin = sb("cos", [P, L], F32, ret), sb("sin", [P, L], F32, ret)
        decx, decm = sb("decx", [P, HEADS, SEQ], F32, ret), sb("decm", [META, HEADS, L], F32, ret)
        mean_g = sb("mean_g", [P, P], F32, ret)
        kq = sb("kq", [P, 4, L], F32, ret)
        kr, qr = sb("kr", [P, 2, L], F32, ret), sb("qr", [P, 2, L], F32, ret)
        r1, r2 = sb("r1", [P, L], F32, ret), sb("r2", [P, L], F32, ret)
        vraw, zs = ea, r1
        zsg = ea
        rvn = sb("rvn", [P, 5, 4 * P], F32, ret)
        vmean = sb("vmean", [P, 5], F32, ret)
        vneg = sb("vneg", [P, 5], F32, ret)
        sd = sb("sd", [P, 5, L], F32, ret)
        o = sb("o", [P, 4, L], F32, ret)
        rh, rl = sb("rh", [P, 4, L], F32R, ret), sb("rl", [P, 4, L], F32R, ret)
        keep = ExitStack()
        ret.close()
        sb("keep_tables", [P, 2 * L + HEADS * SEQ + HEADS * L + P], F32, keep)
        ch, cl = sb("ch", [P, KT, L], F32R, keep), sb("cl", [P, KT, L], F32R, keep)
        eh = sb("eh", [P, L], F32, keep)
        cu = sb("cu", [P, L + 2], F32, keep)
        c0, c1, c2, cb_, cs = (sb("cv_" + n, [P, L], F32, keep) for n in ("c0", "c1", "c2", "b", "s"))
        ya, g1, g2 = (sb(n, [P, 2, L], F32, keep) for n in ("ya", "g1", "g2"))
        m1, m2 = sb("m1", [P, L], F32, keep), sb("m2", [P, L], F32, keep)
        keep.close()

        ps = ctx.enter_context(nc.psum_tensor("ps", [P, 8, 512], F32))

        raw_full = [sem(f"raw_full{i}") for i in range(4)]
        hi_ready, lo_ready = sem("hi_ready"), sem("lo_ready")
        panel_done = sem("panel_done")
        half_done = sem("half_done")
        acc_free = [sem(f"acc_free{i}") for i in range(2)]
        h_loaded = [sem(f"h_loaded{i}") for i in range(4)]
        small_loaded, tables_loaded = sem("small_loaded"), sem("tables_loaded")
        consts_set, masks_loaded, fox_loaded = sem("consts_set"), sem("masks_loaded"), sem("fox_loaded")
        sq_ready, sq_free = sem("sq_ready"), sem("sq_free")
        ssum_ready = sem("ssum_ready")
        meansq_ready = sem("meansq_ready")
        root_ready = sem("root_ready")
        val_ready, valhi_ready, vallo_ready = sem("val_ready"), sem("valhi_ready"), sem("vallo_ready")
        h_tile = sem("h_tile")
        sig_ready = sem("sig_ready")
        wff_hi, wff_lo, ff_psum, ff_abs, ff_ln, cum_ready = (sem(n) for n in (
            "wff_hi", "wff_lo", "ff_psum", "ff_abs", "ff_ln", "cum_ready"))
        fv_psum, fv_ready, fox_in, scores_ready, negmax_ready, probs_ready = (sem(n) for n in (
            "fv_psum", "fv_ready", "fox_in", "scores_ready", "negmax_ready", "probs_ready"))
        probsT_psum, probsT_ready, heads_psum, heads_ready, headsT_psum = (sem(n) for n in (
            "probsT_psum", "probsT_ready", "heads_psum", "heads_ready", "headsT_psum"))
        hg_sig, hg_f, hg_g, hg_vt, hg_vpsum, hg_vn, hg_exp_in, hg_exp_out = (sem("hg_" + n) for n in (
            "sig", "f_ready", "g_ready", "vt_ready", "v_psum", "v_nat", "exp_in", "exp_out"))
        hg_q, hg_s, hg_pred, hg_min, hg_mout, hg_km, hg_kpsum, hg_kn, hg_upsum, hg_state = (
            sem("hg_" + n) for n in ("q_ready", "s_psum", "a_ready", "meta_in", "meta_out",
                                     "meta_k", "k_psum", "k_nat", "u_psum", "state_ready"))
        hg_o, hg_sq, hg_ss, hg_root, hg_inv = (sem("hg_" + n) for n in (
            "o_psum", "squares", "meansq_psum", "root_ready", "iter_free"))
        hg_kl = sem("hg_k_ready")
        lb_exp, lb_in = sem("lb_exp"), sem("lb_in")
        rope_ready, vt_psum, vn_ready, v_centred, s_psum, sd_ready, o_psum = (sem(n) for n in (
            "rope_ready", "vt_psum", "vn_ready", "v_centred", "s_psum", "sd_ready", "o_psum"))
        om_ready, o_psum_m, gate_used = sem("om_ready"), sem("o_psum_meta"), sem("gate_used")
        y_ready, out_stored = sem("y_ready"), sem("out_stored")

        block = ctx.enter_context(nc.Block())

        def full(t):
            return t.rearrange("p (a b) -> p a b", a=2)

        def seq(t):
            return t[:, META:L].rearrange("p (a b) -> p a b", a=2)

        def acc(slot, n=L):
            return ps[:, 2 * slot:2 * slot + 2, 0:n // 2]

        def col(c, width=1):
            return vec[:, bass.ds(c, width)]

        def tile(t, i):
            return t[:, bass.ds(i, 1), :].rearrange("p a b -> p (a b)")

        def scores(b):
            return ps[:, 2 * b:2 * b + 2, :].rearrange("p a b -> p (a b)")[:, 240:240 + L]

        def bias(quad, s):
            return col(4 * quad + (s + V_BIAS - 4 * Q_B2))

        @block.sync
        def _(sp):
            sp.dma_start(h[:, :, 0:META], io["meta"]).then_inc(h_loaded[0], 16)
            for k in range(4):
                sp.dma_start(h[:, 2 * k:2 * k + 2, META:L], io["x"][:, 2 * k:2 * k + 2, :]).then_inc(h_loaded[k], 16)
            for s in range(4):
                sp.dma_start(raw[:, s, :], io["weights"][s]).then_inc(raw_full[s], 16)
            with sp.Fori(1, QUADS) as q:
                for s in range(4):
                    sp.wait_ge(lo_ready, 4 * q + (s - 3))
                    sp.dma_start(raw[:, s, :], io["weights"][4 * q + s]).then_inc(raw_full[s], 16)
            for s in range(2):
                sp.wait_ge(lo_ready, 4 * QUADS - 3 + s)
                sp.dma_start(raw[:, s, :], io["weights"][4 * QUADS + s]).then_inc(raw_full[s], 16)
            for k in range(KT):
                sp.wait_ge(h_tile, 2 * KT + k + 1)
                sp.dma_start(io["out"][:, k, :], h[:, k, META:L]).then_inc(out_stored, 16)
            sp.wait_ge(out_stored, 16 * KT)

        @block.gpsimd
        def _(pool):
            pool.dma_start(vec[:], io["vec"]).then_inc(small_loaded, 16)
            pool.dma_start(ident[:], io["ident"]).then_inc(small_loaded, 16)
            pool.dma_start(wff_raw, io["wff"]).then_inc(small_loaded, 16)
            pool.dma_start(fbias[:], io["fbias"]).then_inc(small_loaded, 16)
            pool.dma_start(meta2[:], io["meta2"]).then_inc(small_loaded, 16)
            pool.dma_start(masks[:], io["masks"]).then_inc(masks_loaded, 16)
            pool.memset(ones[:], 1.0)
            pool.memset(mean_d[:], 1.0 / D)
            pool.memset(mean_h[:], 1.0 / P)
            pool.memset(cone, 1.0)
            pool.memset(cparts[:], 0.0)
            pool.memset(resets[:], 1.0)
            pool.memset(odd[:], 0.0)
            pool.drain()
            for l in range(1, LEVELS + 1):
                pool.memset(resets[:, l - 1, :].rearrange("p (n b) -> p n b", b=2 ** l)[:, :, 0:1], 0.0)
            pool.memset(odd.rearrange("p (n b) -> p n b", b=2)[:, :, 1:2], 1.0)
            pool.drain().then_inc(consts_set, 1)

            def split_low(q, s):
                pool.wait_ge(hi_ready, 4 * q + (s + 1))
                nc.gpsimd.tensor_tensor(wl[:, s % 2, :], raw[:, s, :], wh[:, s % 2, :].bitcast(F32),
                                        ALU.subtract).then_inc(lo_ready, 1)

            with pool.Fori(0, 3) as q:
                for s in range(4):
                    split_low(q, s)
            for s in range(2):
                split_low(3, s)
            with pool.Fori(0, HEADS) as hd:
                for s in range(4):
                    for l in (2 * s, 2 * s + 1):
                        pool.wait_ge(hg_exp_out, (LEVELS + 1) * hd + (l + 1))
                        if l >= 2:
                            pool.wait_ge(hg_s, LEVELS * hd + (l - 1))
                        nc.gpsimd.tensor_tensor(kl[:, l % 2, :], sgq[:, META:L], ek[:, l % 2, :],
                                                ALU.mult).then_inc(hg_kl, 1)
                    split_low(hd + 3 + (s + 2) // 4, (s + 2) % 4)
            pool.wait_ge(hg_inv, HEADS + 1)
            pool.dma_start(val[0:96].rearrange("p a b -> p (a b)")[:, 0:8 * P], io["sel"]).then_inc(fox_loaded, 16)
            pool.dma_start(sq[:, 0, 0:P], io["causal"]).then_inc(fox_loaded, 16)
            for s in (2, 3):
                split_low(7, s)
            with pool.Fori(8, Q_B2) as q:
                for s in range(4):
                    split_low(q, s)
            pool.wait_ge(ssum_ready, 2)
            for dst, name in ((cos, "cos"), (sin, "sin"), (decx, "decx"), (decm, "decm")):
                pool.dma_start(dst[:], io[name]).then_inc(tables_loaded, 16)
            pool.memset(mean_g[:], 1.0 / (4 * P)).then_inc(consts_set, 1)
            with pool.Fori(Q_B2, QUADS) as q:
                for s in range(4):
                    split_low(q, s)

        @block.scalar
        def _(act):
            def split_ahead(quad, s):
                s2 = (s + 2) % 4
                act.wait_ge(raw_full[s2], 16 * quad + 16 * (1 + (s + 2) // 4))
                act.wait_ge(panel_done, 4 * quad + (s + 1))
                nc.scalar.activation(wh[:, s2 % 2, :], raw[:, s2, :], ACT.Copy).then_inc(hi_ready, 1)

            def split_value(index, slot, dst, vindex=None, c0=0):
                act.wait_ge(val_ready, (index if vindex is None else vindex) + 1)
                nc.scalar.activation(dst, val[:, slot, c0:L], ACT.Copy).then_inc(valhi_ready, 1)

            def squares(first, tile0=None):
                for k in range(KT):
                    if tile0 is not None:
                        act.wait_ge(h_tile, tile0 + (k + 1))
                    elif k % 2 == 0:
                        act.wait_ge(h_loaded[k // 2], 32 if k == 0 else 16)
                    act.wait_ge(sq_free, first + (k + 1))
                    nc.scalar.activation(sq[:, k % 2, :], h[:, k, :], ACT.Square).then_inc(sq_ready, 1)

            eps, gn_eps = col(V_EPS), col(V_EPS + 1)

            def take_root(nth, eps, c0=0):
                act.wait_ge(meansq_ready, nth + 1)
                view = seq if c0 else full
                nc.scalar.activation(view(rstd[:]), acc(2, L - c0), ACT.Sqrt, bias=eps).then_inc(root_ready, 1)

            for s in range(2):
                act.wait_ge(raw_full[s], 16)
                nc.scalar.activation(wh[:, s, :], raw[:, s, :], ACT.Copy).then_inc(hi_ready, 1)
            act.wait_ge(small_loaded, 16 * 5)
            nc.scalar.activation(wffh[:], wff_raw, ACT.Copy).then_inc(wff_hi, 1)
            act.wait_ge(lb_in, 1)
            nc.scalar.activation(lbt[:, 1, :], lbt[:, 0, :], ACT.Exp).then_inc(lb_exp, 1)
            squares(0)
            take_root(0, eps)
            for k in range(KT):
                split_value(k, k % 2, uh[:, k, :])
            act.wait_ge(ff_psum, 1)
            nc.scalar.activation(full(cz), ps[0:8, 4:6, 0:L // 2], ACT.Identity, bias=fbias[:])
            act.drain()
            nc.scalar.activation(ct, cz, ACT.Abs)
            act.drain()
            nc.scalar.activation(ct, ct, ACT.Exp, scale=-1.0)
            act.drain()
            nc.scalar.activation(ct, ct, ACT.Ln, bias=1.0).then_inc(ff_ln, 1)

            def evacuate(s, dst):
                nc.scalar.activation(full(dst), acc(s % 2), ACT.Copy).then_inc(acc_free[s % 2], 1)

            with act.Fori(0, 3) as q:
                for s in range(4):
                    split_ahead(q, s)
                    evacuate(s, tile(proj, 4 * q + (12 + s)))
            with act.Fori(0, HEADS) as hd:
                act.wait_ge(hg_inv, hd + 1)
                nc.scalar.activation(gl[:], tile(proj, hd + 16), ACT.Sigmoid, scale=-1.0)
                nc.scalar.activation(sgq[:], tile(proj, hd + 12), ACT.Sigmoid).then_inc(hg_sig, 1)
                act.wait_ge(hg_f, hd + 1)
                nc.scalar.activation(gl[:], gl[:], ACT.Ln).then_inc(hg_g, 1)
                for s, first in enumerate((24, 0, 4, 8)):
                    for l in (2 * s, 2 * s + 1):
                        act.wait_ge(hg_exp_in, (LEVELS + 1) * hd + (l + 1))
                        nc.scalar.activation(eq[:, l % 2, :], eq[:, l % 2, :], ACT.Exp)
                        nc.scalar.activation(ek[:, l % 2, :], ek[:, l % 2, :], ACT.Exp).then_inc(hg_exp_out, 1)
                    split_ahead(hd + 3, s)
                    evacuate(s, tile(proj, hd + first))
                act.wait_ge(hg_kl, (LEVELS + 1) * hd + (LEVELS + 1))
                act.wait_ge(hg_min, hd + 1)
                nc.scalar.activation(em[:], em[:], ACT.Exp)
                nc.scalar.activation(sgq[:], tile(proj, hd + 24), ACT.Sigmoid).then_inc(hg_mout, 1)
                act.wait_ge(hg_o, hd + 1)
                nc.scalar.activation(sq[:, 0, 0:SEQ], ps[:, 6, :], ACT.Square).then_inc(hg_sq, 1)
                act.wait_ge(hg_ss, hd + 1)
                nc.scalar.activation(rstd[:, 0:SEQ], ps[:, 7, :], ACT.Sqrt, bias=eps).then_inc(hg_root, 1)
            act.wait_ge(val_ready, 8 + HEADS)
            for k in range(HEADS):
                nc.scalar.activation(uh[:, 4 + k, META:L], proj[:, 24 + k, META:L], ACT.Copy)                    .then_inc(valhi_ready, 1)

            with act.Fori(0, 4) as hp:
                for n in range(8):
                    b, i = n % 2, n % 4
                    nk = KEYS[i + 1][1]
                    act.wait_ge(negmax_ready, 8 * hp + (n + 1))
                    act.wait_ge(probsT_psum, 8 * hp + (n + 1))
                    act.wait_ge(heads_ready, 8 * hp + (n + 1))
                    nc.scalar.activation(probs[:, b, 0:nk], scores(b)[:, 0:nk], ACT.Exp,
                                         bias=fneg[:, b:b + 1], scale=0.125,
                                         accum_out=fsum[:, b:b + 1]).then_inc(probs_ready, 1)
            for k in range(4):
                split_value(12 + k, k % 2, uh[:, k, META:L], c0=META)

            with act.Fori(Q_OUT, Q_FF) as q:
                for s in range(4):
                    split_ahead(q, s)
            take_root(1, eps, META)
            for k in range(KT):
                split_value(16 + k, k % 2, uh[:, k, META:L], c0=META)
            with act.Fori(0, 11) as r:
                for s in range(4):
                    split_ahead(r + Q_FF, s)
                    if s % 2 == 0:
                        nc.scalar.activation(seq(ea[:, s // 2, :]), acc(0, SEQ), ACT.Sigmoid).then_inc(sig_ready, 1)
                    else:
                        j = s // 2
                        split_value(2 * r + (24 + j), j, tile(gh, 2 * r + j), c0=META)
            with act.Fori(Q_DOWN, Q_B2) as q:
                for s in range(4):
                    split_ahead(q, s)
            take_root(2, eps, META)

            with act.Fori(0, 2) as lay:
                quad0 = lay * Q_LAYER + Q_B2
                v0, i0 = 32 * lay + 46, 40 * lay + 46
                squares(8 * lay + 8, 8 * lay)
                take_root(6 * lay + 3, eps)
                for k in range(KT):
                    split_value(i0 + k, k % 2, uh[:, k, :], v0 + k)
                with act.Fori(0, HEADS) as hd:
                    quad = 4 * hd + quad0
                    it = 4 * lay + hd
                    for s in range(4):
                        split_ahead(quad, s)
                        nc.scalar.activation(full(kq[:, s, :]), acc(s % 2), ACT.Identity,
                                             bias=bias(quad, s)).then_inc(acc_free[s % 2], 1)
                    for s in range(4):
                        split_ahead(quad + 1, s)
                        if s >= 2:
                            act.wait_ge(vt_psum, 4 * it + (s - 1))
                        nc.scalar.activation(full(vraw[:, s % 2, :]), acc(s % 2), ACT.Identity,
                                             bias=bias(quad + 1, s)).then_inc(acc_free[s % 2], 1)
                    for s in range(2):
                        split_ahead(quad + 2, s)
                        nc.scalar.activation(full(ea[:, s, :]), acc(s), ACT.Sigmoid,
                                             bias=bias(quad + 2, s)).then_inc(sig_ready, 1)
                    take_root(6 * lay + hd + 4, gn_eps)
                    split_ahead(quad + 2, 2)
                    act.wait_ge(gate_used, 2 * it + 1)
                    nc.scalar.activation(full(ea[:, 0, :]), acc(0), ACT.Sigmoid,
                                         bias=bias(quad + 2, 2)).then_inc(sig_ready, 1)
                    for s in range(3):
                        split_value(i0 + 4 * hd + (8 + s), s % 2, rh[:, s, :], v0 + 4 * hd + (8 + s))
                    act.wait_ge(gate_used, 2 * it + 2)
                    act.wait_ge(panel_done, 4 * quad + 12)
                    nc.scalar.activation(full(ea[:, 1, :]), acc(1), ACT.Sigmoid,
                                         bias=bias(quad + 2, 3)).then_inc(sig_ready, 1)
                    split_ahead(quad + 2, 3)
                    split_value(i0 + 4 * hd + 11, 1, rh[:, 3, :], v0 + 4 * hd + 11)
                    for s in range(4):
                        split_ahead(quad + 3, s)
                with act.Fori(0, KT) as j:
                    quad = quad0 + Q_CONV + j
                    for s in range(4):
                        split_ahead(quad, s)
                        if s == 0:
                            nc.scalar.activation(full(eh[:]), acc(0), ACT.Identity,
                                                 bias=bias(quad, 0)).then_inc(acc_free[0], 1)
                        if s == 3:
                            nc.scalar.activation(full(ea[:, 1, :]), acc(1), ACT.Sigmoid,
                                                 bias=bias(quad, 3)).then_inc(sig_ready, 1)
                            split_value(i0 + 24 + j, 0, tile(ch, j), v0 + 24 + j)
                with act.Fori(0, 2) as r:
                    quad = quad0 + Q_MERGE + 3 * r
                    for n in range(12):
                        t, m = n // 3, n % 3
                        split_ahead(quad + n // 4, n % 4)
                        if m == 0:
                            act.wait_ge(y_ready, 8 * lay + 4 * r + (t + 1))
                        dst = (ya, g1, g2)[m][:, t % 2, :]
                        if m == 0:
                            nc.scalar.activation(full(dst), acc(n % 2), ACT.Copy).then_inc(acc_free[n % 2], 1)
                        else:
                            nc.scalar.activation(full(dst), acc(n % 2), ACT.Sigmoid,
                                                 bias=bias(quad + n // 4, n % 4)).then_inc(acc_free[n % 2], 1)
                for k in range(KT):
                    act.wait_ge(y_ready, 8 * lay + (k + 3))
                    nc.scalar.activation(uh[:, k, :], y[:, k, :], ACT.Copy).then_inc(valhi_ready, 1)
                with act.Fori(0, 2) as r:
                    for s in range(4):
                        split_ahead(quad0 + Q_WO + r, s)
                        if s == 0:
                            act.wait_ge(vallo_ready, i0 + 40)
                        nc.scalar.activation(full(tile(y, 4 * r + s)), acc(s % 2), ACT.Copy)\
                            .then_inc(acc_free[s % 2], 1)
                take_root(6 * lay + 8, eps)

        @block.vector
        def _(dve):
            v = nc.vector

            def low_part(index, slot, dst, hi, c0=0):
                dve.wait_ge(valhi_ready, index + 1)
                v.tensor_tensor(dst, val[:, slot, c0:L], hi.bitcast(F32), ALU.subtract).then_inc(vallo_ready, 1)
                dve.drain()

            def inv_rms(nth, c0=0):
                dve.wait_ge(root_ready, nth + 2)
                v.reciprocal(rstd[:, c0:L], rstd[:, c0:L])
                dve.drain()

            def add_square(t, first=False, c0=0):
                t = t[:, c0:L]
                if first:
                    v.tensor_tensor(ssum[:, c0:L], t, t, ALU.mult)
                else:
                    v.tensor_tensor(sq[:, 0, c0:L], t, t, ALU.mult)
                    dve.drain()
                    v.tensor_tensor(ssum[:, c0:L], ssum[:, c0:L], sq[:, 0, c0:L], ALU.add)

            def apply_norm(index, nth, src, wcol, c0):
                inv_rms(nth, c0)
                for k in range(KT + 1):
                    if k < KT:
                        v.scalar_tensor_tensor(val[:, k % 2, c0:L], src[:, k, c0:L], wcol(k), rstd[:, c0:L],
                                               ALU.mult, ALU.mult).then_inc(val_ready, 1)
                    if k >= 1:
                        low_part(index + (k - 1), (k - 1) % 2, ul[:, k - 1, c0:L], uh[:, k - 1, c0:L], c0)

            dve.wait_ge(small_loaded, 16 * 5)
            v.tensor_tensor(lbt[:, 0, :], vec[:, V_LB:V_LB + 4], vec[:, V_LB:V_LB + 4], ALU.subtract).then_inc(lb_in, 1)
            dve.wait_ge(lb_exp, 1)
            v.reciprocal(lbt[:, 2, :], lbt[:, 1, :])
            dve.drain()
            v.tensor_tensor(lbt[:, 3, :], lbt[:, 1, :], lbt[:, 2, :], ALU.mult)
            dve.drain()
            v.tensor_tensor(lbt[:, 4, :], lbt[:, 3, :], lbt[:, 3, :], ALU.subtract)
            dve.drain()
            v.tensor_scalar(lbt[:, 5, :], lbt[:, 4, :], -1.0, 1.0, ALU.mult, ALU.add)
            dve.wait_ge(wff_hi, 1)
            v.tensor_tensor(wffl[:], wff_raw, wffh[:].bitcast(F32), ALU.subtract).then_inc(wff_lo, 1)
            apply_norm(0, 0, h, lambda k: col(V_MIX + k), 0)
            dve.wait_ge(ff_ln, 1)
            v.scalar_tensor_tensor(cz, cz, 0.0, ct, ALU.min, ALU.subtract)
            dve.wait_ge(consts_set, 1)
            dve.drain()
            v.tensor_tensor_scan(ccum, cone, cz, 0.0, ALU.mult, ALU.add)
            dve.drain()
            for n, (left, rest) in enumerate(((ccum, cres), (cres, cz), (cz, None))):
                v.tensor_copy(cparts[32 * n:32 * n + 8, :], left)
                v.tensor_copy(cparts0[n][:], left)
                dve.drain()
                if rest is not None:
                    v.tensor_tensor(rest, left, cparts0[n][:], ALU.subtract)
                    dve.drain()
            dve.drain().then_inc(cum_ready, 1)
            dve.wait_ge(masks_loaded, 16)
            with dve.Fori(0, HEADS) as hd:
                lev = (LEVELS + 1) * hd
                qh, kin = tile(proj, hd + 12), tile(proj, hd + 16)
                dve.wait_ge(hg_sig, hd + 1)
                v.tensor_scalar(kin, gl[:], lbt[:, 5, bass.ds(hd, 1)], None, ALU.mult)
                dve.drain()
                v.tensor_scalar(gl[:], kin, -1.0, 1.0, ALU.mult, ALU.add)
                dve.drain()
                v.tensor_scalar(gl[:], gl[:], F_MIN, None, ALU.max).then_inc(hg_f, 1)
                v.tensor_copy(vt[:], tile(proj, hd + 20)).then_inc(hg_vt, 1)
                v.scalar_tensor_tensor(qh, qh, float(P) ** -0.5, sgq[:], ALU.mult, ALU.mult)
                v.memset(amat[:], 0.0)
                dve.drain()
                v.tensor_copy(sgq[:], kin)
                dve.wait_ge(hg_vpsum, hd + 1)
                v.tensor_copy(vn[:, 1:5, :], ps[:, 4, :].rearrange("p (a b) -> p a b", a=4))
                v.tensor_copy(vn[0:META, 0, :], ps[0:META, 5, 0:P]).then_inc(hg_vn, 1)
                dve.wait_ge(hg_g, hd + 1)

                def exponents(l):
                    b = l % 2
                    if l == 0:
                        v.tensor_tensor(eq[:, b, :], gl[:, META:L], odd[:], ALU.mult)
                        dve.drain()
                        v.tensor_scalar(ek[:, b, :], eq[:, b, :], -1.0, None, ALU.mult).then_inc(hg_exp_in, 1)
                        return
                    v.tensor_tensor_scan(eq[:, b, :], resets[:, l - 1, :], gl[:, META:L], 0.0, ALU.mult, ALU.add)
                    dve.drain()
                    w = 2 ** l
                    e3 = eq[:, b, :].rearrange("p (n b) -> p n b", b=w)
                    v.tensor_tensor(ek[:, b, :].rearrange("p (n b) -> p n b", b=w),
                                    e3[:, :, w - 1:w].broadcast_to([P, SEQ // w, w]), e3,
                                    ALU.subtract).then_inc(hg_exp_in, 1)

                exponents(0)
                for l in range(LEVELS + 2):
                    b = l % 2
                    if l <= LEVELS:
                        if l < LEVELS:
                            if l >= 1:
                                dve.drain()
                                dve.wait_ge(hg_kl, lev + l)
                            exponents(l + 1)
                        dve.wait_ge(hg_exp_out, lev + (l + 1))
                        if l >= 2:
                            dve.wait_ge(hg_s, LEVELS * hd + (l - 1))
                        v.tensor_tensor(ql[:, b, :], qh[:, META:L], eq[:, b, :], ALU.mult).then_inc(hg_q, 1)
                    if 1 <= l <= LEVELS:
                        m = l - 1
                        dve.drain()
                        dve.wait_ge(hg_s, LEVELS * hd + l)
                        v.memset(carrier[:, m:m + 1], 0.0)
                        v.copy_predicated(amat.rearrange("p (a b) -> p a b", a=XT),
                                          masks[:, m:m + 1, :].broadcast_to([P, XT, P]),
                                          ps[:, 6 + m % 2, :].rearrange("p (a b) -> p a b", a=XT)).then_inc(hg_pred, 1)
                v.tensor_tensor_scan(pm[:], ones[:, 0:META], gl[:, 0:META], 0.0, ALU.mult, ALU.add)
                dve.drain()
                v.tensor_tensor(em[:], pm[:, META - 1:META].broadcast_to([P, META]), pm[:],
                                ALU.subtract).then_inc(hg_min, 1)
                dve.wait_ge(hg_mout, hd + 1)
                v.tensor_tensor(km[:], kin[:, 0:META], em[:], ALU.mult).then_inc(hg_km, 1)
                dve.wait_ge(hg_kpsum, hd + 1)
                v.tensor_copy(kn[:, 1:4, :], ps[:, 4, 0:3 * P].rearrange("p (a b) -> p a b", a=3))
                v.tensor_copy(kn[0:META, 0, :], ps[0:META, 5, 0:P]).then_inc(hg_kn, 1)
                dve.wait_ge(hg_upsum, hd + 1)
                v.tensor_copy(st[:, 0, :], ps[:, 4, 0:P])
                for i in range(1, XT):
                    dve.drain()
                    step = v.scalar_tensor_tensor(st[:, i, :], st[:, i - 1, :],
                                                  eq[:, LEVELS % 2, P * i - 1:P * i],
                                                  ps[:, 4, P * i:P * i + P], ALU.mult, ALU.add)
                step.then_inc(hg_state, 1)
                v.tensor_tensor(sgq[:], tile(proj, hd + 24), sgq[:], ALU.mult)
                dve.wait_ge(hg_root, hd + 1)
                v.reciprocal(rstd[:, 0:SEQ], rstd[:, 0:SEQ])
                dve.drain()
                v.scalar_tensor_tensor(ot, ps[:, 6, :], col(V_HNORM), rstd[:, 0:SEQ], ALU.mult, ALU.mult)
                dve.drain()
                v.tensor_tensor(tile(proj, hd + 24)[:, META:L], ot, sgq[:, META:L], ALU.mult).then_inc(val_ready, 1)
                dve.drain().then_inc(hg_inv, 1)
            for k in range(HEADS):
                dve.wait_ge(valhi_ready, 9 + k)
                v.tensor_tensor(ul[:, 4 + k, META:L], proj[:, 24 + k, META:L],
                                uh[:, 4 + k, META:L].bitcast(F32), ALU.subtract).then_inc(vallo_ready, 1)
            dve.wait_ge(fox_loaded, 32)
            v.tensor_copy(sel[:], val[0:96].rearrange("p a b -> p (a b)")[:, 0:8 * P].rearrange("p (a b) -> p a b", b=P))
            v.tensor_copy(causal[:], sq[:, 0, 0:P])
            v.tensor_copy(identb[:], ident[:])
            dve.drain()

            for j in range(4):
                dve.wait_ge(fv_psum, j + 1)
                v.tensor_copy(vnat[:, 1:5, P * j:P * j + P], ps[:, 4, :].rearrange("p (a b) -> p a b", a=4))
                v.tensor_copy(vnat[0:META, 0, P * j:P * j + P], ps[0:META, 5, 0:P]).then_inc(fv_ready, 1)
            dve.drain()

            with dve.Fori(0, 4) as hp:
                dve.wait_ge(heads_psum, 8 * hp + 1)
                v.tensor_copy(qs[:], tile(proj, hp))
                v.tensor_copy(ks[:], tile(proj, hp + 4))
                v.tensor_copy(selp[:], sel[:, bass.ds(2 * hp, 2), :])
                v.tensor_copy(vs[0:META, 0, :], vnat[0:META, 0, bass.ds(P * hp, P)])
                v.tensor_copy(vs[:, 1:5, :], vnat[:, 1:5, bass.ds(P * hp, P)]).then_inc(fox_in, 1)
                for n in range(10):
                    if n < 8:
                        b, i = n % 2, n % 4
                        nk = KEYS[i + 1][1]
                        dve.wait_ge(scores_ready, 8 * hp + (n + 1))
                        v.tensor_reduce(fmax[:, b:b + 1], scores(b)[:, 0:nk], AX.X, ALU.max)
                        dve.drain()
                        dve.wait_ge(probs_ready, 8 * hp + (n + 1))
                        v.tensor_scalar(fneg[:, b:b + 1], fmax[:, b:b + 1], -0.125, None, ALU.mult)\
                            .then_inc(negmax_ready, 1)
                    if 1 <= n < 9:
                        m = n - 1
                        b, i, e = m % 2, m % 4, m // 4
                        dve.wait_ge(probsT_psum, 8 * hp + (m + 3))
                        v.tensor_copy(pT[0:META, b, 0, :], ps[0:META, 5, 0:P])
                        v.tensor_copy(pT[:, b, 1:i + 2, :], ps[:, 4, 0:P * (i + 1)].rearrange(
                            "p (a b) -> p a b", b=P)).then_inc(probsT_ready, 1)
                    if n >= 2:
                        m = n - 2
                        b, i, e = m % 2, m % 4, m // 4
                        dve.wait_ge(probs_ready, 8 * hp + (m + 3))
                        v.reciprocal(finv[:, b:b + 1], fsum[:, b:b + 1])
                        dve.drain()
                        dve.wait_ge(heads_psum, 8 * hp + (m + 2))
                        v.tensor_scalar(onat[:, i, bass.ds(P * hp + 64 * e, 64)], ps[:, 6 + b, 0:64],
                                        finv[:, b:b + 1], None, ALU.mult).then_inc(heads_ready, 1)
            for k in range(4):
                dve.wait_ge(headsT_psum, k + 1)
                v.tensor_copy(val[:, k % 2, META:L], ps[:, k, :]).then_inc(val_ready, 1)
                low_part(12 + k, k % 2, ul[:, k, META:L], uh[:, k, META:L], META)

            v.memset(ssum[:], 0.0)
            with dve.Fori(0, 2) as r:
                for s in range(4):
                    dve.wait_ge(panel_done, 4 * r + (4 * Q_OUT + s + 1))
                    t = seq(tile(h, 4 * r + s))
                    v.tensor_tensor(t, acc(s % 2, SEQ), t, ALU.add).then_inc(acc_free[s % 2], 1)
                    dve.drain()
                    add_square(tile(h, 4 * r + s), c0=META)
            dve.drain().then_inc(ssum_ready, 1)
            apply_norm(16, 1, h, lambda k: col(V_FFN + k), META)
            with dve.Fori(0, 11) as r:
                for s in range(4):
                    j = s // 2
                    if s % 2 == 0:
                        dve.wait_ge(sig_ready, 2 * r + (j + 1))
                        v.tensor_tensor(seq(gs[:]), acc(0, SEQ), seq(ea[:, j, :]), ALU.mult).then_inc(acc_free[0], 1)
                        dve.drain()
                    else:
                        dve.wait_ge(panel_done, 4 * r + (4 * Q_FF + s + 1))
                        v.tensor_tensor(seq(val[:, j, :]), acc(1, SEQ), seq(gs[:]), ALU.mult).then_inc(acc_free[1], 1)
                        dve.drain().then_inc(val_ready, 1)
                        low_part(2 * r + (24 + j), j, tile(gl_, 2 * r + j), tile(gh, 2 * r + j), META)
            v.memset(ssum[:], 0.0)
            with dve.Fori(0, 2) as r:
                for t in range(4):
                    dve.wait_ge(panel_done, 12 * r + (4 * Q_DOWN + 3 * t + 3))
                    x = seq(tile(h, 4 * r + t))
                    v.tensor_tensor(x, acc(t % 2, SEQ), x, ALU.add).then_inc(acc_free[t % 2], 1)
                    dve.drain()
                    add_square(tile(h, 4 * r + t), c0=META)
            v.tensor_copy(h[:, :, 0:META], meta2[:])
            dve.drain().then_inc(ssum_ready, 1)
            inv_rms(2, META)
            for k in range(KT):
                v.scalar_tensor_tensor(h[:, k, META:L], h[:, k, META:L], col(V_FINAL + k), rstd[:, META:L],
                                       ALU.mult, ALU.mult).then_inc(h_tile, 1)

            with dve.Fori(0, 2) as lay:
                quad0 = lay * Q_LAYER + Q_B2
                i0 = 40 * lay + 46
                apply_norm(i0, 6 * lay + 3, h, lambda k: col(8 * lay + (V_PRE + k)), 0)
                v.memset(y[:], 0.0)
                dve.wait_ge(tables_loaded, 64)
                with dve.Fori(0, HEADS) as hd:
                    quad = 4 * hd + quad0
                    it = 4 * lay + hd
                    a0 = A_LAYER * lay + A_HEAD * hd + A_B2
                    for n, dst in enumerate((kr, qr)):
                        dve.wait_ge(acc_free[0], a0 + (n + 2))
                        dve.wait_ge(acc_free[1], a0 + (n + 2))
                        x1, x2 = kq[:, 2 * n, :], kq[:, 2 * n + 1, :]
                        v.tensor_tensor(r1[:], x1, cos[:], ALU.mult)
                        v.tensor_tensor(r2[:], x2, sin[:], ALU.mult)
                        dve.drain()
                        v.tensor_tensor(dst[:, 0, :], r1[:], r2[:], ALU.subtract)
                        dve.drain()
                        v.tensor_tensor(r1[:], x1, sin[:], ALU.mult)
                        v.tensor_tensor(r2[:], x2, cos[:], ALU.mult)
                        dve.drain()
                        v.tensor_tensor(dst[:, 1, :], r1[:], r2[:], ALU.add).then_inc(rope_ready, 1)
                        dve.drain()
                    def silu(s, dst):
                        dve.wait_ge(sig_ready, 24 * lay + 4 * hd + (22 + s + 1))
                        v.scalar_tensor_tensor(full(dst), acc(s % 2), bias(quad + 2, s), full(ea[:, s % 2, :]),
                                               ALU.add, ALU.mult).then_inc(acc_free[s % 2], 1)

                    for j in range(4):
                        if j == 3:
                            silu(0, zsg[:, 0, :])
                        dve.wait_ge(vt_psum, 4 * it + (j + 1))
                        v.tensor_copy(rvn[:, 1:5, P * j:P * j + P], ps[:, 4, :].rearrange("p (a b) -> p a b", a=4))
                        v.tensor_copy(rvn[0:META, 0, P * j:P * j + P], ps[0:META, 5, 0:P]).then_inc(vn_ready, 1)
                    dve.drain()
                    v.tensor_reduce(vmean[:, 1:5], rvn[:, 1:5, :], AX.X, ALU.add)
                    v.tensor_reduce(vmean[0:META, 0:1], rvn[0:META, 0, :], AX.X, ALU.add)
                    dve.drain()
                    v.tensor_scalar(vneg[:, 1:5], vmean[:, 1:5], -1.0 / (4 * P), None, ALU.mult)
                    v.tensor_scalar(vneg[0:META, 0:1], vmean[0:META, 0:1], -1.0 / (4 * P), None, ALU.mult)
                    dve.drain()
                    v.tensor_scalar(rvn[0:META, 0, :], rvn[0:META, 0, :], vneg[0:META, 0:1], None, ALU.add)
                    for i in range(1, 5):
                        last = v.tensor_scalar(rvn[:, i, :], rvn[:, i, :], vneg[:, i:i + 1], None, ALU.add)
                    last.then_inc(v_centred, 1)
                    dve.wait_ge(s_psum, 5 * it + 1)
                    dm = decm[:, bass.ds(hd, 1), :].rearrange("p a b -> p (a b)")
                    v.tensor_tensor(sd[0:META, 0, META:L], ps[0:META, 6, :], dm[:, META:L], ALU.mult)
                    v.tensor_tensor(sd[0:META, 0, 0:META], ps[0:META, 7, 0:META], dm[:, 0:META],
                                    ALU.mult).then_inc(sd_ready, 1)
                    for i in range(XT):
                        w = SEQ - P * i
                        dx = decx[:, bass.ds(hd, 1), :].rearrange("p a b -> p (a b)")
                        dve.wait_ge(s_psum, 5 * it + (i + 2))
                        v.tensor_tensor(sd[:, i + 1, META + P * i:L], ps[:, 4 + i % 2, 0:w], dx[:, 0:w],
                                        ALU.mult).then_inc(sd_ready, 1)
                    silu(1, zsg[:, 1, :])
                    dve.wait_ge(o_psum_m, it + 1)
                    v.tensor_copy(o[:, :, 0:META], ps[:, 7, 0:4 * META].rearrange("p (a b) -> p a b", a=4))\
                        .then_inc(om_ready, 1)
                    for j in range(4):
                        dve.wait_ge(o_psum, 4 * it + (j + 1))
                        v.tensor_copy(o[:, j, META:L], ps[:, 4 + j, :])
                        dve.drain()
                        add_square(o[:, j, :], j == 0)
                        if j < 2:
                            dve.drain()
                            v.scalar_tensor_tensor(o[:, j, :], o[:, j, :], col(16 * lay + 4 * hd + (V_GN + j)),
                                                   zsg[:, j, :], ALU.mult, ALU.mult).then_inc(gate_used, 1)
                    dve.drain().then_inc(ssum_ready, 1)
                    inv_rms(6 * lay + hd + 4)
                    v0 = i0 + 4 * hd + 8
                    for s in range(2):
                        v.tensor_tensor(val[:, s, :], o[:, s, :], rstd[:], ALU.mult).then_inc(val_ready, 1)
                    for s in range(2):
                        v.scalar_tensor_tensor(o[:, 2 + s, :], o[:, 2 + s, :], col(16 * lay + 4 * hd + (V_GN + 2 + s)),
                                               rstd[:], ALU.mult, ALU.mult)
                        low_part(v0 + s, s, rl[:, s, :], rh[:, s, :])
                    for s in (2, 3):
                        silu(s, zs[:])
                        dve.drain()
                        v.tensor_tensor(val[:, s % 2, :], zs[:], o[:, s, :], ALU.mult).then_inc(val_ready, 1)
                        low_part(v0 + s, s % 2, rl[:, s, :], rh[:, s, :])
                    for s in range(4):
                        dve.wait_ge(half_done, 4 * it + (s + 1))
                        v.tensor_tensor(full(y[:, 2 * s, :]), acc(0), full(y[:, 2 * s, :]), ALU.add)\
                            .then_inc(acc_free[0], 1)
                        dve.wait_ge(panel_done, 4 * quad + (12 + s + 1))
                        v.tensor_tensor(full(y[:, 2 * s + 1, :]), acc(1), full(y[:, 2 * s + 1, :]), ALU.add)\
                            .then_inc(acc_free[1], 1)
                with dve.Fori(0, KT) as j:
                    quad = quad0 + Q_CONV + j
                    a0 = A_LAYER * lay + 2 * j + (A_B2 + A_CONV)
                    dve.wait_ge(acc_free[0], a0 + 2)
                    dve.wait_ge(panel_done, 4 * quad + 2)
                    v.memset(cu[:, 0:2], 0.0)
                    v.scalar_tensor_tensor(full(cu[:, 2:L + 2]), acc(1), bias(quad, 1), full(eh[:]),
                                           ALU.add, ALU.mult).then_inc(acc_free[1], 1)
                    dve.drain()
                    cw = 24 * lay + j + V_CW
                    v.tensor_scalar(c0[:], cu[:, 2:L + 2], col(cw + 16), col(8 * lay + j + V_CB), ALU.mult, ALU.add)
                    dve.drain()
                    v.scalar_tensor_tensor(c1[:], cu[:, 1:L + 1], col(cw + 8), c0[:], ALU.mult, ALU.add)
                    dve.drain()
                    v.scalar_tensor_tensor(c2[:], cu[:, 0:L], col(cw), c1[:], ALU.mult, ALU.add)
                    dve.drain()
                    dve.wait_ge(panel_done, 4 * quad + 3)
                    v.scalar_tensor_tensor(full(cb_[:]), acc(0), bias(quad, 2), full(c2[:]),
                                           ALU.add, ALU.mult).then_inc(acc_free[0], 1)
                    dve.wait_ge(sig_ready, 24 * lay + j + (22 + 16 + 1))
                    v.scalar_tensor_tensor(full(cs[:]), acc(1), bias(quad, 3), full(ea[:, 1, :]),
                                           ALU.add, ALU.mult).then_inc(acc_free[1], 1)
                    dve.drain()
                    v.tensor_tensor(val[:, 0, :], cs[:], cb_[:], ALU.mult).then_inc(val_ready, 1)
                    low_part(i0 + 24 + j, 0, tile(cl, j), tile(ch, j))
                with dve.Fori(0, 2) as r:
                    a0 = A_LAYER * lay + 6 * r + (A_B2 + A_MERGE)
                    for t in range(4):
                        for n in range(3 * t + 1, 3 * t + 3):
                            dve.wait_ge(acc_free[n % 2], a0 + (n // 2 + 2))
                        yt = tile(y, 4 * r + t)
                        v.tensor_tensor(m1[:], ya[:, t % 2, :], g1[:, t % 2, :], ALU.mult)
                        v.tensor_tensor(m2[:], yt, g2[:, t % 2, :], ALU.mult)
                        dve.drain()
                        v.tensor_tensor(yt, m1[:], m2[:], ALU.add).then_inc(y_ready, 1)
                        dve.drain()
                for k in range(KT):
                    dve.wait_ge(valhi_ready, i0 + (33 + k))
                    v.tensor_tensor(ul[:, k, :], y[:, k, :], uh[:, k, :].bitcast(F32), ALU.subtract)\
                        .then_inc(vallo_ready, 1)
                v.memset(ssum[:], 0.0)
                with dve.Fori(0, 2) as r:
                    for s in range(4):
                        dve.wait_ge(acc_free[s % 2], A_LAYER * lay + 2 * r + (A_B2 + A_WO + s // 2 + 2))
                        add_square(tile(y, 4 * r + s))
                        dve.drain()
                dve.drain().then_inc(ssum_ready, 1)
                inv_rms(6 * lay + 8)
                for k in range(KT):
                    v.scalar_tensor_tensor(m1[:], y[:, k, :], col(8 * lay + (V_POST + k)), rstd[:],
                                           ALU.mult, ALU.mult)
                    dve.drain()
                    v.tensor_tensor(h[:, k, :], h[:, k, :], m1[:], ALU.add).then_inc(h_tile, 1)
                    dve.drain()

        @block.tensor
        def _(pe):
            mm = nc.tensor.matmul

            for s in acc_free:
                pe.sem_inc(s, 1)
            pe.sem_inc(sq_free, 2)
            pe.sem_inc(root_ready, 1)
            pe.sem_inc(probsT_psum, 2)
            pe.sem_inc(heads_ready, 2)
            pe.sem_inc(probs_ready, 2)
            pe.sem_inc(heads_psum, 1)
            pe.sem_inc(hg_inv, 1)
            pe.sem_inc(y_ready, 2)

            def product(slot, wslot, xh, xl, k0, k1, rows0, first, last, n, ready=None):
                half = n // 2
                c = L - n
                for k in range(k0, k1):
                    if ready is not None and k - k0 < ready[1]:
                        pe.wait_ge(vallo_ready, ready[0] + (k - k0 + 1))
                    wcol = slice(P * k, P * k + P)
                    for w, x, part in ((wh, xh, 0), (wh, xl, 1), (wl, xh, 2)):
                        for a in range(2):
                            out = mm(ps[:, 2 * slot + a, 0:half], w[:, wslot, wcol],
                                     x(rows0 + k - k0, c + a * half, c + (a + 1) * half),
                                     start=first and k == k0 and part == 0,
                                     stop=last and k == k1 - 1 and part == 2)
                return out

            def xu(t, off=0):
                return lambda k, a, b: t[:, k, a - off:b - off]

            def use_panel(quad, s, a, xh=xu(uh), xl=xu(ul), n=L, ready=None):
                pe.wait_ge(lo_ready, 4 * quad + (s + 1))
                pe.wait_ge(acc_free[s % 2], a + 1)
                product(s % 2, s % 2, xh, xl, 0, KT, 0, True, True, n, ready).then_inc(panel_done, 1)

            def sum_squares(first, nth):
                pe.wait_ge(root_ready, nth + 1)
                half = L // 2
                for k in range(KT):
                    pe.wait_ge(sq_ready, first + (k + 1))
                    for a in range(2):
                        out = mm(ps[:, 4 + a, 0:half], mean_d[:], sq[:, k % 2, a * half:(a + 1) * half],
                                 start=k == 0, stop=k == KT - 1)
                    out.then_inc(sq_free, 1)
                pe.drain().then_inc(meansq_ready, 1)

            def mean_square(sums, nth, weight, n=L):
                pe.wait_ge(root_ready, nth + 1)
                pe.wait_ge(ssum_ready, sums + 1)
                half, c = n // 2, L - n
                for a in range(2):
                    out = mm(ps[:, 4 + a, 0:half], weight[:], ssum[:, c + a * half:c + (a + 1) * half],
                             start=True, stop=True)
                out.then_inc(meansq_ready, 1)

            def transposes(src, done, blocks=KEYS):
                for n, (a, b) in enumerate(blocks):
                    dst = ps[0:b - a, 5, 0:P] if b - a == META else ps[:, 4, P * (n - 1):P * n]
                    out = nc.tensor.transpose(dst, src[:, a:b], ident[:])
                out.then_inc(done, 1)

            pe.wait_ge(small_loaded, 16 * 5)
            pe.wait_ge(consts_set, 1)
            sum_squares(0, 0)
            pe.wait_ge(wff_lo, 1)
            pe.wait_ge(root_ready, 2)
            for k in range(KT):
                pe.wait_ge(vallo_ready, k + 1)
                for w, x, part in ((wffh, uh, 0), (wffh, ul, 1), (wffl, uh, 2)):
                    for a in range(2):
                        out = mm(ps[0:8, 4 + a, 0:L // 2], w[:, 8 * k:8 * k + 8], x[:, k, a * (L // 2):(a + 1) * (L // 2)],
                                 start=k == 0 and part == 0, stop=k == KT - 1 and part == 2)
            out.then_inc(ff_psum, 1)
            with pe.Fori(0, 3) as q:
                for s in range(4):
                    use_panel(q, s, 2 * q + s // 2)
            with pe.Fori(0, HEADS) as hd:
                last = LEVELS % 2
                for s in range(4):
                    use_panel(hd + 3, s, 2 * hd + (6 + s // 2))
                    if s == 0:
                        pe.wait_ge(hg_vt, hd + 1)
                        pe.wait_ge(hg_inv, hd + 1)
                        pe.wait_ge(ff_ln, 1)
                        transposes(vt[:], hg_vpsum)
                    for l in (2 * s, 2 * s + 1):
                        b = l % 2
                        pe.wait_ge(hg_kl, (LEVELS + 1) * hd + (l + 1))
                        pe.wait_ge(hg_q, (LEVELS + 1) * hd + (l + 1))
                        if l == LEVELS:
                            continue
                        if l >= 2:
                            pe.wait_ge(hg_pred, LEVELS * hd + (l - 1))
                        for i in range(XT):
                            out = mm(ps[:, 6 + b, P * i:P * i + P], kl[:, b, P * i:P * i + P],
                                     ql[:, b, P * i:P * i + P], start=True, stop=True)
                        out.then_inc(hg_s, 1)
                pe.wait_ge(hg_km, hd + 1)
                pe.wait_ge(hg_vn, hd + 1)
                nc.tensor.transpose(ps[0:META, 5, 0:P], km[:], ident[:])
                for i in range(XT - 1):
                    out = nc.tensor.transpose(ps[:, 4, P * i:P * i + P], kl[:, last, P * i:P * i + P], ident[:])
                out.then_inc(hg_kpsum, 1)
                pe.wait_ge(hg_kn, hd + 1)
                for i in range(XT):
                    rows = META if i == 0 else P
                    out = mm(ps[:, 4, P * i:P * i + P], kn[0:rows, i, :], vn[0:rows, i, :], start=True, stop=True)
                out.then_inc(hg_upsum, 1)
                pe.wait_ge(hg_pred, LEVELS * hd + LEVELS)
                pe.wait_ge(hg_state, hd + 1)
                for i in range(XT):
                    dst = ps[:, 6, P * i:P * i + P]
                    mm(dst, vn[:, i + 1, :], amat[:, P * i:P * i + P], start=True, stop=False)
                    out = mm(dst, st[:, i, :], ql[:, last, P * i:P * i + P], start=False, stop=True)
                out.then_inc(hg_o, 1)
                pe.wait_ge(hg_sq, hd + 1)
                mm(ps[:, 7, :], mean_h[:], sq[:, 0, 0:SEQ], start=True, stop=True).then_inc(hg_ss, 1)

            pe.wait_ge(hg_inv, HEADS + 1)
            pe.wait_ge(acc_free[1], A_OUT + 1)
            for j in range(4):
                if j:
                    pe.wait_ge(fv_ready, j)
                transposes(proj[:, 8 + j, :], fv_psum)
            pe.wait_ge(cum_ready, 1)
            pe.wait_ge(fv_ready, 4)
            pe.wait_ge(acc_free[0], A_OUT + 1)
            with pe.Fori(0, 4) as hp:
                pe.wait_ge(fox_in, hp + 1)
                for n in range(10):
                    if n < 8:
                        b, i, e = n % 2, n % 4, n // 4
                        q0, nk = KEYS[i + 1]
                        pe.wait_ge(probs_ready, 8 * hp + (n + 1))
                        for bank, (ka, kb) in enumerate(((0, min(nk, 272)), (272, nk))):
                            if ka >= kb:
                                continue
                            c = 240 if bank == 0 else 0
                            diag = ka <= q0 < kb
                            dst = ps[:, 2 * b + bank, c:c + kb - ka]
                            mm(dst, qs[64 * e:64 * e + 64, q0:nk], ks[64 * e:64 * e + 64, ka:kb], start=True, stop=False)
                            out = mm(dst, selp[:, e, :], cparts[:, ka:kb], start=False, stop=not diag)
                            if diag:
                                out = mm(ps[:, 2 * b + bank, c + q0 - ka:c + nk - ka], identb[:], causal[:],
                                         start=False, stop=True)
                        out.then_inc(scores_ready, 1)
                    if 1 <= n < 9:
                        m = n - 1
                        b, i, e = m % 2, m % 4, m // 4
                        pe.wait_ge(probs_ready, 8 * hp + (m + 3))
                        if m >= 1:
                            pe.wait_ge(probsT_ready, 8 * hp + m)
                        transposes(probs[:, b, :], probsT_psum, KEYS[:i + 2])
                    if n >= 2:
                        m = n - 2
                        b, i, e = m % 2, m % 4, m // 4
                        pe.wait_ge(probsT_ready, 8 * hp + (m + 1))
                        pe.wait_ge(heads_ready, 8 * hp + (m + 1))
                        for t in range(i + 2):
                            rows = META if t == 0 else P
                            out = mm(ps[:, 6 + b, 0:64], pT[0:rows, b, t, :], vs[0:rows, t, 64 * e:64 * e + 64],
                                     start=t == 0, stop=t == i + 1)
                        out.then_inc(heads_psum, 1)
            pe.wait_ge(heads_ready, 34)
            for k in range(4):
                for i in range(XT):
                    out = nc.tensor.transpose(ps[:, k, P * i:P * i + P], onat[:, i, P * k:P * k + P], ident[:])
                out.then_inc(headsT_psum, 1)

            pe.wait_ge(val_ready, 16)
            with pe.Fori(0, 2) as r:
                for s in range(4):
                    use_panel(r + Q_OUT, s, 2 * r + (A_OUT + s // 2), n=SEQ, ready=(12, 4) if s == 0 else None)
            mean_square(0, 1, mean_d, SEQ)
            with pe.Fori(0, 11) as r:
                for s in range(4):
                    use_panel(r + Q_FF, s, 2 * r + (A_FF + s // 2), n=SEQ, ready=(16, KT) if s == 0 else None)
            with pe.Fori(0, 2) as r:
                for n in range(12):
                    t, third = n // 3, n % 3
                    pe.wait_ge(lo_ready, 12 * r + (4 * Q_DOWN + n + 1))
                    if third == 0:
                        pe.wait_ge(acc_free[t % 2], 2 * r + (A_DOWN + t // 2 + 1))
                    product(t % 2, n % 2, xu(gh, META), xu(gl_, META), 0, KT if third < 2 else FT - 2 * KT,
                            KT * third, third == 0, third == 2, SEQ,
                            (24 + KT * third, KT) if t == 0 else None).then_inc(panel_done, 1)
            mean_square(1, 2, mean_d, SEQ)
            pe.wait_ge(consts_set, 2)

            with pe.Fori(0, 2) as lay:
                quad0 = lay * Q_LAYER + Q_B2
                i0 = 40 * lay + 46
                sum_squares(8 * lay + 8, 6 * lay + 3)
                with pe.Fori(0, HEADS) as hd:
                    quad = 4 * hd + quad0
                    it = 4 * lay + hd
                    a0 = A_LAYER * lay + A_HEAD * hd + A_B2
                    for s in range(4):
                        use_panel(quad, s, a0 + s // 2, ready=(i0, KT) if s == 0 else None)

                    def v_transposes(j):
                        pe.wait_ge(acc_free[j % 2], a0 + (2 + j // 2 + 2))
                        if j:
                            pe.wait_ge(vn_ready, 4 * it + j)
                        else:
                            pe.wait_ge(root_ready, 6 * lay + hd + 5)
                        transposes(vraw[:, j % 2, :], vt_psum)

                    for s in range(4):
                        use_panel(quad + 1, s, a0 + (2 + s // 2))
                        if s:
                            v_transposes(s - 1)
                    use_panel(quad + 2, 0, a0 + 4)
                    v_transposes(3)
                    use_panel(quad + 2, 1, a0 + 4)
                    pe.wait_ge(rope_ready, 2 * it + 2)
                    for j, (ka, kb) in enumerate(KEYS):
                        if j == 1:
                            pe.wait_ge(vn_ready, 4 * it + 4)
                        if j >= 3:
                            pe.wait_ge(sd_ready, 5 * it + (j - 1))
                        bank = 6 if j == 0 else 4 + (j - 1) % 2
                        qa = META if j == 0 else ka
                        for c in range(2):
                            out = mm(ps[0:kb - ka, bank, 0:L - qa], kr[:, c, ka:kb], qr[:, c, qa:L],
                                     start=c == 0, stop=c == 1)
                        if j == 0:
                            for c in range(2):
                                out = mm(ps[0:META, 7, 0:META], kr[:, c, 0:META], qr[:, c, 0:META],
                                         start=c == 0, stop=c == 1)
                        out.then_inc(s_psum, 1)
                    pe.wait_ge(v_centred, it + 1)
                    pe.wait_ge(sd_ready, 5 * it + 5)
                    for j in range(4):
                        out = mm(ps[:, 7, META * j:META * (j + 1)], rvn[0:META, 0, P * j:P * j + P],
                                 sd[0:META, 0, 0:META], start=True, stop=True)
                    out.then_inc(o_psum_m, 1)
                    for j in range(4):
                        if j == 3:
                            pe.wait_ge(om_ready, it + 1)
                        for t, (ka, kb) in enumerate(KEYS):
                            qa = META if t == 0 else ka
                            out = mm(ps[:, 4 + j, qa - META:SEQ], rvn[0:kb - ka, t, P * j:P * j + P],
                                     sd[0:kb - ka, t, qa:L], start=t == 0, stop=t == 4)
                        out.then_inc(o_psum, 1)
                    pe.wait_ge(lo_ready, 4 * quad + 11)
                    pe.wait_ge(acc_free[0], a0 + 6)
                    product(0, 0, xu(uh), xu(ul), 0, 4, 0, True, False, L)
                    mean_square(5 * lay + hd + 2, 6 * lay + hd + 4, mean_g)
                    product(0, 0, xu(uh), xu(ul), 4, KT, 4, False, True, L).then_inc(panel_done, 1)
                    use_panel(quad + 2, 3, a0 + 5)
                    for s in range(4):
                        pe.wait_ge(lo_ready, 4 * quad + (12 + s + 1))
                        pe.wait_ge(acc_free[0], a0 + (6 + s + 1))
                        product(0, s % 2, xu(rh), xu(rl), 0, 4, 0, True, True, L,
                                (i0 + 4 * hd + 8, 4) if s == 0 else None).then_inc(half_done, 1)
                        pe.wait_ge(acc_free[1], a0 + (6 + s + 1))
                        product(1, s % 2, xu(rh), xu(rl), 4, 8, 0, True, True, L).then_inc(panel_done, 1)
                with pe.Fori(0, KT) as j:
                    for s in range(4):
                        use_panel(quad0 + Q_CONV + j, s, A_LAYER * lay + 2 * j + (A_B2 + A_CONV + s // 2))
                with pe.Fori(0, 2) as r:
                    for n in range(12):
                        a = A_LAYER * lay + 6 * r + (A_B2 + A_MERGE + n // 2)
                        x = (xu(ch), xu(cl)) if n % 3 == 0 else (xu(uh), xu(ul))
                        use_panel(quad0 + Q_MERGE + 3 * r + n // 4, n % 4, a, *x,
                                  ready=(i0 + 24, KT) if n == 0 else None)
                with pe.Fori(0, 2) as r:
                    for s in range(4):
                        use_panel(quad0 + Q_WO + r, s, A_LAYER * lay + 2 * r + (A_B2 + A_WO + s // 2),
                                  ready=(i0 + 32, KT) if s == 0 else None)
                mean_square(5 * lay + 6, 6 * lay + 8, mean_d)


def panels(w):
    import numpy as np
    k, n = w.shape
    out = np.zeros((n // P, P, KT, P), np.float32)
    out[:, :, :k // P] = w.reshape(k // P, P, n // P, P).transpose(2, 1, 0, 3)
    return out


def weight_stream(i):
    import numpy as np
    win, wd = i["w_in"][0], i["w_ffn_down"][0]
    parts = [panels(win[:, c:c + 512]) for c in (1544, 2056, 2568)]
    hg_, fq, fk, fv = (panels(win[:, c:c + 512]) for c in (3080, 0, 512, 1024))
    parts.append(np.stack([hg_, fq, fk, fv], 1).reshape(16, P, KT, P))
    parts.append(panels(i["w_out"][0]))
    gate, up = panels(i["w_ffn_gate"][0]), panels(i["w_ffn_up"][0])
    parts.append(np.stack([gate, up], 1).reshape(2 * FT, P, KT, P))
    down = [panels(wd[r:r + D]) for r in range(0, FF, D)]
    parts.append(np.stack(down, 1).reshape(3 * KT, P, KT, P))
    for l in range(2):
        w = i["w_in_2"][l]
        p = panels(w)
        wr = i["w_ret_out_2"][l]
        for hd in range(HEADS):
            parts += [p[40 + 2 * hd:42 + 2 * hd], p[32 + 2 * hd:34 + 2 * hd], p[48 + 4 * hd:52 + 4 * hd],
                      p[64 + 4 * hd:68 + 4 * hd]]
            r = wr[512 * hd:512 * hd + 512].reshape(4, P, 4, 2, P)
            parts.append(r.transpose(2, 1, 3, 0, 4).reshape(4, P, KT, P))
        parts.append(np.stack([p[0:8], p[16:24], p[8:16], p[24:32]], 1).reshape(32, P, KT, P))
        parts.append(np.stack([panels(i["w_conv_out_2"][l]), p[80:88], p[88:96]], 1).reshape(24, P, KT, P))
        parts.append(panels(i["w_o_2"][l]))
    parts.append(np.zeros((2, P, KT, P), np.float32))
    return np.concatenate(parts).reshape(4 * QUADS + 2, P, KT * P)


def vector_table(i):
    import numpy as np
    v = np.zeros((P, V_COLS), np.float32)

    def put(c, x):
        x = np.asarray(x).reshape(-1, P)
        v[:, c:c + len(x)] = x.T
    put(V_MIX, i["norm_mix_w"][0])
    put(V_FFN, i["norm_ffn_w"][0])
    put(V_FINAL, i["norm_final_w"])
    put(V_HNORM, i["hgrn_norm_w"][0])
    put(V_LB, i["hgrn_lb_raw"][0])
    for l in range(2):
        put(V_PRE + 8 * l, i["pre_norm_g_2"][l])
        put(V_POST + 8 * l, i["post_norm_g_2"][l])
        put(V_CW + 24 * l, i["conv_w_2"][l])
        put(V_CB + 8 * l, i["conv_b_2"][l])
        put(V_GN + 16 * l, i["ret_gn_g_2"][l])
        b = i["b_in_2"][l].reshape(96, P)
        c = V_BIAS + 4 * Q_LAYER * l
        for hd in range(HEADS):
            put(c + 16 * hd, np.concatenate([b[40 + 2 * hd:42 + 2 * hd], b[32 + 2 * hd:34 + 2 * hd],
                                             b[48 + 4 * hd:52 + 4 * hd], b[64 + 4 * hd:68 + 4 * hd]]))
        put(c + 4 * Q_CONV, np.stack([b[0:8], b[16:24], b[8:16], b[24:32]], 1))
        put(c + 4 * Q_MERGE, np.stack([np.zeros((8, P), np.float32), b[80:88], b[88:96]], 1))
    v[:, V_EPS], v[:, V_EPS + 1] = EPS, GN_EPS
    return v


def tables():
    import numpy as np
    inv = (10000.0 ** (-np.arange(P, dtype=np.float64) / P)).astype(np.float32)
    ang = (np.arange(L, dtype=np.float32)[None, :] * inv[:, None]).astype(np.float64)
    lg = np.log(1.0 - 2.0 ** (-5.0 - np.arange(HEADS)))[None, :, None]
    p, x = np.arange(P)[:, None, None], np.arange(SEQ)[None, None, :]
    decx = np.exp(lg * abs(x - p)) * (p // 64 <= x // 64) / 16.0
    p, x = np.arange(META)[:, None, None], np.arange(L)[None, None, :]
    decm = np.exp(lg * abs(x - p)) / 16.0
    s, t = np.arange(P)[:, None], np.arange(P)[None, :]
    masks = np.zeros((P, LEVELS, P), np.int32)
    masks[:, 0] = (s // 2 == t // 2) & (s <= t)
    for l in range(1, LEVELS):
        b = 2 ** l
        masks[:, l] = (s // b + 1 == t // b) & (s // b % 2 == 0)
    sel = np.zeros((96, 8, P), np.float32)
    for part in (0, 32, 64):
        sel[part + np.arange(8), np.arange(8)] = -8.0
    f = np.float32
    return {"cos": np.cos(ang).astype(f), "sin": np.sin(ang).astype(f), "decx": decx.astype(f),
            "decm": decm.astype(f), "masks": masks, "sel": sel.reshape(96, 8 * P), "ident": np.eye(P, dtype=f),
            "causal": np.where(t > s, f(-8e30), f(0)).astype(f)}


def kernel(**inputs):
    import numpy as np
    import concourse.bacc as bacc
    from concourse.bass_utils import run_bass_kernel_spmd as run

    i = {k: np.asarray(a) for k, a in inputs.items()}

    def feature_major(a):
        return np.ascontiguousarray(a.reshape(-1, KT, P).transpose(2, 1, 0))

    arrays = tables()
    arrays["x"] = feature_major(i["x"][0])
    arrays["meta"] = feature_major(i["meta"])
    arrays["meta2"] = feature_major(i["meta_2"])
    arrays["weights"] = weight_stream(i)
    arrays["wff"] = np.ascontiguousarray(i["w_in"][0][:, 1536:1544].reshape(KT, P, 8).transpose(1, 0, 2)).reshape(P, KT * 8)
    arrays["fbias"] = np.ascontiguousarray(i["fox_f_bias"][0].reshape(8, 1))
    arrays["vec"] = vector_table(i)

    nc = bacc.Bacc("TRN2", target_bir_lowering=False, num_devices=1)
    io = {n: nc.dram_tensor("in_" + n, a.shape, mybir.dt.from_np(a.dtype), kind="ExternalInput").ap()
          for n, a in arrays.items()}
    io["out"] = nc.dram_tensor("out", (P, KT, SEQ), F32, kind="ExternalOutput").ap()
    build(nc, io)
    r = run(nc, [{"in_" + n: a for n, a in arrays.items()}], core_ids=[0])
    return r.results[0]["out"].transpose(2, 1, 0).reshape(1, SEQ, D)
```

```python
from contextlib import ExitStack

import concourse.bass as bass
from concourse import mybir

F32 = mybir.dt.float32
F32R = mybir.dt.float32r
BF16 = mybir.dt.bfloat16
I32 = mybir.dt.int32
ALU = mybir.AluOpType
ACT = mybir.ActivationFunctionType
AX = mybir.AxisListType

P = 128
D = 1024
KT = D // P
META = 16
SEQ = 512
L = META + SEQ
XT = SEQ // P
FF = 2816
FT = FF // P
HEADS = 4
EPS = 1e-6
GN_EPS = 1e-5
F_MIN = 9.357622968840175e-14
LEVELS = 7
LEVELS_AT = ((0, 1), (2, 3), (4, 5, 6, 7), ())

Q_IN, Q_OUT, Q_FF, Q_DOWN, Q_B2 = 0, 7, 9, 20, 26
Q_HEAD, Q_CONV, Q_MERGE, Q_WO, Q_LAYER = 4, 16, 24, 30, 32
QUADS = Q_B2 + 2 * Q_LAYER
A_OUT, A_FF, A_DOWN, A_B2 = 14, 18, 40, 44
A_HEAD, A_CONV, A_MERGE, A_WO, A_LAYER = 10, 40, 56, 68, 72

V_MIX, V_FFN, V_FINAL, V_HNORM, V_LB, V_PRE, V_POST = 0, 8, 16, 24, 25, 29, 45
V_CW, V_CB, V_GN, V_BIAS = 61, 109, 125, 157
V_EPS = V_BIAS + 2 * 4 * Q_LAYER
V_COLS = V_EPS + 2

KEYS = [(0, META)] + [(META + P * i, META + P * (i + 1)) for i in range(XT)]


def build(nc, io):
    with ExitStack() as ctx:
        def sb(name, shape, dt=F32, scope=ctx):
            return scope.enter_context(nc.sbuf_tensor(name, shape, dt))

        def sem(name):
            return ctx.enter_context(nc.semaphore(name))

        h = sb("h", [P, KT, L])
        uh, ul = sb("uh", [P, KT, L], F32R), sb("ul", [P, KT, L], F32R)
        raw = sb("raw", [P, 4, KT * P])
        wh, wl = sb("wh", [P, 2, KT * P], F32R), sb("wl", [P, 2, KT * P], F32R)
        vec = sb("vec", [P, V_COLS])
        ident = sb("ident", [P, P])
        mean_d, mean_h = sb("mean_d", [P, P]), sb("mean_h", [P, P])
        ones = sb("ones", [P, META])
        val = sb("val", [P, 2, L])
        sq = sb("sq", [P, 2, L])
        ssum = sb("ssum", [P, L])
        rstd = sb("rstd", [P, L])
        meta2 = sb("meta2", [P, KT, META])
        ea = sb("ea", [P, 2, L])

        mix = ExitStack()
        proj = sb("proj", [P, 28, L], F32, mix)
        lbt = sb("lbt", [P, 5, 4], F32, mix)
        lb1 = sb("lb1", [P, 5], F32, mix)
        fbias = sb("fbias", [8, 1], F32, mix)
        wffh, wffl = sb("wffh", [P, KT * 8], F32R, mix), sb("wffl", [P, KT * 8], F32R, mix)
        cparts = sb("cparts", [96, L], BF16, mix)
        cz, ct, cone, ccum, cres = (proj[0:8, i, :] for i in range(5))
        cparts0 = [sb(f"cpart{n}", [8, L], BF16, mix) for n in range(3)]
        wff_raw = proj[:, 6, 0:KT * 8]
        hg = ExitStack()
        gl, sgq, vt = (sb("hg_" + n, [P, L], F32, hg) for n in ("g", "sgq", "vt"))
        vn = sb("hg_vn", [P, 5, P], F32, hg)
        eq, ek = sb("hg_eq", [P, 2, SEQ], F32, hg), sb("hg_ek", [P, 2, SEQ], F32, hg)
        ql, kl = sb("hg_ql", [P, 2, SEQ], F32, hg), sb("hg_kl", [P, 2, SEQ], F32, hg)
        em, km, pm = (sb("hg_" + n, [P, META], F32, hg) for n in ("em", "km", "pm"))
        resets = sb("hg_resets", [P, LEVELS, SEQ], BF16, hg)
        odd = sb("hg_odd", [P, SEQ], BF16, hg)
        masks = sb("hg_masks", [P, LEVELS, P], I32, hg)
        carrier = sb("hg_carrier", [P, LEVELS], F32, hg)
        act_carrier = sb("hg_act_carrier", [P, 1], F32, hg)
        amat = sb("hg_amat", [P, SEQ], F32, hg)
        kn = sb("hg_kn", [P, 4, P], F32, hg)
        st = sb("hg_state", [P, 4, P], F32, hg)
        ot = val[:, 0, 0:SEQ]
        hg.close()
        staged_sel = (val[0:96, 1, 0:4 * P], ssum[0:96, 0:4 * P])
        fox = ExitStack()
        sel = sb("sel", [96, 8, P], BF16, fox)
        selp = sb("selp", [96, 2, P], BF16, fox)
        causal, identb = sb("causal", [P, P], BF16, fox), sb("identb", [P, P], BF16, fox)
        vnat = sb("vnat", [P, 5, 4 * P], F32, fox)
        qs, ks = sb("qs", [P, L], F32, fox), sb("ks", [P, L], F32, fox)
        probs = sb("probs", [P, 2, L], F32, fox)
        pT = sb("pT", [P, 2, 5, P], F32, fox)
        fmax, fneg, fsum, finv = (sb(n, [P, 4], F32, fox) for n in ("fmax", "fneg", "fsum", "finv"))
        onat = proj[:, 8:8 + XT, 0:4 * P]
        fox.close()
        mix.close()

        ffn = ExitStack()
        gs = sb("gs", [P, L], F32, ffn)
        gh, gl_ = sb("gh", [P, FT, SEQ], F32R, ffn), sb("gl", [P, FT, SEQ], F32R, ffn)
        ffn.close()

        y = sb("y", [P, KT, L])
        ret = ExitStack()
        cos, sin = sb("cos", [P, L], F32, ret), sb("sin", [P, L], F32, ret)
        decx, decm = sb("decx", [P, HEADS, SEQ], F32, ret), sb("decm", [META, HEADS, L], F32, ret)
        mean_g = sb("mean_g", [P, P], F32, ret)
        kq = sb("kq", [P, 4, L], F32, ret)
        r1, r2 = sb("r1", [P, L], F32, ret), sb("r2", [P, L], F32, ret)
        vraw = ea
        zg = (ea[:, 0, :], ea[:, 1, :], r1[:], r2[:])
        full32 = ExitStack()
        rvn = sb("rvn", [P, 5, 4 * P], F32, full32)
        sd = sb("sd", [P, 5, L], F32, full32)
        kr, qr = sb("kr", [P, 2, L], F32, full32), sb("qr", [P, 2, L], F32, full32)
        full32.close()
        rvl, sdl = sb("rvl", [P, 5, 4 * P], F32R, ret), sb("sdl", [P, 5, L], F32R, ret)
        rh = sb("rh", [P, 4, L], F32R, ret)
        vmean = sb("vmean", [P, 5], F32, ret)
        vneg = sb("vneg", [P, 5], F32, ret)
        rvh, sdh = sb("rvh", [P, 4, 4 * P], F32R, ret), sb("sdh", [P, 4, L], F32R, ret)
        om = sb("om", [P, 4, META], F32, ret)
        rl = sb("rl", [P, 4, L], F32R, ret)
        keep = ExitStack()
        ret.close()
        sb("keep_tables", [P, 2 * L + HEADS * SEQ + HEADS * L + P], F32, keep)
        ch, cl = sb("ch", [P, KT, L], F32R, keep), sb("cl", [P, KT, L], F32R, keep)
        eh = sb("eh", [P, L], F32, keep)
        cu = sb("cu", [P, L + 2], F32, keep)
        c0, c1, c2, cb_, cs = (sb("cv_" + n, [P, L], F32, keep) for n in ("c0", "c1", "c2", "b", "s"))
        ya, g1, g2 = (sb(n, [P, 2, L], F32, keep) for n in ("ya", "g1", "g2"))
        m1, m2 = sb("m1", [P, L], F32, keep), sb("m2", [P, L], F32, keep)
        keep.close()

        ps = ctx.enter_context(nc.psum_tensor("ps", [P, 8, 512], F32))

        raw_full = [sem(f"raw_full{i}") for i in range(4)]
        hi_ready, lo_ready = sem("hi_ready"), sem("lo_ready")
        panel_done = sem("panel_done")
        half_done = sem("half_done")
        acc_free = [sem(f"acc_free{i}") for i in range(2)]
        h_loaded = [sem(f"h_loaded{i}") for i in range(4)]
        small_loaded, tables_loaded = sem("small_loaded"), sem("tables_loaded")
        consts_set, masks_loaded, fox_loaded = sem("consts_set"), sem("masks_loaded"), sem("fox_loaded")
        sq_ready, sq_free = sem("sq_ready"), sem("sq_free")
        ssum_ready = sem("ssum_ready")
        meansq_ready = sem("meansq_ready")
        root_ready = sem("root_ready")
        val_ready, valhi_ready, vallo_ready = sem("val_ready"), sem("valhi_ready"), sem("vallo_ready")
        h_even, h_odd = sem("h_even"), sem("h_odd")
        post_ready = sem("post_ready")
        sig_ready = sem("sig_ready")
        wff_hi, wff_lo, ff_psum, ff_abs, ff_ln, cum_ready = (sem(n) for n in (
            "wff_hi", "wff_lo", "ff_psum", "ff_abs", "ff_ln", "cum_ready"))
        fv_psum, fv_ready, fox_in, scores_ready, negmax_ready, probs_ready = (sem(n) for n in (
            "fv_psum", "fv_ready", "fox_in", "scores_ready", "negmax_ready", "probs_ready"))
        probsT_psum, probsT_ready, heads_psum, heads_ready, headsT_psum = (sem(n) for n in (
            "probsT_psum", "probsT_ready", "heads_psum", "heads_ready", "headsT_psum"))
        hg_sig, hg_f, hg_g, hg_vt, hg_vpsum, hg_vn, hg_exp_in, hg_exp_out = (sem("hg_" + n) for n in (
            "sig", "f_ready", "g_ready", "vt_ready", "v_psum", "v_nat", "exp_in", "exp_out"))
        hg_q, hg_s, hg_pred, hg_min, hg_mout, hg_km, hg_kpsum, hg_kn, hg_upsum, hg_state = (
            sem("hg_" + n) for n in ("q_ready", "s_psum", "a_ready", "meta_in", "meta_out",
                                     "meta_k", "k_psum", "k_nat", "u_psum", "state_ready"))
        hg_o, hg_sq, hg_ss, hg_root, hg_inv = (sem("hg_" + n) for n in (
            "o_psum", "squares", "meansq_psum", "root_ready", "iter_free"))
        hg_kl, hg_gate = sem("hg_k_ready"), sem("hg_gate_ready")
        lb_exp, lb_in = sem("lb_exp"), sem("lb_in")
        rope_ready, vt_psum, vn_ready, v_centred, s_psum, sd_ready, o_psum = (sem(n) for n in (
            "rope_ready", "vt_psum", "vn_ready", "v_centred", "s_psum", "sd_ready", "o_psum"))
        vh_ready, sh_ready, parts_ready = sem("vh_ready"), sem("sh_ready"), sem("parts_ready")
        osq_ready = sem("osq_ready")
        om_ready, o_psum_m = sem("om_ready"), sem("o_psum_meta")
        ret_ready, ret_used = sem("ret_ready"), sem("ret_used")
        y_ready, out_stored = sem("y_ready"), sem("out_stored")

        block = ctx.enter_context(nc.Block())

        def full(t):
            return t.rearrange("p (a b) -> p a b", a=2)

        def seq(t):
            return t[:, META:L].rearrange("p (a b) -> p a b", a=2)

        def acc(slot, n=L):
            return ps[:, 2 * slot:2 * slot + 2, 0:n // 2]

        def col(c, width=1):
            return vec[:, bass.ds(c, width)]

        def tile(t, i):
            return t[:, bass.ds(i, 1), :].rearrange("p a b -> p (a b)")

        def scores(b):
            return ps[:, 2 * b:2 * b + 2, :].rearrange("p a b -> p (a b)")[:, 240:240 + L]

        def bias(quad, s):
            return col(4 * quad + (s + V_BIAS - 4 * Q_B2))

        @block.sync
        def _(sp):
            sp.dma_start(h[:, :, 0:META], io["meta"]).then_inc(h_loaded[0], 16)
            for k in range(4):
                sp.dma_start(h[:, 2 * k:2 * k + 2, META:L], io["x"][:, 2 * k:2 * k + 2, :]).then_inc(h_loaded[k], 16)
            for s in range(4):
                sp.dma_start(raw[:, s, :], io["weights"][s]).then_inc(raw_full[s], 16)
            with sp.Fori(1, QUADS) as q:
                for s in range(4):
                    sp.wait_ge(lo_ready, 4 * q + (s - 3))
                    sp.dma_start(raw[:, s, :], io["weights"][4 * q + s]).then_inc(raw_full[s], 16)
            for s in range(2):
                sp.wait_ge(lo_ready, 4 * QUADS - 3 + s)
                sp.dma_start(raw[:, s, :], io["weights"][4 * QUADS + s]).then_inc(raw_full[s], 16)
            for k in range(KT):
                sp.wait_ge((h_even, h_odd)[k % 2], KT + k // 2 + 1)
                sp.dma_start(io["out"][:, k, :], h[:, k, META:L]).then_inc(out_stored, 16)
            sp.wait_ge(out_stored, 16 * KT)

        @block.gpsimd
        def _(pool):
            pool.memset(mean_d[:], 1.0 / D)
            pool.memset(ones[:], 1.0)
            pool.drain().then_inc(consts_set, 1)
            pool.dma_start(vec[:], io["vec"]).then_inc(small_loaded, 16)
            pool.dma_start(ident[:], io["ident"]).then_inc(small_loaded, 16)
            pool.dma_start(wff_raw, io["wff"]).then_inc(small_loaded, 16)
            pool.dma_start(fbias[:], io["fbias"]).then_inc(small_loaded, 16)
            pool.dma_start(meta2[:], io["meta2"]).then_inc(small_loaded, 16)
            pool.dma_start(masks[:], io["masks"]).then_inc(masks_loaded, 16)
            pool.memset(mean_h[:], 1.0 / P)
            pool.memset(cone, 1.0)
            pool.memset(cparts[:], 0.0)
            pool.memset(resets[:], 1.0)
            pool.memset(odd[:], 0.0)
            pool.drain()
            for l in range(1, LEVELS + 1):
                pool.memset(resets[:, l - 1, :].rearrange("p (n b) -> p n b", b=2 ** l)[:, :, 0:1], 0.0)
            pool.memset(odd.rearrange("p (n b) -> p n b", b=2)[:, :, 1:2], 1.0)
            pool.drain().then_inc(consts_set, 1)

            def split_low(q, s):
                pool.wait_ge(hi_ready, 4 * q + (s + 1))
                nc.gpsimd.tensor_tensor(wl[:, s % 2, :], raw[:, s, :], wh[:, s % 2, :].bitcast(F32),
                                        ALU.subtract).then_inc(lo_ready, 1)

            with pool.Fori(0, 3) as q:
                for s in range(4):
                    split_low(q, s)
            for s in range(2):
                split_low(3, s)
            for dst, src in zip(staged_sel, (io["sel"][:, 0:4 * P], io["sel"][:, 4 * P:8 * P])):
                pool.dma_start(dst, src).then_inc(fox_loaded, 16)
            pool.dma_start(sq[:, 1, 0:P], io["causal"]).then_inc(fox_loaded, 16)
            with pool.Fori(0, HEADS) as hd:
                for s in range(4):
                    for l in LEVELS_AT[s]:
                        pool.wait_ge(hg_exp_out, (LEVELS + 1) * hd + (l + 1))
                        if l >= 2:
                            pool.wait_ge(hg_s, LEVELS * hd + (l - 1))
                        nc.gpsimd.tensor_tensor(kl[:, l % 2, :], sgq[:, META:L], ek[:, l % 2, :],
                                                ALU.mult).then_inc(hg_kl, 1)
                    split_low(hd + 3 + (s + 2) // 4, (s + 2) % 4)
            for s in (2, 3):
                split_low(7, s)
            with pool.Fori(8, Q_B2) as q:
                for s in range(4):
                    split_low(q, s)
            pool.wait_ge(ssum_ready, 2)
            for dst, name in ((cos, "cos"), (sin, "sin"), (decx, "decx"), (decm, "decm")):
                pool.dma_start(dst[:], io[name]).then_inc(tables_loaded, 16)
            pool.memset(mean_g[:], 1.0 / (4 * P)).then_inc(consts_set, 1)
            with pool.Fori(0, 2) as lay:
                with pool.Fori(0, Q_LAYER) as q:
                    for s in range(4):
                        split_low(Q_LAYER * lay + q + Q_B2, s)
                for k in range(4):
                    pool.wait_ge(post_ready, 4 * lay + (k + 1))
                    nc.gpsimd.tensor_tensor(h[:, 2 * k + 1, :], h[:, 2 * k + 1, :], y[:, 2 * k + 1, :],
                                            ALU.add).then_inc(h_odd, 1)

        @block.scalar
        def _(act):
            def split_ahead(quad, s):
                s2 = (s + 2) % 4
                act.wait_ge(raw_full[s2], 16 * quad + 16 * (1 + (s + 2) // 4))
                act.wait_ge(panel_done, 4 * quad + (s + 1))
                nc.scalar.activation(wh[:, s2 % 2, :], raw[:, s2, :], ACT.Copy).then_inc(hi_ready, 1)

            def split_value(index, slot, dst, vindex=None, c0=0):
                act.wait_ge(val_ready, (index if vindex is None else vindex) + 1)
                nc.scalar.activation(dst, val[:, slot, c0:L], ACT.Copy).then_inc(valhi_ready, 1)

            def squares(first, tile0=None):
                for k in range(KT):
                    if tile0 is not None:
                        act.wait_ge((h_even, h_odd)[k % 2], tile0 + (k // 2 + 1))
                    elif k % 2 == 0:
                        act.wait_ge(h_loaded[k // 2], 32 if k == 0 else 16)
                    act.wait_ge(sq_free, first + (k + 1))
                    nc.scalar.activation(sq[:, k % 2, :], h[:, k, :], ACT.Square).then_inc(sq_ready, 1)

            eps, gn_eps = col(V_EPS), col(V_EPS + 1)

            def take_root(nth, eps, c0=0):
                act.wait_ge(meansq_ready, nth + 1)
                view = seq if c0 else full
                nc.scalar.activation(view(rstd[:]), acc(2, L - c0), ACT.Sqrt, bias=eps).then_inc(root_ready, 1)

            squares(0)
            act.wait_ge(small_loaded, 16 * 5)
            nc.scalar.activation(wffh[:], wff_raw, ACT.Copy).then_inc(wff_hi, 1)
            take_root(0, eps)
            for s in range(2):
                act.wait_ge(raw_full[s], 16)
                nc.scalar.activation(wh[:, s, :], raw[:, s, :], ACT.Copy).then_inc(hi_ready, 1)
            for k in range(KT):
                split_value(k, k % 2, uh[:, k, :])
            act.wait_ge(ff_psum, 1)
            nc.scalar.activation(full(cz), ps[0:8, 4:6, 0:L // 2], ACT.Identity, bias=fbias[:])
            act.drain()
            nc.scalar.activation(ct, cz, ACT.Abs)
            act.drain()
            nc.scalar.activation(ct, ct, ACT.Exp, scale=-1.0)
            act.wait_ge(lb_in, 1)
            nc.scalar.activation(lbt[:, 1, :], lbt[:, 0, :], ACT.Exp).then_inc(lb_exp, 1)
            act.drain()
            nc.scalar.activation(ct, ct, ACT.Ln, bias=1.0).then_inc(ff_ln, 1)

            def evacuate(s, dst):
                nc.scalar.activation(full(dst), acc(s % 2), ACT.Copy).then_inc(acc_free[s % 2], 1)

            with act.Fori(0, 3) as q:
                for s in range(4):
                    split_ahead(q, s)
                    evacuate(s, tile(proj, 4 * q + (12 + s)))
            def head_sigmoids(hd):
                nc.scalar.activation(gl[:], tile(proj, hd + 16), ACT.Sigmoid, scale=-1.0)
                nc.scalar.activation(sgq[:], tile(proj, hd + 12), ACT.Sigmoid).then_inc(hg_sig, 1)

            act.drain()
            head_sigmoids(0)
            with act.Fori(0, HEADS) as hd:
                act.wait_ge(hg_f, hd + 1)
                nc.scalar.activation(gl[:], gl[:], ACT.Ln).then_inc(hg_g, 1)
                act.wait_ge(hg_min, hd + 1)
                nc.scalar.activation(em[:], em[:], ACT.Exp).then_inc(hg_mout, 1)
                for s, first in enumerate((24, 0, 4, 8)):
                    for l in LEVELS_AT[s]:
                        act.wait_ge(hg_exp_in, (LEVELS + 1) * hd + (l + 1))
                        nc.scalar.activation(eq[:, l % 2, :], eq[:, l % 2, :], ACT.Exp)
                        nc.scalar.activation(ek[:, l % 2, :], ek[:, l % 2, :], ACT.Exp).then_inc(hg_exp_out, 1)
                    if s == 3:
                        act.wait_ge(hg_kl, (LEVELS + 1) * hd + (LEVELS + 1))
                        nc.scalar.activation(act_carrier[:], eps, ACT.Copy)
                        nc.scalar.activation(ea[:, 0, :], tile(proj, hd + 24), ACT.Sigmoid).then_inc(hg_gate, 1)
                        head_sigmoids(hd + 1)
                    split_ahead(hd + 3, s)
                    evacuate(s, tile(proj, hd + first))
                act.wait_ge(hg_o, hd + 1)
                nc.scalar.activation(sq[:, 0, 0:SEQ], ps[:, 6, :], ACT.Square).then_inc(hg_sq, 1)
                act.wait_ge(hg_ss, hd + 1)
                nc.scalar.activation(rstd[:, 0:SEQ], ps[:, 7, :], ACT.Sqrt, bias=eps).then_inc(hg_root, 1)
            act.wait_ge(val_ready, 8 + HEADS)
            for k in range(HEADS):
                nc.scalar.activation(uh[:, 4 + k, META:L], proj[:, 24 + k, META:L],
                                     ACT.Copy).then_inc(valhi_ready, 1)

            with act.Fori(0, 4) as hp:
                for n in range(8):
                    b, i = n % 2, n % 4
                    nk = KEYS[i + 1][1]
                    act.wait_ge(negmax_ready, 8 * hp + (n + 1))
                    act.wait_ge(probsT_psum, 8 * hp + (n + 1))
                    act.wait_ge(heads_ready, 8 * hp + (n + 1))
                    nc.scalar.activation(probs[:, b, 0:nk], scores(b)[:, 0:nk], ACT.Exp,
                                         bias=fneg[:, b:b + 1], scale=0.125,
                                         accum_out=fsum[:, n % 4:n % 4 + 1]).then_inc(probs_ready, 1)
            for k in range(4):
                split_value(12 + k, k % 2, uh[:, k, META:L], c0=META)

            with act.Fori(Q_OUT, Q_FF) as q:
                for s in range(4):
                    split_ahead(q, s)
            take_root(1, eps, META)
            for k in range(KT):
                split_value(16 + k, k % 2, uh[:, k, META:L], c0=META)
            with act.Fori(0, 11) as r:
                for s in range(4):
                    split_ahead(r + Q_FF, s)
                    if s % 2 == 0:
                        nc.scalar.activation(seq(ea[:, s // 2, :]), acc(0, SEQ), ACT.Sigmoid).then_inc(sig_ready, 1)
                    else:
                        j = s // 2
                        split_value(2 * r + (24 + j), j, tile(gh, 2 * r + j), c0=META)
            with act.Fori(Q_DOWN, Q_B2) as q:
                for s in range(4):
                    split_ahead(q, s)
            take_root(2, eps, META)

            with act.Fori(0, 2) as lay:
                quad0 = lay * Q_LAYER + Q_B2
                v0, i0 = 32 * lay + 46, 40 * lay + 46
                squares(8 * lay + 8, 4 * lay)
                take_root(6 * lay + 3, eps)
                for k in range(KT):
                    split_value(i0 + k, k % 2, uh[:, k, :], v0 + k)
                with act.Fori(0, HEADS) as hd:
                    quad = 4 * hd + quad0
                    it = 4 * lay + hd
                    for s in range(4):
                        split_ahead(quad, s)
                        act.wait_ge(ret_used, 8 * it + (s + 1))
                        nc.scalar.activation(full(kq[:, s, :]), acc(s % 2), ACT.Identity,
                                             bias=bias(quad, s)).then_inc(acc_free[s % 2], 1)
                    for s in range(4):
                        split_ahead(quad + 1, s)
                        if s >= 2:
                            act.wait_ge(vt_psum, 4 * it + (s - 1))
                        nc.scalar.activation(full(vraw[:, s % 2, :]), acc(s % 2), ACT.Identity,
                                             bias=bias(quad + 1, s)).then_inc(acc_free[s % 2], 1)
                    for s in range(4):
                        split_ahead(quad + 2, s)
                        nc.scalar.activation(full(zg[s]), acc(s % 2), ACT.Sigmoid,
                                             bias=bias(quad + 2, s)).then_inc(sig_ready, 1)
                        if s == 1:
                            act.wait_ge(v_centred, it + 1)
                            nc.scalar.activation(rvh[0:META, 0, :], rvn[0:META, 0, :], ACT.Copy)
                            nc.scalar.activation(rvh[:, 1:4, :], rvn[:, 1:4, :], ACT.Copy).then_inc(vh_ready, 1)
                            for t, (ka, kb) in enumerate(KEYS[:4]):
                                act.wait_ge(sd_ready, 5 * it + (t + 1))
                                part = (slice(0, kb - ka), t, slice(ka, L))
                                nc.scalar.activation(sdh[part], sd[part], ACT.Copy).then_inc(sh_ready, 1)
                    for s in range(4):
                        split_value(i0 + 4 * hd + (8 + s), s % 2, rh[:, s, :], v0 + 4 * hd + (8 + s))
                        dst = sq[:, s % 2, :] if s else ssum
                        nc.scalar.activation(dst[:, 0:META], om[:, s, :], ACT.Square)
                        nc.scalar.activation(dst[:, META:L], ps[:, 4 + s, :], ACT.Square).then_inc(osq_ready, 1)
                    for s in range(4):
                        act.wait_ge(half_done, 4 * it + (s + 1))
                        act.wait_ge(ret_used, 8 * it + (2 * s + 1))
                        nc.scalar.activation(full(kq[:, 2 * s % 4, :]), acc(0), ACT.Copy).then_inc(acc_free[0], 1)
                        act.drain().then_inc(ret_ready, 1)
                        split_ahead(quad + 3, s)
                        act.wait_ge(ret_used, 8 * it + (2 * s + 2))
                        nc.scalar.activation(full(kq[:, 2 * s % 4 + 1, :]), acc(1), ACT.Copy).then_inc(acc_free[1], 1)
                        act.drain().then_inc(ret_ready, 1)
                        if s == 0:
                            take_root(6 * lay + hd + 4, gn_eps)
                with act.Fori(0, KT) as j:
                    quad = quad0 + Q_CONV + j
                    for s in range(4):
                        split_ahead(quad, s)
                        if s == 0:
                            nc.scalar.activation(full(eh[:]), acc(0), ACT.Identity,
                                                 bias=bias(quad, 0)).then_inc(acc_free[0], 1)
                        if s == 3:
                            nc.scalar.activation(full(ea[:, 1, :]), acc(1), ACT.Sigmoid,
                                                 bias=bias(quad, 3)).then_inc(sig_ready, 1)
                            split_value(i0 + 24 + j, 0, tile(ch, j), v0 + 24 + j)
                with act.Fori(0, 2) as r:
                    quad = quad0 + Q_MERGE + 3 * r
                    for n in range(12):
                        t, m = n // 3, n % 3
                        split_ahead(quad + n // 4, n % 4)
                        if m == 0:
                            act.wait_ge(y_ready, 8 * lay + 4 * r + (t + 1))
                        dst = (ya, g1, g2)[m][:, t % 2, :]
                        if m == 0:
                            nc.scalar.activation(full(dst), acc(n % 2), ACT.Copy).then_inc(acc_free[n % 2], 1)
                        else:
                            nc.scalar.activation(full(dst), acc(n % 2), ACT.Sigmoid,
                                                 bias=bias(quad + n // 4, n % 4)).then_inc(acc_free[n % 2], 1)
                for k in range(KT):
                    act.wait_ge(y_ready, 8 * lay + (k + 3))
                    nc.scalar.activation(uh[:, k, :], y[:, k, :], ACT.Copy).then_inc(valhi_ready, 1)
                with act.Fori(0, 2) as r:
                    for s in range(4):
                        split_ahead(quad0 + Q_WO + r, s)
                        if s == 0:
                            act.wait_ge(vallo_ready, i0 + 40)
                        nc.scalar.activation(full(tile(y, 4 * r + s)), acc(s % 2), ACT.Copy)\
                            .then_inc(acc_free[s % 2], 1)
                take_root(6 * lay + 8, eps)

        @block.vector
        def _(dve):
            v = nc.vector

            def low_part(index, slot, dst, hi, c0=0):
                dve.wait_ge(valhi_ready, index + 1)
                v.tensor_tensor(dst, val[:, slot, c0:L], hi.bitcast(F32), ALU.subtract).then_inc(vallo_ready, 1)
                dve.drain()

            def inv_rms(nth, c0=0):
                dve.wait_ge(root_ready, nth + 2)
                v.reciprocal(rstd[:, c0:L], rstd[:, c0:L])
                dve.drain()

            def add_square(t, c0=0):
                t = t[:, c0:L]
                v.tensor_tensor(sq[:, 0, c0:L], t, t, ALU.mult)
                dve.drain()
                v.tensor_tensor(ssum[:, c0:L], ssum[:, c0:L], sq[:, 0, c0:L], ALU.add)

            def apply_norm(index, nth, src, wcol, c0):
                inv_rms(nth, c0)
                for k in range(KT + 1):
                    if k < KT:
                        v.scalar_tensor_tensor(val[:, k % 2, c0:L], src[:, k, c0:L], wcol(k), rstd[:, c0:L],
                                               ALU.mult, ALU.mult).then_inc(val_ready, 1)
                    if k >= 1:
                        low_part(index + (k - 1), (k - 1) % 2, ul[:, k - 1, c0:L], uh[:, k - 1, c0:L], c0)

            dve.wait_ge(small_loaded, 16 * 5)
            v.tensor_tensor(lbt[:, 0, :], vec[:, V_LB:V_LB + 4], vec[:, V_LB:V_LB + 4], ALU.subtract).then_inc(lb_in, 1)
            dve.wait_ge(wff_hi, 1)
            v.tensor_tensor(wffl[:], wff_raw, wffh[:].bitcast(F32), ALU.subtract).then_inc(wff_lo, 1)
            apply_norm(0, 0, h, lambda k: col(V_MIX + k), 0)
            dve.wait_ge(ff_ln, 1)
            v.scalar_tensor_tensor(cz, cz, 0.0, ct, ALU.min, ALU.subtract)
            dve.wait_ge(consts_set, 2)
            dve.drain()
            v.tensor_tensor_scan(ccum, cone, cz, 0.0, ALU.mult, ALU.add)
            dve.drain()
            for n, (left, rest) in enumerate(((ccum, cres), (cres, cz), (cz, None))):
                v.tensor_copy(cparts[32 * n:32 * n + 8, :], left)
                v.tensor_copy(cparts0[n][:], left)
                dve.drain()
                if rest is not None:
                    v.tensor_tensor(rest, left, cparts0[n][:], ALU.subtract)
                    dve.drain()
            dve.drain().then_inc(cum_ready, 1)
            dve.wait_ge(lb_exp, 1)
            v.reciprocal(lbt[:, 2, :], lbt[:, 1, :])
            dve.drain()
            v.tensor_tensor(lbt[:, 3, :], lbt[:, 1, :], lbt[:, 2, :], ALU.mult)
            dve.drain()
            v.tensor_tensor(lbt[:, 4, :], lbt[:, 3, :], lbt[:, 3, :], ALU.subtract)
            dve.drain()
            v.memset(lb1[:, HEADS:HEADS + 1], 0.0)
            v.tensor_scalar(lb1[:, 0:HEADS], lbt[:, 4, :], -1.0, 1.0, ALU.mult, ALU.add)
            dve.drain()
            dve.wait_ge(masks_loaded, 16)
            def head_start(hd):
                qh, kin = tile(proj, hd + 12), tile(proj, hd + 16)
                dve.wait_ge(hg_sig, hd + 1)
                v.tensor_scalar(kin, gl[:], lb1[:, bass.ds(hd, 1)], None, ALU.mult)
                dve.drain()
                v.tensor_scalar(gl[:], kin, -1.0, 1.0, ALU.mult, ALU.add)
                dve.drain()
                v.tensor_scalar(gl[:], gl[:], F_MIN, None, ALU.max).then_inc(hg_f, 1)
                v.tensor_copy(vt[:], tile(proj, hd + 20)).then_inc(hg_vt, 1)
                v.scalar_tensor_tensor(qh, qh, float(P) ** -0.5, sgq[:], ALU.mult, ALU.mult)
                dve.drain()
                v.tensor_copy(sgq[:], kin)

            head_start(0)
            with dve.Fori(0, HEADS) as hd:
                lev = (LEVELS + 1) * hd
                qh, kin = tile(proj, hd + 12), tile(proj, hd + 16)
                v.memset(amat[:], 0.0)
                dve.wait_ge(hg_g, hd + 1)
                v.tensor_tensor_scan(pm[:], ones[:, 0:META], gl[:, 0:META], 0.0, ALU.mult, ALU.add)
                dve.drain()
                v.tensor_tensor(em[:], pm[:, META - 1:META].broadcast_to([P, META]), pm[:],
                                ALU.subtract).then_inc(hg_min, 1)

                def exponents(l):
                    b = l % 2
                    if l == 0:
                        v.tensor_tensor(eq[:, b, :], gl[:, META:L], odd[:], ALU.mult)
                        dve.drain()
                        v.tensor_scalar(ek[:, b, :], eq[:, b, :], -1.0, None, ALU.mult).then_inc(hg_exp_in, 1)
                        return
                    v.tensor_tensor_scan(eq[:, b, :], resets[:, l - 1, :], gl[:, META:L], 0.0, ALU.mult, ALU.add)
                    dve.drain()
                    w = 2 ** l
                    e3 = eq[:, b, :].rearrange("p (n b) -> p n b", b=w)
                    v.tensor_tensor(ek[:, b, :].rearrange("p (n b) -> p n b", b=w),
                                    e3[:, :, w - 1:w].broadcast_to([P, SEQ // w, w]), e3,
                                    ALU.subtract).then_inc(hg_exp_in, 1)

                exponents(0)
                dve.wait_ge(hg_mout, hd + 1)
                v.tensor_tensor(km[:], kin[:, 0:META], em[:], ALU.mult).then_inc(hg_km, 1)
                dve.wait_ge(hg_vpsum, hd + 1)
                v.tensor_copy(vn[:, 1:5, :], ps[:, 4, :].rearrange("p (a b) -> p a b", a=4))
                v.tensor_copy(vn[0:META, 0, :], ps[0:META, 5, 0:P]).then_inc(hg_vn, 1)
                for l in range(LEVELS + 2):
                    b = l % 2
                    if l <= LEVELS:
                        if l < LEVELS:
                            if l >= 1:
                                dve.drain()
                                dve.wait_ge(hg_kl, lev + l)
                            exponents(l + 1)
                        dve.wait_ge(hg_exp_out, lev + (l + 1))
                        if l >= 2:
                            dve.wait_ge(hg_s, LEVELS * hd + (l - 1))
                        v.tensor_tensor(ql[:, b, :], qh[:, META:L], eq[:, b, :], ALU.mult).then_inc(hg_q, 1)
                    if 1 <= l <= LEVELS:
                        m = l - 1
                        dve.drain()
                        dve.wait_ge(hg_s, LEVELS * hd + l)
                        v.memset(carrier[:, m:m + 1], 0.0)
                        v.copy_predicated(amat.rearrange("p (a b) -> p a b", a=XT),
                                          masks[:, m:m + 1, :].broadcast_to([P, XT, P]),
                                          ps[:, 6 + m % 2, :].rearrange("p (a b) -> p a b", a=XT)).then_inc(hg_pred, 1)
                dve.wait_ge(hg_kpsum, hd + 1)
                v.tensor_copy(kn[:, 1:4, :], ps[:, 4, 0:3 * P].rearrange("p (a b) -> p a b", a=3))
                v.tensor_copy(kn[0:META, 0, :], ps[0:META, 5, 0:P]).then_inc(hg_kn, 1)
                dve.wait_ge(hg_upsum, hd + 1)
                v.tensor_copy(st[:, 0, :], ps[:, 4, 0:P])
                for i in range(1, XT):
                    dve.drain()
                    step = v.scalar_tensor_tensor(st[:, i, :], st[:, i - 1, :],
                                                  eq[:, LEVELS % 2, P * i - 1:P * i],
                                                  ps[:, 4, P * i:P * i + P], ALU.mult, ALU.add)
                step.then_inc(hg_state, 1)
                dve.drain()
                dve.wait_ge(hg_gate, hd + 1)
                v.tensor_tensor(ea[:, 0, :], tile(proj, hd + 24), ea[:, 0, :], ALU.mult)
                head_start(hd + 1)
                dve.wait_ge(hg_root, hd + 1)
                v.reciprocal(rstd[:, 0:SEQ], rstd[:, 0:SEQ])
                dve.drain()
                v.scalar_tensor_tensor(ot, ps[:, 6, :], col(V_HNORM), rstd[:, 0:SEQ], ALU.mult, ALU.mult)
                dve.drain()
                v.tensor_tensor(tile(proj, hd + 24)[:, META:L], ot, ea[:, 0, META:L], ALU.mult).then_inc(val_ready, 1)
                dve.drain().then_inc(hg_inv, 1)
            dve.wait_ge(fox_loaded, 48)
            for n, part in enumerate(staged_sel):
                v.tensor_copy(sel[:, 4 * n:4 * n + 4, :], part.rearrange("p (a b) -> p a b", b=P))
            v.tensor_copy(causal[:], sq[:, 1, 0:P])
            v.tensor_copy(identb[:], ident[:])
            dve.drain()

            for j in range(4):
                dve.wait_ge(fv_psum, j + 1)
                v.tensor_copy(vnat[:, 1:5, P * j:P * j + P], ps[:, 4, :].rearrange("p (a b) -> p a b", a=4))
                v.tensor_copy(vnat[0:META, 0, P * j:P * j + P], ps[0:META, 5, 0:P]).then_inc(fv_ready, 1)
            dve.drain()

            def fox_step(hp, n, first=False):
                if n == 0:
                    v.tensor_copy(qs[:], tile(proj, hp))
                    v.tensor_copy(ks[:], tile(proj, hp + 4))
                    v.tensor_copy(selp[:], sel[:, bass.ds(2 * hp, 2), :]).then_inc(fox_in, 1)
                if n < 8:
                    b, i = n % 2, n % 4
                    nk = KEYS[i + 1][1]
                    dve.wait_ge(scores_ready, 8 * hp + (n + 1))
                    v.tensor_reduce(fmax[:, b:b + 1], scores(b)[:, 0:nk], AX.X, ALU.max)
                    dve.drain()
                    dve.wait_ge(probs_ready, 8 * hp + (n + 1))
                    v.tensor_scalar(fneg[:, b:b + 1], fmax[:, b:b + 1], -0.125, None, ALU.mult)\
                        .then_inc(negmax_ready, 1)
                if (n >= 2 or not first) and n < 10:
                    m = n - 2
                    b, i = m % 2, m % 4
                    dve.wait_ge(probsT_psum, 8 * hp + (m + 3))
                    v.tensor_copy(pT[0:META, b, 0, :], ps[0:META, 5, 0:P])
                    v.tensor_copy(pT[:, b, 1:i + 2, :], ps[:, 4, 0:P * (i + 1)].rearrange(
                        "p (a b) -> p a b", b=P)).then_inc(probsT_ready, 1)
                if n >= 3 or not first:
                    m = n - 3
                    b, i, e, c = m % 2, m % 4, m % 8 // 4, m % 4
                    dve.wait_ge(probs_ready, 8 * hp + (m + 3))
                    v.reciprocal(finv[:, c:c + 1], fsum[:, c:c + 1])
                    dve.drain()
                    dve.wait_ge(heads_psum, 8 * hp + (m + 1))
                    v.tensor_scalar(onat[:, i, bass.ds(P * hp + (P * (m // 8) + 64 * e), 64)], ps[:, 6 + b, 0:64],
                                    finv[:, c:c + 1], None, ALU.mult).then_inc(heads_ready, 1)

            for n in range(8):
                fox_step(0, n, first=True)
            with dve.Fori(1, 4) as hp:
                for n in range(8):
                    fox_step(hp, n)
            for n in range(8, 11):
                fox_step(3, n)
            for k in range(HEADS):
                dve.wait_ge(valhi_ready, 9 + k)
                v.tensor_tensor(ul[:, 4 + k, META:L], proj[:, 24 + k, META:L],
                                uh[:, 4 + k, META:L].bitcast(F32), ALU.subtract).then_inc(vallo_ready, 1)
            for k in range(4):
                dve.wait_ge(headsT_psum, k + 1)
                v.tensor_copy(val[:, k % 2, META:L], ps[:, k, :]).then_inc(val_ready, 1)
                low_part(12 + k, k % 2, ul[:, k, META:L], uh[:, k, META:L], META)

            v.memset(ssum[:], 0.0)
            with dve.Fori(0, 2) as r:
                for s in range(4):
                    dve.wait_ge(panel_done, 4 * r + (4 * Q_OUT + s + 1))
                    t = seq(tile(h, 4 * r + s))
                    v.tensor_tensor(t, acc(s % 2, SEQ), t, ALU.add).then_inc(acc_free[s % 2], 1)
                    dve.drain()
                    add_square(tile(h, 4 * r + s), c0=META)
            dve.drain().then_inc(ssum_ready, 1)
            apply_norm(16, 1, h, lambda k: col(V_FFN + k), META)
            with dve.Fori(0, 11) as r:
                for s in range(4):
                    j = s // 2
                    if s % 2 == 0:
                        dve.wait_ge(sig_ready, 2 * r + (j + 1))
                        v.tensor_tensor(seq(gs[:]), acc(0, SEQ), seq(ea[:, j, :]), ALU.mult).then_inc(acc_free[0], 1)
                        dve.drain()
                    else:
                        dve.wait_ge(panel_done, 4 * r + (4 * Q_FF + s + 1))
                        v.tensor_tensor(seq(val[:, j, :]), acc(1, SEQ), seq(gs[:]), ALU.mult).then_inc(acc_free[1], 1)
                        dve.drain().then_inc(val_ready, 1)
                        low_part(2 * r + (24 + j), j, tile(gl_, 2 * r + j), tile(gh, 2 * r + j), META)
            v.memset(ssum[:], 0.0)
            with dve.Fori(0, 2) as r:
                for t in range(4):
                    dve.wait_ge(panel_done, 12 * r + (4 * Q_DOWN + 3 * t + 3))
                    x = seq(tile(h, 4 * r + t))
                    v.tensor_tensor(x, acc(t % 2, SEQ), x, ALU.add).then_inc(acc_free[t % 2], 1)
                    dve.drain()
                    add_square(tile(h, 4 * r + t), c0=META)
            v.tensor_copy(h[:, :, 0:META], meta2[:])
            dve.drain().then_inc(ssum_ready, 1)
            inv_rms(2, META)
            for k in range(KT):
                v.scalar_tensor_tensor(h[:, k, META:L], h[:, k, META:L], col(V_FINAL + k), rstd[:, META:L],
                                       ALU.mult, ALU.mult).then_inc((h_even, h_odd)[k % 2], 1)

            with dve.Fori(0, 2) as lay:
                quad0 = lay * Q_LAYER + Q_B2
                i0 = 40 * lay + 46
                apply_norm(i0, 6 * lay + 3, h, lambda k: col(8 * lay + (V_PRE + k)), 0)
                v.memset(y[:], 0.0)
                dve.wait_ge(tables_loaded, 64)
                with dve.Fori(0, HEADS) as hd:
                    quad = 4 * hd + quad0
                    it = 4 * lay + hd
                    a0 = A_LAYER * lay + A_HEAD * hd + A_B2
                    for n, dst in enumerate((kr, qr)):
                        dve.wait_ge(acc_free[0], a0 + (n + 2))
                        dve.wait_ge(acc_free[1], a0 + (n + 2))
                        x1, x2 = kq[:, 2 * n, :], kq[:, 2 * n + 1, :]
                        v.tensor_tensor(r1[:], x1, cos[:], ALU.mult)
                        v.tensor_tensor(r2[:], x2, sin[:], ALU.mult)
                        dve.drain()
                        v.tensor_tensor(dst[:, 0, :], r1[:], r2[:], ALU.subtract)
                        dve.drain()
                        v.tensor_tensor(r1[:], x1, sin[:], ALU.mult)
                        v.tensor_tensor(r2[:], x2, cos[:], ALU.mult)
                        dve.drain()
                        v.tensor_tensor(dst[:, 1, :], r1[:], r2[:], ALU.add).then_inc(rope_ready, 1)
                        dve.drain()
                    def silu(s):
                        dve.wait_ge(sig_ready, 24 * lay + 4 * hd + (22 + s + 1))
                        v.scalar_tensor_tensor(full(zg[s]), acc(s % 2), bias(quad + 2, s), full(zg[s]),
                                               ALU.add, ALU.mult).then_inc(acc_free[s % 2], 1)

                    for j in range(4):
                        dve.wait_ge(vt_psum, 4 * it + (j + 1))
                        v.tensor_copy(rvn[:, 1:5, P * j:P * j + P], ps[:, 4, :].rearrange("p (a b) -> p a b", a=4))
                        v.tensor_copy(rvn[0:META, 0, P * j:P * j + P], ps[0:META, 5, 0:P]).then_inc(vn_ready, 1)
                    dve.drain()
                    v.tensor_reduce(vmean[:, 1:5], rvn[:, 1:5, :], AX.X, ALU.add)
                    v.tensor_reduce(vmean[0:META, 0:1], rvn[0:META, 0, :], AX.X, ALU.add)
                    dve.drain()
                    v.tensor_scalar(vneg[:, 1:5], vmean[:, 1:5], -1.0 / (4 * P), None, ALU.mult)
                    v.tensor_scalar(vneg[0:META, 0:1], vmean[0:META, 0:1], -1.0 / (4 * P), None, ALU.mult)
                    dve.drain()
                    v.tensor_scalar(rvn[0:META, 0, :], rvn[0:META, 0, :], vneg[0:META, 0:1], None, ALU.add)
                    for i in range(1, 5):
                        last = v.tensor_scalar(rvn[:, i, :], rvn[:, i, :], vneg[:, i:i + 1], None, ALU.add)
                    last.then_inc(v_centred, 1)
                    silu(0)
                    silu(1)
                    dve.wait_ge(s_psum, 5 * it + 1)
                    dm = decm[:, bass.ds(hd, 1), :].rearrange("p a b -> p (a b)")
                    v.tensor_tensor(sd[0:META, 0, META:L], ps[0:META, 6, :], dm[:, META:L], ALU.mult)
                    v.tensor_tensor(sd[0:META, 0, 0:META], ps[0:META, 7, 0:META], dm[:, 0:META],
                                    ALU.mult).then_inc(sd_ready, 1)
                    for i in range(XT):
                        w = SEQ - P * i
                        dx = decx[:, bass.ds(hd, 1), :].rearrange("p a b -> p (a b)")
                        dve.wait_ge(s_psum, 5 * it + (i + 2))
                        v.tensor_tensor(sd[:, i + 1, META + P * i:L], ps[:, 4 + i % 2, 0:w], dx[:, 0:w],
                                        ALU.mult).then_inc(sd_ready, 1)
                    dve.drain()
                    dve.wait_ge(vh_ready, it + 1)
                    v.tensor_tensor(rvl[0:META, 0, :], rvn[0:META, 0, :], rvh[0:META, 0, :].bitcast(F32), ALU.subtract)
                    v.tensor_tensor(rvl[:, 1:4, :], rvn[:, 1:4, :], rvh[:, 1:4, :].bitcast(F32), ALU.subtract)
                    for t, (ka, kb) in enumerate(KEYS[:4]):
                        dve.wait_ge(sh_ready, 4 * it + (t + 1))
                        part = (slice(0, kb - ka), t, slice(ka, L))
                        v.tensor_tensor(sdl[part], sd[part], sdh[part].bitcast(F32), ALU.subtract)
                    dve.drain().then_inc(parts_ready, 1)
                    silu(2)
                    silu(3)
                    dve.wait_ge(o_psum_m, it + 1)
                    v.tensor_copy(om[:], ps[:, 7, 0:4 * META].rearrange("p (a b) -> p a b", a=4))\
                        .then_inc(om_ready, 1)
                    def add_tile(j):
                        dve.wait_ge(osq_ready, 4 * it + (j + 1))
                        v.tensor_tensor(ssum[:], ssum[:], sq[:, j % 2, :], ALU.add)

                    dve.drain()
                    for j in range(4):
                        gain = col(16 * lay + 4 * hd + (V_GN + j))
                        v.scalar_tensor_tensor(val[:, j % 2, 0:META], om[:, j, :], gain, zg[j][:, 0:META],
                                               ALU.mult, ALU.mult)
                        dve.wait_ge(o_psum, 4 * it + (j + 1))
                        out = ps[:, 4 + j, :]
                        v.scalar_tensor_tensor(val[:, j % 2, META:L], out, gain, zg[j][:, META:L],
                                               ALU.mult, ALU.mult).then_inc(val_ready, 1)
                        if j >= 2:
                            add_tile(j - 1)
                        low_part(i0 + 4 * hd + (8 + j), j % 2, rl[:, j, :], rh[:, j, :])
                    add_tile(3)
                    dve.drain().then_inc(ssum_ready, 1)
                    inv_rms(6 * lay + hd + 4)
                    for s in range(8):
                        dve.wait_ge(ret_ready, 8 * it + (s + 1))
                        v.tensor_tensor(kq[:, s % 4, :], kq[:, s % 4, :], rstd[:], ALU.mult)
                        dve.drain()
                        v.tensor_tensor(y[:, s, :], y[:, s, :], kq[:, s % 4, :], ALU.add).then_inc(ret_used, 1)
                with dve.Fori(0, KT) as j:
                    quad = quad0 + Q_CONV + j
                    a0 = A_LAYER * lay + 2 * j + (A_B2 + A_CONV)
                    dve.wait_ge(acc_free[0], a0 + 2)
                    dve.wait_ge(panel_done, 4 * quad + 2)
                    v.memset(cu[:, 0:2], 0.0)
                    v.scalar_tensor_tensor(full(cu[:, 2:L + 2]), acc(1), bias(quad, 1), full(eh[:]),
                                           ALU.add, ALU.mult).then_inc(acc_free[1], 1)
                    dve.drain()
                    cw = 24 * lay + j + V_CW
                    v.tensor_scalar(c0[:], cu[:, 2:L + 2], col(cw + 16), col(8 * lay + j + V_CB), ALU.mult, ALU.add)
                    dve.drain()
                    v.scalar_tensor_tensor(c1[:], cu[:, 1:L + 1], col(cw + 8), c0[:], ALU.mult, ALU.add)
                    dve.drain()
                    v.scalar_tensor_tensor(c2[:], cu[:, 0:L], col(cw), c1[:], ALU.mult, ALU.add)
                    dve.drain()
                    dve.wait_ge(panel_done, 4 * quad + 3)
                    v.scalar_tensor_tensor(full(cb_[:]), acc(0), bias(quad, 2), full(c2[:]),
                                           ALU.add, ALU.mult).then_inc(acc_free[0], 1)
                    dve.wait_ge(sig_ready, 24 * lay + j + (22 + 16 + 1))
                    v.scalar_tensor_tensor(full(cs[:]), acc(1), bias(quad, 3), full(ea[:, 1, :]),
                                           ALU.add, ALU.mult).then_inc(acc_free[1], 1)
                    dve.drain()
                    v.tensor_tensor(val[:, 0, :], cs[:], cb_[:], ALU.mult).then_inc(val_ready, 1)
                    low_part(i0 + 24 + j, 0, tile(cl, j), tile(ch, j))
                with dve.Fori(0, 2) as r:
                    a0 = A_LAYER * lay + 6 * r + (A_B2 + A_MERGE)
                    for t in range(4):
                        for n in range(3 * t + 1, 3 * t + 3):
                            dve.wait_ge(acc_free[n % 2], a0 + (n // 2 + 2))
                        yt = tile(y, 4 * r + t)
                        v.tensor_tensor(m1[:], ya[:, t % 2, :], g1[:, t % 2, :], ALU.mult)
                        v.tensor_tensor(m2[:], yt, g2[:, t % 2, :], ALU.mult)
                        dve.drain()
                        v.tensor_tensor(yt, m1[:], m2[:], ALU.add).then_inc(y_ready, 1)
                        dve.drain()
                for k in range(KT):
                    dve.wait_ge(valhi_ready, i0 + (33 + k))
                    v.tensor_tensor(ul[:, k, :], y[:, k, :], uh[:, k, :].bitcast(F32), ALU.subtract)\
                        .then_inc(vallo_ready, 1)
                v.memset(ssum[:], 0.0)
                with dve.Fori(0, 2) as r:
                    for s in range(4):
                        dve.wait_ge(acc_free[s % 2], A_LAYER * lay + 2 * r + (A_B2 + A_WO + s // 2 + 2))
                        add_square(tile(y, 4 * r + s))
                        v.tensor_scalar(tile(y, 4 * r + s), tile(y, 4 * r + s), col(8 * lay + (V_POST + s) + 4 * r),
                                        None, ALU.mult)
                        dve.drain()
                dve.drain().then_inc(ssum_ready, 1)
                inv_rms(6 * lay + 8)
                for k in range(KT + 1):
                    if k < KT:
                        step = v.tensor_tensor(y[:, k, :], y[:, k, :], rstd[:], ALU.mult)
                        if k % 2:
                            step.then_inc(post_ready, 1)
                    if k % 2:
                        dve.drain()
                        v.tensor_tensor(h[:, k - 1, :], h[:, k - 1, :], y[:, k - 1, :], ALU.add).then_inc(h_even, 1)
                dve.drain()

        @block.tensor
        def _(pe):
            mm = nc.tensor.matmul

            for s in acc_free:
                pe.sem_inc(s, 1)
            pe.sem_inc(sq_free, 2)
            pe.sem_inc(root_ready, 1)
            pe.sem_inc(probsT_psum, 2)
            pe.sem_inc(heads_ready, 4)
            pe.sem_inc(probs_ready, 2)
            pe.sem_inc(hg_inv, 1)
            pe.sem_inc(y_ready, 2)
            pe.sem_inc(ret_used, 4)

            def product(slot, wslot, xh, xl, k0, k1, rows0, first, last, n, ready=None):
                half = n // 2
                c = L - n
                for k in range(k0, k1):
                    if ready is not None and k - k0 < ready[1]:
                        pe.wait_ge(vallo_ready, ready[0] + (k - k0 + 1))
                    wcol = slice(P * k, P * k + P)
                    for w, x, part in ((wh, xh, 0), (wh, xl, 1), (wl, xh, 2)):
                        for a in range(2):
                            out = mm(ps[:, 2 * slot + a, 0:half], w[:, wslot, wcol],
                                     x(rows0 + k - k0, c + a * half, c + (a + 1) * half),
                                     start=first and k == k0 and part == 0,
                                     stop=last and k == k1 - 1 and part == 2)
                return out

            def xu(t, off=0):
                return lambda k, a, b: t[:, k, a - off:b - off]

            def use_panel(quad, s, a, xh=xu(uh), xl=xu(ul), n=L, ready=None):
                pe.wait_ge(lo_ready, 4 * quad + (s + 1))
                pe.wait_ge(acc_free[s % 2], a + 1)
                product(s % 2, s % 2, xh, xl, 0, KT, 0, True, True, n, ready).then_inc(panel_done, 1)

            def sum_squares(first, nth):
                pe.wait_ge(root_ready, nth + 1)
                half = L // 2
                for k in range(KT):
                    pe.wait_ge(sq_ready, first + (k + 1))
                    for a in range(2):
                        out = mm(ps[:, 4 + a, 0:half], mean_d[:], sq[:, k % 2, a * half:(a + 1) * half],
                                 start=k == 0, stop=k == KT - 1)
                    out.then_inc(sq_free, 1)
                pe.drain().then_inc(meansq_ready, 1)

            def mean_square(sums, nth, weight, n=L):
                pe.wait_ge(root_ready, nth + 1)
                pe.wait_ge(ssum_ready, sums + 1)
                half, c = n // 2, L - n
                for a in range(2):
                    out = mm(ps[:, 4 + a, 0:half], weight[:], ssum[:, c + a * half:c + (a + 1) * half],
                             start=True, stop=True)
                out.then_inc(meansq_ready, 1)

            def transposes(src, done, blocks=KEYS):
                for n, (a, b) in enumerate(blocks):
                    dst = ps[0:b - a, 5, 0:P] if b - a == META else ps[:, 4, P * (n - 1):P * n]
                    out = nc.tensor.transpose(dst, src[:, a:b], ident[:])
                out.then_inc(done, 1)

            pe.wait_ge(consts_set, 1)
            sum_squares(0, 0)
            pe.wait_ge(consts_set, 2)
            pe.wait_ge(small_loaded, 16 * 5)
            pe.wait_ge(wff_lo, 1)
            pe.wait_ge(root_ready, 2)
            for k in range(KT):
                pe.wait_ge(vallo_ready, k + 1)
                for w, x, part in ((wffh, uh, 0), (wffh, ul, 1), (wffl, uh, 2)):
                    for a in range(2):
                        out = mm(ps[0:8, 4 + a, 0:L // 2], w[:, 8 * k:8 * k + 8], x[:, k, a * (L // 2):(a + 1) * (L // 2)],
                                 start=k == 0 and part == 0, stop=k == KT - 1 and part == 2)
            out.then_inc(ff_psum, 1)
            with pe.Fori(0, 3) as q:
                for s in range(4):
                    use_panel(q, s, 2 * q + s // 2)
            pe.wait_ge(ff_ln, 1)
            with pe.Fori(0, HEADS) as hd:
                last = LEVELS % 2


                def level_scores(l):
                    b = l % 2
                    pe.wait_ge(hg_kl, (LEVELS + 1) * hd + (l + 1))
                    pe.wait_ge(hg_q, (LEVELS + 1) * hd + (l + 1))
                    if l >= 2:
                        pe.wait_ge(hg_pred, LEVELS * hd + (l - 1))
                    for i in range(XT):
                        out = mm(ps[:, 6 + b, P * i:P * i + P], kl[:, b, P * i:P * i + P],
                                 ql[:, b, P * i:P * i + P], start=True, stop=True)
                    out.then_inc(hg_s, 1)

                pe.wait_ge(hg_vt, hd + 1)
                transposes(vt[:], hg_vpsum)
                for s in range(3):
                    use_panel(hd + 3, s, 2 * hd + (6 + s // 2))
                    if s == 0:
                        pe.wait_ge(hg_inv, hd + 1)
                    level_scores(2 * s)
                    level_scores(2 * s + 1)
                level_scores(LEVELS - 1)
                pe.wait_ge(hg_kl, (LEVELS + 1) * hd + (LEVELS + 1))
                pe.wait_ge(hg_km, hd + 1)
                pe.wait_ge(hg_vn, hd + 1)
                nc.tensor.transpose(ps[0:META, 5, 0:P], km[:], ident[:])
                for i in range(XT - 1):
                    out = nc.tensor.transpose(ps[:, 4, P * i:P * i + P], kl[:, last, P * i:P * i + P], ident[:])
                out.then_inc(hg_kpsum, 1)
                pe.wait_ge(lo_ready, 4 * hd + 16)
                pe.wait_ge(acc_free[1], 2 * hd + 8)
                product(1, 1, xu(uh), xu(ul), 0, 3, 0, True, False, L)
                pe.wait_ge(hg_kn, hd + 1)
                for i in range(XT):
                    rows = META if i == 0 else P
                    out = mm(ps[:, 4, P * i:P * i + P], kn[0:rows, i, :], vn[0:rows, i, :], start=True, stop=True)
                out.then_inc(hg_upsum, 1)
                product(1, 1, xu(uh), xu(ul), 3, KT, 3, False, True, L).then_inc(panel_done, 1)
                pe.wait_ge(hg_pred, LEVELS * hd + LEVELS)
                pe.wait_ge(hg_state, hd + 1)
                pe.wait_ge(hg_q, (LEVELS + 1) * hd + (LEVELS + 1))
                for i in range(XT):
                    dst = ps[:, 6, P * i:P * i + P]
                    mm(dst, vn[:, i + 1, :], amat[:, P * i:P * i + P], start=True, stop=False)
                    out = mm(dst, st[:, i, :], ql[:, last, P * i:P * i + P], start=False, stop=True)
                out.then_inc(hg_o, 1)
                pe.wait_ge(hg_sq, hd + 1)
                mm(ps[:, 7, :], mean_h[:], sq[:, 0, 0:SEQ], start=True, stop=True).then_inc(hg_ss, 1)

            pe.wait_ge(acc_free[1], A_OUT + 1)
            for j in range(4):
                if j:
                    pe.wait_ge(fv_ready, j)
                transposes(proj[:, 8 + j, :], fv_psum)
            pe.wait_ge(cum_ready, 1)
            pe.wait_ge(fv_ready, 4)
            pe.wait_ge(acc_free[0], A_OUT + 1)

            def fox_step(hp, n, first=False):
                if n < 8:
                    b, i, e = n % 2, n % 4, n // 4
                    q0, nk = KEYS[i + 1]
                    if n == 0:
                        pe.wait_ge(fox_in, hp + 1)
                    pe.wait_ge(probs_ready, 8 * hp + (n + 1))
                    for bank, (ka, kb) in enumerate(((0, min(nk, 272)), (272, nk))):
                        if ka >= kb:
                            continue
                        c = 240 if bank == 0 else 0
                        diag = ka <= q0 < kb
                        dst = ps[:, 2 * b + bank, c:c + kb - ka]
                        mm(dst, qs[64 * e:64 * e + 64, q0:nk], ks[64 * e:64 * e + 64, ka:kb], start=True, stop=False)
                        out = mm(dst, selp[:, e, :], cparts[:, ka:kb], start=False, stop=not diag)
                        if diag:
                            out = mm(ps[:, 2 * b + bank, c + q0 - ka:c + nk - ka], identb[:], causal[:],
                                     start=False, stop=True)
                    out.then_inc(scores_ready, 1)
                if (n >= 2 or not first) and n < 10:
                    m = n - 2
                    b, i = m % 2, m % 4
                    pe.wait_ge(probs_ready, 8 * hp + (m + 3))
                    if m != 0 or not first:
                        pe.wait_ge(probsT_ready, 8 * hp + m)
                    transposes(probs[:, b, :], probsT_psum, KEYS[:i + 2])
                if n >= 3 or not first:
                    m = n - 3
                    b, i, e = m % 2, m % 4, m % 8 // 4
                    pe.wait_ge(probsT_ready, 8 * hp + (m + 1))
                    pe.wait_ge(heads_ready, 8 * hp + (m + 3))
                    for t in (*range(1, i + 2), 0):
                        rows = META if t == 0 else P
                        out = mm(ps[:, 6 + b, 0:64], pT[0:rows, b, t, :],
                                 vnat[0:rows, t, bass.ds(P * hp + (P * (m // 8) + 64 * e), 64)],
                                 start=t == 1, stop=t == 0)
                    out.then_inc(heads_psum, 1)

            for n in range(8):
                fox_step(0, n, first=True)
            with pe.Fori(1, 4) as hp:
                for n in range(8):
                    fox_step(hp, n)
            for n in range(8, 11):
                fox_step(3, n)
            pe.wait_ge(heads_ready, 36)
            for k in range(4):
                for i in range(XT):
                    out = nc.tensor.transpose(ps[:, k, P * i:P * i + P], onat[:, i, P * k:P * k + P], ident[:])
                out.then_inc(headsT_psum, 1)

            pe.wait_ge(val_ready, 16)
            with pe.Fori(0, 2) as r:
                for s in range(4):
                    use_panel(r + Q_OUT, s, 2 * r + (A_OUT + s // 2), n=SEQ, ready=(12, 4) if s == 0 else None)
            mean_square(0, 1, mean_d, SEQ)
            with pe.Fori(0, 11) as r:
                for s in range(4):
                    use_panel(r + Q_FF, s, 2 * r + (A_FF + s // 2), n=SEQ, ready=(16, KT) if s == 0 else None)
            with pe.Fori(0, 2) as r:
                for n in range(12):
                    t, third = n // 3, n % 3
                    pe.wait_ge(lo_ready, 12 * r + (4 * Q_DOWN + n + 1))
                    if third == 0:
                        pe.wait_ge(acc_free[t % 2], 2 * r + (A_DOWN + t // 2 + 1))
                    product(t % 2, n % 2, xu(gh, META), xu(gl_, META), 0, KT if third < 2 else FT - 2 * KT,
                            KT * third, third == 0, third == 2, SEQ,
                            (24 + KT * third, KT) if t == 0 else None).then_inc(panel_done, 1)
            mean_square(1, 2, mean_d, SEQ)
            pe.wait_ge(consts_set, 3)

            with pe.Fori(0, 2) as lay:
                quad0 = lay * Q_LAYER + Q_B2
                i0 = 40 * lay + 46
                sum_squares(8 * lay + 8, 6 * lay + 3)
                with pe.Fori(0, HEADS) as hd:
                    quad = 4 * hd + quad0
                    it = 4 * lay + hd
                    a0 = A_LAYER * lay + A_HEAD * hd + A_B2
                    for s in range(4):
                        use_panel(quad, s, a0 + s // 2, ready=(i0, KT) if s == 0 else None)

                    def v_transposes(j):
                        pe.wait_ge(acc_free[j % 2], a0 + (2 + j // 2 + 2))
                        if j:
                            pe.wait_ge(vn_ready, 4 * it + j)
                        else:
                            pe.wait_ge(root_ready, 6 * lay + hd + 5)
                        transposes(vraw[:, j % 2, :], vt_psum)

                    for s in range(4):
                        use_panel(quad + 1, s, a0 + (2 + s // 2))
                        if s:
                            v_transposes(s - 1)
                    use_panel(quad + 2, 0, a0 + 4)
                    v_transposes(3)
                    use_panel(quad + 2, 1, a0 + 4)
                    pe.wait_ge(rope_ready, 2 * it + 2)
                    for j, (ka, kb) in enumerate(KEYS):
                        if j == 1:
                            pe.wait_ge(vn_ready, 4 * it + 4)
                        if j >= 3:
                            pe.wait_ge(sd_ready, 5 * it + (j - 1))
                        bank = 6 if j == 0 else 4 + (j - 1) % 2
                        qa = META if j == 0 else ka
                        for c in range(2):
                            out = mm(ps[0:kb - ka, bank, 0:L - qa], kr[:, c, ka:kb], qr[:, c, qa:L],
                                     start=c == 0, stop=c == 1)
                        if j == 0:
                            for c in range(2):
                                out = mm(ps[0:META, 7, 0:META], kr[:, c, 0:META], qr[:, c, 0:META],
                                         start=c == 0, stop=c == 1)
                        out.then_inc(s_psum, 1)
                    use_panel(quad + 2, 2, a0 + 5)
                    use_panel(quad + 2, 3, a0 + 5)
                    pe.wait_ge(parts_ready, it + 1)

                    def parts(t, rows, j, qa, qb):
                        w = slice(P * j, P * j + P)
                        return ((rvh[0:rows, t, w], sdh[0:rows, t, qa:qb]), (rvh[0:rows, t, w], sdl[0:rows, t, qa:qb]),
                                (rvl[0:rows, t, w], sdh[0:rows, t, qa:qb]))

                    for j in range(4):
                        for n, (a, b) in enumerate(parts(0, META, j, 0, META)):
                            out = mm(ps[:, 7, META * j:META * (j + 1)], a, b, start=n == 0, stop=n == 2)
                    out.then_inc(o_psum_m, 1)
                    for j in range(4):
                        if j == 3:
                            pe.wait_ge(om_ready, it + 1)
                        for t, (ka, kb) in enumerate(KEYS[:4]):
                            qa = max(ka, META)
                            for n, (a, b) in enumerate(parts(t, kb - ka, j, qa, L)):
                                mm(ps[:, 4 + j, qa - META:SEQ], a, b, start=t == 0 and n == 0, stop=False)
                        ka = KEYS[4][0]
                        mm(ps[:, 4 + j, ka - META:SEQ], rvn[:, 4, P * j:P * j + P], sd[:, 4, ka:L],
                           start=False, stop=True).then_inc(o_psum, 1)
                    for s in range(4):
                        pe.wait_ge(lo_ready, 4 * quad + (12 + s + 1))
                        pe.wait_ge(acc_free[0], a0 + (6 + s + 1))
                        if s == 0:
                            product(0, 0, xu(rh), xu(rl), 0, 3, 0, True, False, L, (i0 + 4 * hd + 8, 3))
                            pe.wait_ge(acc_free[1], a0 + 7)
                            product(1, 0, xu(rh), xu(rl), 4, 7, 0, True, False, L)
                            product(0, 0, xu(rh), xu(rl), 3, 4, 3, False, True, L,
                                    (i0 + 4 * hd + 11, 1)).then_inc(half_done, 1)
                            product(1, 0, xu(rh), xu(rl), 7, 8, 3, False, True, L).then_inc(panel_done, 1)
                        else:
                            product(0, s % 2, xu(rh), xu(rl), 0, 4, 0, True, True, L).then_inc(half_done, 1)
                            pe.wait_ge(acc_free[1], a0 + (6 + s + 1))
                            product(1, s % 2, xu(rh), xu(rl), 4, 8, 0, True, True, L).then_inc(panel_done, 1)
                        if s == 0:
                            mean_square(5 * lay + hd + 2, 6 * lay + hd + 4, mean_g)
                with pe.Fori(0, KT) as j:
                    for s in range(4):
                        use_panel(quad0 + Q_CONV + j, s, A_LAYER * lay + 2 * j + (A_B2 + A_CONV + s // 2))
                with pe.Fori(0, 2) as r:
                    for n in range(12):
                        a = A_LAYER * lay + 6 * r + (A_B2 + A_MERGE + n // 2)
                        x = (xu(ch), xu(cl)) if n % 3 == 0 else (xu(uh), xu(ul))
                        use_panel(quad0 + Q_MERGE + 3 * r + n // 4, n % 4, a, *x,
                                  ready=(i0 + 24, KT) if n == 0 else None)
                with pe.Fori(0, 2) as r:
                    for s in range(4):
                        use_panel(quad0 + Q_WO + r, s, A_LAYER * lay + 2 * r + (A_B2 + A_WO + s // 2),
                                  ready=(i0 + 32, KT) if s == 0 else None)
                mean_square(5 * lay + 6, 6 * lay + 8, mean_d)


def panels(w):
    import numpy as np
    k, n = w.shape
    out = np.zeros((n // P, P, KT, P), np.float32)
    out[:, :, :k // P] = w.reshape(k // P, P, n // P, P).transpose(2, 1, 0, 3)
    return out


def weight_stream(i):
    import numpy as np
    win, wd = i["w_in"][0], i["w_ffn_down"][0]
    parts = [panels(win[:, c:c + 512]) for c in (1544, 2056, 2568)]
    hg_, fq, fk, fv = (panels(win[:, c:c + 512]) for c in (3080, 0, 512, 1024))
    parts.append(np.stack([hg_, fq, fk, fv], 1).reshape(16, P, KT, P))
    parts.append(panels(i["w_out"][0]))
    gate, up = panels(i["w_ffn_gate"][0]), panels(i["w_ffn_up"][0])
    parts.append(np.stack([gate, up], 1).reshape(2 * FT, P, KT, P))
    down = [panels(wd[r:r + D]) for r in range(0, FF, D)]
    parts.append(np.stack(down, 1).reshape(3 * KT, P, KT, P))
    for l in range(2):
        w = i["w_in_2"][l]
        p = panels(w)
        wr = i["w_ret_out_2"][l]
        for hd in range(HEADS):
            parts += [p[40 + 2 * hd:42 + 2 * hd], p[32 + 2 * hd:34 + 2 * hd], p[48 + 4 * hd:52 + 4 * hd],
                      p[64 + 4 * hd:68 + 4 * hd]]
            r = wr[512 * hd:512 * hd + 512].reshape(4, P, 4, 2, P)
            parts.append(r.transpose(2, 1, 3, 0, 4).reshape(4, P, KT, P))
        parts.append(np.stack([p[0:8], p[16:24], p[8:16], p[24:32]], 1).reshape(32, P, KT, P))
        parts.append(np.stack([panels(i["w_conv_out_2"][l]), p[80:88], p[88:96]], 1).reshape(24, P, KT, P))
        parts.append(panels(i["w_o_2"][l]))
    parts.append(np.zeros((2, P, KT, P), np.float32))
    return np.concatenate(parts).reshape(4 * QUADS + 2, P, KT * P)


def vector_table(i):
    import numpy as np
    v = np.zeros((P, V_COLS), np.float32)

    def put(c, x):
        x = np.asarray(x).reshape(-1, P)
        v[:, c:c + len(x)] = x.T
    put(V_MIX, i["norm_mix_w"][0])
    put(V_FFN, i["norm_ffn_w"][0])
    put(V_FINAL, i["norm_final_w"])
    put(V_HNORM, i["hgrn_norm_w"][0])
    put(V_LB, i["hgrn_lb_raw"][0])
    for l in range(2):
        put(V_PRE + 8 * l, i["pre_norm_g_2"][l])
        put(V_POST + 8 * l, i["post_norm_g_2"][l])
        put(V_CW + 24 * l, i["conv_w_2"][l])
        put(V_CB + 8 * l, i["conv_b_2"][l])
        put(V_GN + 16 * l, i["ret_gn_g_2"][l])
        b = i["b_in_2"][l].reshape(96, P)
        c = V_BIAS + 4 * Q_LAYER * l
        for hd in range(HEADS):
            put(c + 16 * hd, np.concatenate([b[40 + 2 * hd:42 + 2 * hd], b[32 + 2 * hd:34 + 2 * hd],
                                             b[48 + 4 * hd:52 + 4 * hd], b[64 + 4 * hd:68 + 4 * hd]]))
        put(c + 4 * Q_CONV, np.stack([b[0:8], b[16:24], b[8:16], b[24:32]], 1))
        put(c + 4 * Q_MERGE, np.stack([np.zeros((8, P), np.float32), b[80:88], b[88:96]], 1))
    v[:, V_EPS], v[:, V_EPS + 1] = EPS, GN_EPS
    return v


def tables():
    import numpy as np
    inv = (10000.0 ** (-np.arange(P, dtype=np.float64) / P)).astype(np.float32)
    ang = (np.arange(L, dtype=np.float32)[None, :] * inv[:, None]).astype(np.float64)
    lg = np.log(1.0 - 2.0 ** (-5.0 - np.arange(HEADS)))[None, :, None]
    p, x = np.arange(P)[:, None, None], np.arange(SEQ)[None, None, :]
    decx = np.exp(lg * abs(x - p)) * (p // 64 <= x // 64) / 16.0
    p, x = np.arange(META)[:, None, None], np.arange(L)[None, None, :]
    decm = np.exp(lg * abs(x - p)) / 16.0
    s, t = np.arange(P)[:, None], np.arange(P)[None, :]
    masks = np.zeros((P, LEVELS, P), np.int32)
    masks[:, 0] = (s // 2 == t // 2) & (s <= t)
    for l in range(1, LEVELS):
        b = 2 ** l
        masks[:, l] = (s // b + 1 == t // b) & (s // b % 2 == 0)
    sel = np.zeros((96, 8, P), np.float32)
    for part in (0, 32, 64):
        sel[part + np.arange(8), np.arange(8)] = -8.0
    f = np.float32
    return {"cos": np.cos(ang).astype(f), "sin": np.sin(ang).astype(f), "decx": decx.astype(f),
            "decm": decm.astype(f), "masks": masks, "sel": sel.reshape(96, 8 * P), "ident": np.eye(P, dtype=f),
            "causal": np.where(t > s, f(-8e30), f(0)).astype(f)}


def kernel(**inputs):
    import numpy as np
    import concourse.bacc as bacc
    from concourse.bass_utils import run_bass_kernel_spmd as run

    i = {k: np.asarray(a) for k, a in inputs.items()}

    def feature_major(a):
        return np.ascontiguousarray(a.reshape(-1, KT, P).transpose(2, 1, 0))

    arrays = tables()
    arrays["x"] = feature_major(i["x"][0])
    arrays["meta"] = feature_major(i["meta"])
    arrays["meta2"] = feature_major(i["meta_2"])
    arrays["weights"] = weight_stream(i)
    arrays["wff"] = np.ascontiguousarray(i["w_in"][0][:, 1536:1544].reshape(KT, P, 8).transpose(1, 0, 2)).reshape(P, KT * 8)
    arrays["fbias"] = np.ascontiguousarray(i["fox_f_bias"][0].reshape(8, 1))
    arrays["vec"] = vector_table(i)

    nc = bacc.Bacc("TRN2", target_bir_lowering=False, num_devices=1)
    io = {n: nc.dram_tensor("in_" + n, a.shape, mybir.dt.from_np(a.dtype), kind="ExternalInput").ap()
          for n, a in arrays.items()}
    io["out"] = nc.dram_tensor("out", (P, KT, SEQ), F32, kind="ExternalOutput").ap()
    build(nc, io)
    r = run(nc, [{"in_" + n: a for n, a in arrays.items()}], core_ids=[0])
    return r.results[0]["out"].transpose(2, 1, 0).reshape(1, SEQ, D)
```
